# Optimizing a Trainium2 kernel written in Bass

```python
import math
import jax, jax.numpy as jnp
from jax import lax
import numpy as np

D_MODEL = 1024
BATCH = 1
SEQ = 256
DEPTH = 1

GRID_W = 64
CTX_LEN = 256
EPS = 1e-6
CONV_W = 1024
CONV_K = 31
GLA_H = 4
GLA_DK = 128
GLA_DV = 256
GLA_KD = GLA_H * GLA_DK
GLA_VD = GLA_H * GLA_DV
GLA_RANK = 16
GLA_TAU = 16.0
GLA_CHUNK = 64
N_EXPERTS = 32
TOP_K = 4
D_FF = 1024
SWIGLU_ALPHA = 1.702
SWIGLU_LIMIT = 7.0
MOE_BLOCK = 128
MIX_SPLITS = (CONV_W, CONV_W, GLA_KD, GLA_KD, GLA_VD, GLA_VD, 2 * GLA_RANK, D_MODEL, D_MODEL)
D_IN = sum(MIX_SPLITS)

kernel_name = "hybrid_conv_gla_moe_dit_block"

def _rmsnorm(x, g):
    xf = x.astype(jnp.float32)
    y = xf * lax.rsqrt(jnp.mean(xf * xf, axis=-1, keepdims=True) + EPS)
    return y.astype(x.dtype) * g

def _layernorm(x, g, b):
    xf = x.astype(jnp.float32)
    mu = jnp.mean(xf, axis=-1, keepdims=True)
    var = jnp.mean(jnp.square(xf - mu), axis=-1, keepdims=True)
    return ((xf - mu) * lax.rsqrt(var + EPS)).astype(x.dtype) * g + b

def _modulate(h, shift, scale):
    return h * (1.0 + scale) + shift

def _conv_module(u, w_dw, b_dw, g_ln, b_ln, w_pw):
    y = lax.conv_general_dilated(
        u, w_dw[:, None, :], window_strides=(1,),
        padding=[(CONV_K // 2, CONV_K // 2)],
        dimension_numbers=("NWC", "WIO", "NWC"),
        feature_group_count=CONV_W) + b_dw
    y = _layernorm(y, g_ln, b_ln)
    return jax.nn.silu(y) @ w_pw

def _flip_segments(z, n_ctx):
    return jnp.concatenate([z[:, :n_ctx][:, ::-1], z[:, n_ctx:][:, ::-1]], axis=1)

def _gla_chunked(q, k, v, log_a):
    B, T, H, DK = q.shape
    DV = v.shape[-1]
    N = T // GLA_CHUNK

    def chunks(z):
        return z.reshape(B, N, GLA_CHUNK, H, z.shape[-1]).transpose(1, 0, 3, 2, 4)

    q, k, v, log_a = chunks(q), chunks(k), chunks(v), chunks(log_a)
    b = jnp.cumsum(log_a, axis=3)
    b_last = b[:, :, :, -1:, :]
    q_dec = q * jnp.exp(b)
    k_inv = k * jnp.exp(-b)
    k_to_end = k * jnp.exp(b_last - b)
    lower = jnp.tril(jnp.ones((GLA_CHUNK, GLA_CHUNK), dtype=bool))
    scores = jnp.einsum("nbhcd,nbhsd->nbhcs", q_dec, k_inv)
    o_intra = jnp.einsum("nbhcs,nbhsv->nbhcv", jnp.where(lower, scores, 0.0), v)

    def step(state, xs):
        q_n, k_n, v_n, bl_n = xs
        o_n = jnp.einsum("bhcd,bhdv->bhcv", q_n, state)
        state = state * jnp.exp(bl_n)[:, :, 0, :, None] + jnp.einsum("bhcd,bhcv->bhdv", k_n, v_n)
        return state, o_n

    s0 = jnp.zeros((B, H, DK, DV), jnp.float32)
    _, o_inter = lax.scan(step, s0, (q_dec, k_to_end, v, b_last))
    o = o_intra + o_inter
    return o.transpose(1, 0, 3, 2, 4).reshape(B, T, H, DV)

def _gla_bidirectional(q, k, v, g, a_lr, w_alpha, b_alpha, g_norm, n_ctx):
    B, T, _ = q.shape
    qf = q.reshape(B, T, GLA_H, GLA_DK).astype(jnp.float32) * (GLA_DK ** -0.5)
    kf = k.reshape(B, T, GLA_H, GLA_DK).astype(jnp.float32)
    vf = v.reshape(B, T, GLA_H, GLA_DV).astype(jnp.float32)
    a_fwd, a_bwd = jnp.split(a_lr, 2, axis=-1)

    def log_decay(a, d):
        z = (a @ w_alpha[d] + b_alpha[d]).astype(jnp.float32)
        return (jax.nn.log_sigmoid(z) / GLA_TAU).reshape(B, T, GLA_H, GLA_DK)

    o_fwd = _gla_chunked(qf, kf, vf, log_decay(a_fwd, 0))
    o_bwd = _flip_segments(
        _gla_chunked(_flip_segments(qf, n_ctx), _flip_segments(kf, n_ctx),
                     _flip_segments(vf, n_ctx), _flip_segments(log_decay(a_bwd, 1), n_ctx)),
        n_ctx)
    o = o_fwd + o_bwd
    o = o * lax.rsqrt(jnp.mean(o * o, axis=-1, keepdims=True) + EPS)
    o = (o.astype(g.dtype) * g_norm).reshape(B, T, GLA_VD)
    return o * jax.nn.silu(g)

def _clamped_swiglu(hid):
    x_glu = jnp.minimum(hid[..., ::2], SWIGLU_LIMIT)
    x_lin = jnp.clip(hid[..., 1::2], -SWIGLU_LIMIT, SWIGLU_LIMIT)
    return x_glu * jax.nn.sigmoid(SWIGLU_ALPHA * x_glu) * (x_lin + 1.0)

def _moe(h, w_router, b_router, w1, b1, w2, b2):
    N, D = h.shape
    logits = (h @ w_router + b_router).astype(jnp.float32)
    top_val, top_idx = lax.top_k(logits, TOP_K)
    probs = jax.nn.softmax(top_val, axis=-1)
    NK = N * TOP_K
    e_flat = top_idx.reshape(NK).astype(jnp.int32)
    tok_flat = jnp.repeat(jnp.arange(N, dtype=jnp.int32), TOP_K)
    p_flat = probs.reshape(NK)
    order = jnp.argsort(e_flat, stable=True)
    e_sorted = e_flat[order]
    counts = jnp.zeros((N_EXPERTS,), jnp.int32).at[e_flat].add(1)
    padded = (counts + MOE_BLOCK - 1) // MOE_BLOCK * MOE_BLOCK
    pad_end = jnp.cumsum(padded)
    pad_start = pad_end - padded
    start = jnp.cumsum(counts) - counts
    dest = pad_start[e_sorted] + (jnp.arange(NK, dtype=jnp.int32) - start[e_sorted])
    n_blocks = (NK + N_EXPERTS * (MOE_BLOCK - 1) + MOE_BLOCK - 1) // MOE_BLOCK
    P = n_blocks * MOE_BLOCK
    row_tok = jnp.full((P,), N, jnp.int32).at[dest].set(tok_flat[order])
    row_p = jnp.zeros((P,), jnp.float32).at[dest].set(p_flat[order])
    blk_expert = jnp.minimum(
        jnp.searchsorted(pad_end, jnp.arange(n_blocks, dtype=jnp.int32) * MOE_BLOCK, side="right"),
        N_EXPERTS - 1)
    h_pad = jnp.concatenate([h, jnp.zeros((1, D), h.dtype)], axis=0)

    def body(acc, blk):
        rows = lax.dynamic_slice(row_tok, (blk * MOE_BLOCK,), (MOE_BLOCK,))
        wts = lax.dynamic_slice(row_p, (blk * MOE_BLOCK,), (MOE_BLOCK,))
        e = blk_expert[blk]
        hid = h_pad[rows] @ w1[e] + b1[e]
        y = _clamped_swiglu(hid) @ w2[e] + b2[e]
        return acc.at[rows].add(y * wts[:, None].astype(y.dtype)), None

    acc, _ = lax.scan(body, jnp.zeros((N + 1, D), h.dtype), jnp.arange(n_blocks, dtype=jnp.int32))
    return acc[:N]

def setup_inputs(seed: int = 0) -> dict:
    key = jax.random.key(seed)
    ks = iter(jax.random.split(key, 32))
    f32 = jnp.float32

    def nrm(shape, scale):
        return jax.random.normal(next(ks), shape, f32) * scale

    L, D = DEPTH, D_MODEL
    return {
        "x": nrm((BATCH, SEQ, D), 1.0),
        "c": nrm((BATCH, D), 1.0),
        "ctx": nrm((BATCH, CTX_LEN, D), 1.0),
        "c_ctx": nrm((D,), 1.0),
        "w_ada": nrm((L, D, 6 * D), D ** -0.5),
        "b_ada": nrm((L, 6 * D), 0.02),
        "g_mix_norm": 1.0 + nrm((L, D), 0.05),
        "w_in": nrm((L, D, D_IN), D ** -0.5),
        "w_dw": nrm((L, CONV_K, CONV_W), CONV_K ** -0.5),
        "b_dw": nrm((L, CONV_W), 0.02),
        "g_conv_ln": 1.0 + nrm((L, CONV_W), 0.05),
        "b_conv_ln": nrm((L, CONV_W), 0.02),
        "w_conv_out": nrm((L, CONV_W, D), CONV_W ** -0.5),
        "w_alpha": nrm((L, 2, GLA_RANK, GLA_KD), GLA_RANK ** -0.5),
        "b_alpha": nrm((L, 2, GLA_KD), 0.5),
        "g_gla_norm": 1.0 + nrm((L, GLA_DV), 0.05),
        "w_gla_out": nrm((L, GLA_VD, D), GLA_VD ** -0.5),
        "w_out": nrm((L, D, D), D ** -0.5),
        "g_ffn_norm": 1.0 + nrm((L, D), 0.05),
        "w_router": nrm((L, D, N_EXPERTS), D ** -0.5),
        "b_router": nrm((L, N_EXPERTS), 0.01),
        "w_exp_in": nrm((L, N_EXPERTS, D, 2 * D_FF), D ** -0.5),
        "b_exp_in": nrm((L, N_EXPERTS, 2 * D_FF), 0.01),
        "w_exp_out": nrm((L, N_EXPERTS, D_FF, D), D_FF ** -0.5),
        "b_exp_out": nrm((L, N_EXPERTS, D), 0.01),
        "g_final": 1.0 + nrm((D,), 0.05),
    }

def reference(x, c, ctx, c_ctx, w_ada, b_ada, g_mix_norm, w_in, w_dw, b_dw, g_conv_ln, b_conv_ln,
              w_conv_out, w_alpha, b_alpha, g_gla_norm, w_gla_out, w_out, g_ffn_norm, w_router,
              b_router, w_exp_in, b_exp_in, w_exp_out, b_exp_out, g_final):
    B, S, D = x.shape
    L = ctx.shape[1]
    ROWS = S // GRID_W
    split_idx = [int(i) for i in np.cumsum(MIX_SPLITS)[:-1]]

    for l in range(DEPTH):
        last = l == DEPTH - 1
        mod_lat = jax.nn.silu(c) @ w_ada[l] + b_ada[l]
        mod_ctx = jax.nn.silu(c_ctx) @ w_ada[l] + b_ada[l]
        sh1, sc1, gt1, sh2, sc2, gt2 = jnp.split(mod_lat, 6, axis=-1)
        csh1, csc1, cgt1, csh2, csc2, cgt2 = jnp.split(mod_ctx, 6, axis=-1)

        h_lat = _modulate(_rmsnorm(x, g_mix_norm[l]), sh1[:, None], sc1[:, None])
        h_ctx = _modulate(_rmsnorm(ctx, g_mix_norm[l]), csh1, csc1)
        h = jnp.concatenate([h_ctx, h_lat], axis=1)
        proj = h @ w_in[l]
        conv_a, conv_b, q, k, v, g, a_lr, gate_conv, gate_gla = jnp.split(proj, split_idx, axis=-1)

        u = conv_a * jax.nn.sigmoid(conv_b)
        y_conv_lat = _conv_module(u[:, L:].reshape(B * ROWS, GRID_W, CONV_W), w_dw[l], b_dw[l],
                                  g_conv_ln[l], b_conv_ln[l], w_conv_out[l]).reshape(B, S, D)
        o_gla = _gla_bidirectional(q, k, v, g, a_lr, w_alpha[l], b_alpha[l], g_gla_norm[l], L)
        y_gla_lat = o_gla[:, L:] @ w_gla_out[l]
        m_lat = jax.nn.sigmoid(gate_conv[:, L:]) * y_conv_lat + jax.nn.sigmoid(gate_gla[:, L:]) * y_gla_lat
        x = x + gt1[:, None] * (m_lat @ w_out[l])

        h2_lat = _modulate(_rmsnorm(x, g_ffn_norm[l]), sh2[:, None], sc2[:, None])
        moe_args = (w_router[l], b_router[l], w_exp_in[l], b_exp_in[l], w_exp_out[l], b_exp_out[l])
        if not last:
            y_conv_ctx = _conv_module(u[:, :L], w_dw[l], b_dw[l], g_conv_ln[l], b_conv_ln[l], w_conv_out[l])
            y_gla_ctx = o_gla[:, :L] @ w_gla_out[l]
            m_ctx = jax.nn.sigmoid(gate_conv[:, :L]) * y_conv_ctx + jax.nn.sigmoid(gate_gla[:, :L]) * y_gla_ctx
            ctx = ctx + cgt1 * (m_ctx @ w_out[l])
            h2_ctx = _modulate(_rmsnorm(ctx, g_ffn_norm[l]), csh2, csc2)
            y_all = _moe(jnp.concatenate([h2_ctx.reshape(B * L, D), h2_lat.reshape(B * S, D)], axis=0), *moe_args)
            ctx = ctx + cgt2 * y_all[:B * L].reshape(B, L, D)
            y_lat = y_all[B * L:].reshape(B, S, D)
        else:
            y_lat = _moe(h2_lat.reshape(B * S, D), *moe_args).reshape(B, S, D)
        x = x + gt2[:, None] * y_lat

    return _rmsnorm(x, g_final)


_drawn_inputs = setup_inputs


def setup_inputs(seed=0):
    import zlib

    import numpy as np

    out = dict(_drawn_inputs(seed))
    spreads = {}
    factors = {'b_dw': 4.061, 'b_conv_ln': 3.242, 'b_exp_in': 8.0, 'b_exp_out': 8.0, 'b_router': 3.002}
    for name, (base, spread) in spreads.items():
        noise = np.random.default_rng([zlib.crc32(name.encode()), seed]).standard_normal(out[name].shape)
        drawn = base * np.exp(spread * noise) if base else spread * noise
        out[name] = __import__('jax').numpy.asarray(drawn.astype(out[name].dtype))
    for name, factor in factors.items():
        out[name] = (out[name] * factor).astype(out[name].dtype)
    return out
```

```python
from contextlib import ExitStack

import concourse.bass as bass
from concourse import mybir

F32 = mybir.dt.float32
F32R = mybir.dt.float32r
I32 = mybir.dt.int32
ALU = mybir.AluOpType
ACT = mybir.ActivationFunctionType
AX_X = mybir.AxisListType.X

P = 128
EPS = 1e-6
TAU = 16.0
ALPHA = 1.702
LIMIT = 7.0
BIG = 65536.0


class Tally:

    def __init__(self, sem):
        self.sem, self.n = sem, 0

    def sign(self, ins):
        ins.then_inc(self.sem, 1)
        self.n += 1


def build(nc, x, c, ctx_tokens, c_ctx, w_ada, b_ada, g_mix_norm, w_in, w_dw, b_dw, g_conv_ln, b_conv_ln,
          w_conv_out, w_alpha, b_alpha, g_gla_norm, w_gla_out, w_out, g_ffn_norm, w_router, b_router,
          w_exp_in, b_exp_in, w_exp_out, b_exp_out, g_final, out, debug=None):
    _, SEQ, D = x.shape
    LCTX = ctx_tokens.shape[1]
    T = LCTX + SEQ
    KT = D // P
    CTX_TT, LAT_TT = LCTX // P, SEQ // P
    TT = CTX_TT + LAT_TT
    TAPS = w_dw.shape[1]
    PAD = TAPS // 2
    GRID_W = 64
    ROWS = SEQ // GRID_W
    RANK, KD = w_alpha.shape[2], w_alpha.shape[3]
    DK = P
    HEADS = KD // DK
    DV = g_gla_norm.shape[1]
    CHUNK = 64
    NCHUNK = T // CHUNK
    E, FF = w_exp_in.shape[1], w_exp_out.shape[2]
    TOPK = 4
    SLOTS = 64
    NF = 512
    ITEMS_MAX = (SEQ * TOPK + E * (SLOTS - 1)) // SLOTS
    ITEM_COLS = ITEMS_MAX + 1
    HD = 2 * HEADS
    c0 = dict(conv_a=0, conv_b=D, q=2 * D, k=2 * D + KD, v=2 * D + 2 * KD)
    c0["g"] = c0["v"] + HEADS * DV
    c0["a_lr"] = c0["g"] + HEADS * DV
    c0["gate_conv"] = c0["a_lr"] + 2 * RANK
    c0["gate_gla"] = c0["gate_conv"] + D

    def chunked(w, col):
        return w.rearrange("(t p) n -> p t n", p=P)[:, :, col:col + NF]

    stream = []
    ada = lambda part: [chunked(w_ada[0], part * D + n * NF) for n in range(D // NF)]
    proj = lambda name, n: chunked(w_in[0], c0[name] + n * NF)
    stream += ada(0) + ada(1)
    stream += [proj("k", 0), proj("q", 0), proj("conv_a", 0), proj("conv_b", 0), proj("conv_a", 1), proj("conv_b", 1)]
    stream += [proj(name, n) for name in ("v", "g", "gate_conv", "gate_gla") for n in range(2)]
    n_proj = len(stream)
    stream += ada(2) + ada(3) + ada(4) + ada(5)
    stream += [chunked(w[0], n * NF) for w in (w_gla_out, w_conv_out, w_out) for n in range(2)]
    NSTREAM = len(stream)
    NRING = 3
    NPART = 2
    CPI = 2 * FF // NF + D // NF

    base = (nc.sbuf_base + 511) // 512 * 512
    KB = 1024

    def at(name, kb, shape, dt=F32):
        return nc.alloc_sbuf_tensor_at(name, list(shape), dt, offset=base + int(kb * KB))

    class Bump:

        def __init__(self, kb, end):
            self.kb, self.end = kb, end

        def __call__(self, name, shape, dt=F32):
            size = 4
            for s in shape[1:]:
                size *= s
            t = at(name, self.kb, shape, dt)
            self.kb += (size + 63) // 64 * 64 / KB
            assert self.kb <= self.end, name
            return t

    ring = [at(f"weights{s}", 16 * s, [P, KT, NF]) for s in range(NRING)]
    small = Bump(48, 68)
    ident = small("ident", [P, P])
    ones = small("ones", [P, P])
    slot_of_col = small("slot_of_col", [P, P])
    mask_f = small("mask_f", [P, P])
    mask_b = small("mask_b", [P, P])
    before = small("before", [P, P])
    scan_keep = small("scan_keep", [P, T])
    fold = small("fold", [P, SLOTS])
    vecT = small("vecT", [P, 112])
    wdwT = small("wdwT", [P, KT, TAPS])
    decay = small("decay", [P, HD, NCHUNK])
    stat = small("stat", [P, 32])
    a_lr_w = small("a_lr_w", [P, KT, 2 * RANK])
    wal = small("wal", [RANK, 2, KD])
    wr = small("wr", [P, KT, E])
    sc_act = small("sc_act", [P, 2 * KT])
    scT = small("scT", [P, KT, 2])
    modT = small("modT", [P, 2 * KT, 2])
    b1T = small("b1T", [P, E, 2 * FF // P])
    slot_tok = small("slot_tok", [P, LAT_TT, ITEM_COLS])
    prob_tok = small("prob_tok", [P, LAT_TT, ITEM_COLS])
    item_expert = small("item_expert", [1, ITEM_COLS + 1], I32)
    neg_half = small("neg_half", [P, SEQ])
    x1 = at("x1", 68, [P, LAT_TT, D])
    gt2 = at("gt2", 76, [P, D])
    h2_hi = at("h2_hi", 80, [P, LAT_TT, D], F32R)
    h2_lo = at("h2_lo", 88, [P, LAT_TT, D], F32R)
    tokens = at("tokens", 68, [P, TT, D])
    sq_junk = at("sq_junk", 116, [P, D])
    o_junk = at("o_junk", 188, [P, DV])
    mod_rows = at("mod_rows", 84, [2, 2 * D])
    b1_rows = at("b1_rows", 92, [E, 2 * FF])
    vec_rows = at("vec_rows", 100, [112, P])
    wdw_rows = at("wdw_rows", 101, [TAPS, D])
    hT = at("hT", 100, [P, KT, T])
    a_lrT = at("a_lrT", 92, [RANK, 2, T])
    k_end = at("k_end", 116, [P, HD, TT, P])
    q_dec = at("q_dec", 132, [P, HD, SEQ])
    scores = at("scores", 140, [P, HEADS, LAT_TT, P])
    yT = at("yT", 144, [P, KT, SEQ])
    u = at("u", 152, [P, KT, ROWS, GRID_W + 2 * PAD])
    kT = at("kT", 164, [P, HEADS, T])
    qT = at("qT", 172, [P, HEADS, SEQ])
    z_t = at("z_t", 176, [P, T])
    e_t = at("e_t", 178, [P, T])
    la_t = at("la_t", 180, [P, T])
    pre_t = at("pre_t", 182, [P, T])
    te_t = at("te_t", 184, [P, T])
    et_t = at("et_t", 186, [P, T])
    kte_t = at("kte_t", 188, [P, T])
    v = at("v", 190, [P, TT, HEADS * DV])
    state = at("state", 68, [P, 4, HD, DV])
    sgn = at("sgn", 164, [P, LAT_TT, HEADS * DV])
    sg_conv = at("sg_conv", 172, [P, LAT_TT, D])
    sg_gla = at("sg_gla", 180, [P, LAT_TT, D])
    gla_g = at("gla_g", 206, [P, DV])
    o_sb = at("o_sb", 116, [P, LAT_TT, HEADS * DV])
    oT = at("oT", 124, [P, KT, SEQ])
    b_ada_b = at("b_ada_b", 100, [P, 4 * D])
    sc_wide = at("sc_wide", 92, [P, KT, P])
    gt1 = at("gt1", 96, [P, D])
    sh2 = at("sh2", 202, [P, D])
    a2 = at("a2", 198, [P, D])
    ysq = at("ysq", 190, [P, KT, SEQ])
    mu = at("mu", 160, [P, SEQ])
    rstd = at("rstd", 161, [P, SEQ])
    var = at("var", 162, [P, SEQ])
    musq = at("musq", 163, [P, SEQ])
    m = at("m", 152, [P, LAT_TT, D])
    gated = at("gated", 164, [P, NF])
    mT = at("mT", 124, [P, KT, SEQ])
    ln_t = at("ln_t", 116, [P, KT, SEQ])
    h2 = at("h2", 140, [P, LAT_TT, D])
    g_ffn_b = at("g_ffn_b", 104, [P, D])
    b_router_b = at("b_router_b", 108, [P, E])
    h2T = at("h2T", 132, [P, KT, SEQ])
    b2_rows = at("b2_rows", 100, [E, D])
    rt = Bump(152, 164)
    logits = rt("logits", [P, LAT_TT, E])
    top8 = rt("top8", [P, LAT_TT, 8])
    above = rt("above", [P, LAT_TT, E])
    equal = rt("equal", [P, LAT_TT, E])
    nth = rt("nth", [P, LAT_TT, E])
    need = rt("need", [P, LAT_TT, 4])
    sel = rt("sel", [P, LAT_TT, E])
    expo = rt("expo", [P, LAT_TT, E])
    prob = rt("prob", [P, LAT_TT, E])
    rank = rt("rank", [P, LAT_TT, E])
    blocks = rt("blocks", [P, 4, E])
    ends = rt("ends", [P, 2, E])
    ecol = rt("ecol", [E, 4])
    one_item = rt("one_item", [E, ITEM_COLS])
    item_no = rt("item_no", [P, ITEM_COLS])
    rankT = rt("rankT", [E, LAT_TT, P])
    probT = rt("probT", [E, LAT_TT, P])
    w_hi = [at(f"w_hi{s}", 100 + 16 * s, [P, KT, NF], F32R) for s in range(NPART)]
    w_lo = [at(f"w_lo{s}", 132 + 16 * s, [P, KT, NF], F32R) for s in range(NPART)]
    hid = at("hid", 164, [P, 2 * FF])
    xs = at("xs", 172, [P, KT, 2 * SLOTS], F32R)
    hs = at("hs", 176, [P, FF // P, 2 * SLOTS], F32R)
    y = at("y", 180, [P, D])
    scatter = at("scatter", 184, [P, LAT_TT, P])
    pick = at("pick", 185, [P, LAT_TT, SLOTS], F32R)
    weigh = at("weigh", 186, [P, LAT_TT, P])
    glu = at("glu", 187, [P, FF // P, SLOTS])
    lin = at("lin", 189, [P, FF // P, SLOTS])
    sig = at("sig", 191, [P, FF // P, SLOTS])
    hf = at("hf", 193, [P, FF // P, SLOTS])
    g_final_b = at("g_final_b", 195, [P, D])
    out_sb = at("out_sb", 100, [P, LAT_TT, D])

    stack = ExitStack()
    with stack:
        def sem(name):
            return stack.enter_context(nc.semaphore(name))

        bank = [stack.enter_context(nc.psum_tensor(f"bank{i}", [P, NF], F32)) for i in range(8)]
        A_BANKS, D_BANKS = bank[0:4], bank[4:8]

        landed = [sem(f"weights_landed{s}") for s in range(NRING)]
        vec_in, tok_in, bias_in, rows_in = sem("vec_in"), sem("tok_in"), sem("bias_in"), sem("rows_in")
        b_ada_in, x_again_in, late_in = sem("b_ada_in"), sem("x_again_in"), sem("late_in")
        const_ok = sem("const_ok")
        a_full, a_empty = sem("a_bank_full"), sem("a_bank_empty")
        d_full, d_empty = sem("d_bank_full"), sem("d_bank_empty")
        dve_ok, act_ok, pool_ok = sem("dve_step"), sem("act_step"), sem("pool_step")
        sums_ok, pow_ok = sem("squares_summed"), sem("rstd_ok")
        sc_sig, sc_ok, norm_ok, mod_ok = sem("c_sigmoid"), sem("silu_c_ok"), sem("tokens_normed"), sem("mod_ok")
        z_ok, ln_ok, te_ok, et_ok, kte_ok = sem("z_ok"), sem("ln_ok"), sem("te_ok"), sem("et_ok"), sem("kte_ok")
        conv_ok, ysq_ok, act_conv_ok = sem("conv_ok"), sem("ysq_ok"), sem("act_conv_ok")
        wide_ok, oss_ok, orstd_ok = sem("silu_c_wide"), sem("o_squares"), sem("o_rstd")
        ln_var_ok, ln_rstd_ok, ln_in, ln_sig = sem("ln_var"), sem("ln_rstd"), sem("ln_in"), sem("ln_sig")
        x1_ok, x1_sum, x1_pow, h2_ok, exp_ok = sem("x1_ok"), sem("x1_sum"), sem("x1_rstd"), sem("h2_ok"), sem("exp_ok")
        m_ok, ms_free, max_ok, sel_ok, rank_ok = sem("m_ok"), sem("m_unused"), sem("max_ok"), sem("sel_ok"), sem("rank_ok")
        one_item_ok, items_ok, x2_ok, g_final_in = sem("one_item_ok"), sem("items_ok"), sem("x2_ok"), sem("g_final_in")
        hi_ok, lo_ok = sem("hi_ok"), sem("lo_ok")
        hid_full, hid_out = sem("hid_full"), sem("hid_out")
        xs_full, xs_out = sem("xs_full"), sem("xs_out")
        sc_full, sc_out = sem("scatter_full"), sem("scatter_out")
        ht_full, ht_out = sem("hidT_full"), sem("hidT_out")
        y_full, y_out = sem("y_full"), sem("y_out")
        pick_ok, weigh_ok = sem("pick_ok"), sem("weigh_ok")
        glu_ok, sig_ok, hs_ok = sem("glu_ok"), sem("sig_ok"), sem("hs_ok")
        loop_step = sem("dve_loop_step")
        acc_full, fin_sum, fin_pow, out_ok, stored = sem("acc_full"), sem("fin_sum"), sem("fin_pow"), sem("out_ok"), sem("stored")

        block = stack.enter_context(nc.Block())
        N_CONST = 22
        LO_PRIME = 6

        def CHUNK_OF(direction, s):
            n_ctx = LCTX // CHUNK
            return s if direction == 0 else n_ctx - 1 - s if s < n_ctx else NCHUNK - 1 + n_ctx - s

        def item_count(eng):
            eng.wait_ge(items_ok, 1)
            return eng.value_load(item_expert[0:1, ITEM_COLS:ITEM_COLS + 1], min_val=1, max_val=ITEMS_MAX)

        def front_landed(n):
            return landed[n % NRING], 16 * (n // NRING + 1)

        def item_landed(i, j):
            s = (NSTREAM + j) % NRING
            first = (NSTREAM - s + NRING - 1) // NRING
            return landed[s], 16 * first + 16 * (j // NRING + 1) + i * (16 * CPI // NRING)

        chunk_used = []
        mark = {}
        HID_BANK = [bank[6], bank[7], bank[4], bank[5]]

        @block.tensor
        def _(pe):
            na, nd, taken = [0], [0], [0]

            def a_open():
                if na[0] >= 4:
                    pe.wait_ge(a_empty, na[0] - 3)
                na[0] += 1
                return A_BANKS[(na[0] - 1) % 4]

            def d_open():
                if nd[0] >= 4:
                    pe.wait_ge(d_empty, nd[0] - 3)
                nd[0] += 1
                return D_BANKS[(nd[0] - 1) % 4]

            def next_chunk():
                n = taken[0]
                pe.wait_ge(*front_landed(n))
                taken[0] += 1
                return ring[n % NRING]

            def accumulate(dst, lhs, rhs):
                for k in range(KT):
                    ins = pe.matmul(dst, lhs(k), rhs(k), start=(k == 0), stop=(k == KT - 1))
                return ins

            def used_by_a():
                chunk_used.append((a_full, na[0]))

            def used_by_d():
                chunk_used.append((d_full, nd[0]))

            def transposed(src):
                for g in range(KT // 2):
                    b = a_open()
                    for kk in range(2):
                        for t in range(LAT_TT):
                            kt = 2 * g + kk
                            ins = pe.transpose(b[:, (kk * LAT_TT + t) * P:(kk * LAT_TT + t + 1) * P],
                                               src[:, t, kt * P:(kt + 1) * P], ident[:, :])
                    ins.then_inc(a_full, 1)

            pe.wait_ge(const_ok, N_CONST)
            pe.wait_ge(vec_in, 9 * 16)
            pe.transpose(d_open()[:, 0:112], vec_rows[:, :], ident[0:112, 0:112]).then_inc(d_full, 1)
            pe.wait_ge(rows_in, 32)
            b = d_open()
            for kt in range(KT):
                ins = pe.transpose(b[:, kt * TAPS:(kt + 1) * TAPS], wdw_rows[:, kt * P:(kt + 1) * P], ident[0:TAPS, 0:TAPS])
            ins.then_inc(d_full, 1)
            b = d_open()
            for part in range(2):
                for j in range(FF // P):
                    cols = b1_rows[:, j * 2 * P:(j + 1) * 2 * P].rearrange("e (m two) -> e two m", two=2)[:, part, :]
                    g = part * (FF // P) + j
                    ins = pe.transpose(b[:, g * E:(g + 1) * E], cols, ident[0:E, 0:E])
            ins.then_inc(d_full, 1)
            pe.wait_ge(sc_ok, 1)
            for n in range(4):
                w = next_chunk()
                b = a_open()
                accumulate(b[0:2, :], lambda k: scT[:, k, :], lambda k: w[:, k, :]).then_inc(a_full, 1)
                used_by_a()
            pe.wait_ge(a_empty, na[0])
            b = d_open()
            for j in range(2 * KT):
                ins = pe.transpose(b[:, 2 * j:2 * j + 2], mod_rows[:, j * P:(j + 1) * P], ident[0:2, 0:2])
            ins.then_inc(d_full, 1)
            pe.wait_ge(norm_ok, TT)
            for kt in range(KT):
                b = a_open()
                for t in range(TT):
                    ins = pe.transpose(b[:, t * P:(t + 1) * P], tokens[:, t, kt * P:(kt + 1) * P], ident[:, :])
                ins.then_inc(a_full, 1)
            pe.wait_ge(a_empty, na[0])
            pe.wait_ge(bias_in, 64)
            for d in range(2):
                b = a_open()
                accumulate(b[0:RANK, :], lambda k: a_lr_w[:, k, d * RANK:(d + 1) * RANK], lambda k: hT[:, k, :]).then_inc(a_full, 1)
            n_a_lr = na[0]
            w = next_chunk()
            for h in range(HEADS):
                b = a_open()
                accumulate(b[:, :], lambda k: w[:, k, h * P:(h + 1) * P], lambda k: hT[:, k, :]).then_inc(a_full, 1)
            used_by_a()
            w = next_chunk()
            for h in range(HEADS):
                b = a_open()
                accumulate(b[:, 0:SEQ], lambda k: w[:, k, h * P:(h + 1) * P], lambda k: hT[:, k, LCTX:T]).then_inc(a_full, 1)
            used_by_a()
            pe.wait_ge(a_empty, n_a_lr)
            for it in range(HD + 1):
                if it < HD:
                    d, h = divmod(it, HEADS)
                    b = d_open()
                    pe.matmul(b[:, :], wal[:, d, h * P:(h + 1) * P], a_lrT[:, d, :], start=True, stop=True).then_inc(d_full, 1)
                    for g in (2 * it, 2 * it + 1):
                        if g % 4 == 0:
                            w = next_chunk()
                        b = a_open()
                        cs = slice((g % 4) * P, (g % 4 + 1) * P)
                        accumulate(b[:, 0:SEQ], lambda k: w[:, k, cs], lambda k: hT[:, k, LCTX:T]).then_inc(a_full, 1)
                        if g % 4 == 3:
                            used_by_a()
                if it == HD:
                    mark["conv_in"] = na[0]
                if it >= 1:
                    pe.wait_ge(kte_ok, it)
                    b = a_open()
                    for t in range(TT):
                        ins = pe.transpose(b[:, t * P:(t + 1) * P], kte_t[:, t * P:(t + 1) * P], ident[:, :])
                    ins.then_inc(a_full, 1)
                    b = d_open()
                    for t in range(LAT_TT):
                        ins = pe.matmul(b[:, t * P:(t + 1) * P], te_t[:, t * P:(t + 1) * P],
                                        q_dec[:, it - 1, t * P:(t + 1) * P], start=True, stop=True)
                    ins.then_inc(d_full, 1)
            for n in range(2):
                w = next_chunk()
                for t in range(TT):
                    b = a_open()
                    accumulate(b[:, :], lambda k: hT[:, k, t * P:(t + 1) * P], lambda k: w[:, k, :]).then_inc(a_full, 1)
                used_by_a()
            mark["v"] = na[0]
            for n in range(6):
                w = next_chunk()
                for t in range(LAT_TT):
                    b = a_open()
                    accumulate(b[:, :], lambda k: hT[:, k, LCTX + t * P:LCTX + (t + 1) * P], lambda k: w[:, k, :]).then_inc(a_full, 1)
                used_by_a()
                if n == 1:
                    mark["g"] = na[0]
            pe.wait_ge(a_empty, mark["v"])
            for s in range(NCHUNK - 1):
                for hd in range(HD):
                    ck = CHUNK_OF(hd // HEADS, s)
                    r = slice((ck % 2) * CHUNK, (ck % 2 + 1) * CHUNK)
                    h = hd % HEADS
                    b = d_open()
                    pe.matmul(b[:, 0:DV], k_end[r, hd, ck // 2, :], v[r, ck // 2, h * DV:(h + 1) * DV],
                              start=True, stop=True).then_inc(d_full, 1)
            pe.wait_ge(d_empty, nd[0])
            mark["before_o"] = nd[0]
            for t in range(LAT_TT):
                for h in range(HEADS):
                    b = d_open()
                    pe.matmul(b[:, 0:DV], scores[:, h, t, :], v[:, CTX_TT + t, h * DV:(h + 1) * DV], start=True, stop=False,
                              skip_group_check=True)
                    for d in range(2):
                        for half in range(2):
                            ck = 2 * (CTX_TT + t) + half
                            s = ck if d == 0 else NCHUNK - 1 + LCTX // CHUNK - ck
                            hd = d * HEADS + h
                            q0 = t * P + half * CHUNK
                            ins = pe.matmul(b[half * CHUNK:(half + 1) * CHUNK, 0:DV], q_dec[:, hd, q0:q0 + CHUNK],
                                            state[:, s - LCTX // CHUNK, hd, :], start=False, stop=(d == 1), skip_group_check=True)
                    ins.then_inc(d_full, 1)
            pe.wait_ge(d_empty, nd[0])
            transposed(o_sb)
            pe.wait_ge(wide_ok, 1)
            for n in range(8):
                w = next_chunk()
                b = d_open()
                accumulate(b[:, :], lambda k: sc_wide[:, k, :], lambda k: w[:, k, :]).then_inc(d_full, 1)
                used_by_d()

            def token_rows(src):
                for n in range(2):
                    w = next_chunk()
                    for t in range(LAT_TT):
                        b = d_open()
                        accumulate(b[:, :], lambda k: src[:, k, t * P:(t + 1) * P], lambda k: w[:, k, :]).then_inc(d_full, 1)
                    used_by_d()

            pe.wait_ge(a_empty, na[0])
            token_rows(oT)
            pe.wait_ge(ysq_ok, KT)
            b = d_open()
            accumulate(b[:, 0:SEQ], lambda k: ones[:, :], lambda k: yT[:, k, :])
            accumulate(b[:, SEQ:2 * SEQ], lambda k: ones[:, :], lambda k: ysq[:, k, :]).then_inc(d_full, 1)
            pe.wait_ge(act_conv_ok, KT)
            token_rows(yT)
            pe.wait_ge(m_ok, 4)
            transposed(m)
            pe.wait_ge(a_empty, na[0])
            token_rows(mT)
            pe.wait_ge(h2_ok, LAT_TT)
            transposed(h2)
            pe.wait_ge(a_empty, na[0])
            b = d_open()
            for t in range(LAT_TT):
                ins = accumulate(b[:, t * E:(t + 1) * E], lambda k: h2T[:, k, t * P:(t + 1) * P], lambda k: wr[:, k, :])
            ins.then_inc(d_full, 1)
            pe.wait_ge(sel_ok, 1)
            b = d_open()
            pe.matmul(b[:, 0:E], before[:, :], sel[:, 0, :], start=True, stop=True)
            pe.matmul(b[:, E:2 * E], ones[:, :], sel[:, 0, :], start=True, stop=False)
            pe.matmul(b[:, E:2 * E], before[:, :], sel[:, 1, :], start=False, stop=True)
            pe.matmul(b[:, 2 * E:3 * E], ones[:, :], sel[:, 0, :], start=True, stop=False)
            pe.matmul(b[:, 2 * E:3 * E], ones[:, :], sel[:, 1, :], start=False, stop=True).then_inc(d_full, 1)
            pe.wait_ge(rank_ok, 1)
            b = d_open()
            for t in range(LAT_TT):
                pe.transpose(b[0:E, t * P:(t + 1) * P], rank[:, t, :], ident[:, :])
                ins = pe.transpose(b[0:E, (LAT_TT + t) * P:(LAT_TT + t + 1) * P], prob[:, t, :], ident[:, :])
            ins.then_inc(d_full, 1)
            b = d_open()
            pe.transpose(b[0:E, 0:P], ends[:, 0, :], ident[:, :])
            pe.transpose(b[0:E, P:2 * P], ends[:, 1, :], ident[:, :]).then_inc(d_full, 1)
            pe.wait_ge(one_item_ok, 1)
            b = d_open()
            for t in range(LAT_TT):
                pe.matmul(b[:, t * ITEM_COLS:(t + 1) * ITEM_COLS], rankT[:, t, :], one_item[:, :], start=True, stop=True)
                pe.matmul(b[:, (LAT_TT + t) * ITEM_COLS:(LAT_TT + t + 1) * ITEM_COLS], probT[:, t, :], one_item[:, :], start=True, stop=True)
            pe.matmul(b[0:1, 2 * LAT_TT * ITEM_COLS:(2 * LAT_TT + 1) * ITEM_COLS], ecol[:, 2:3], one_item[:, :],
                      start=True, stop=True).then_inc(d_full, 1)
            pe.wait_ge(late_in, 48)
            for t in range(LAT_TT):
                for n in range(2):
                    ins = pe.matmul(bank[2 * t + n][:, :], probT[:, t, :], b2_rows[:, n * NF:(n + 1) * NF], start=True, stop=False,
                                    skip_group_check=True)
            ins.then_inc(y_full, 2)
            pe.wait_ge(d_empty, nd[0])

            HALF = KT // 2

            def gather(i):
                pe.wait_ge(pick_ok, i + 1)
                for k in range(KT):
                    dst = bank[6 + k // HALF][:, (k % HALF) * P:(k % HALF + 1) * P]
                    for n, src in enumerate((h2_hi, h2_lo)):
                        for t in range(LAT_TT):
                            ins = pe.matmul(dst[:, n * SLOTS:(n + 1) * SLOTS], src[:, t, k * P:(k + 1) * P], pick[:, t, :],
                                            start=(t == 0), stop=(t == LAT_TT - 1))
                    if k % HALF == HALF - 1:
                        ins.then_inc(xs_full, 1)

            def product(i, j, dst, tokens_of):
                for k in range(KT):
                    if k % HALF == 0:
                        pe.wait_ge(lo_ok, i * (2 * CPI) + (LO_PRIME + 2 * j + k // HALF + 1))
                    for n, part in enumerate((w_hi, w_lo)):
                        ins = pe.matmul(dst, tokens_of[:, k, :], part[j % NPART][:, k, :], start=(k == 0 and n == 0),
                                        stop=(k == KT - 1 and n == 1))
                return ins

            def scatter_out(last=False):
                for t in range(LAT_TT):
                    for n in range(2):
                        ins = pe.matmul(bank[2 * t + n][:, :], scatter[:, t, :], y[:, n * NF:(n + 1) * NF], start=False, stop=last,
                                        skip_group_check=True)
                return ins

            gather(0)
            items_pe = item_count(pe)
            with pe.Fori(0, items_pe) as i:
                pe.wait_ge(xs_out, i * 2 + 2)
                pe.wait_ge(y_out, i * 2 + 1)
                product(i, 0, HID_BANK[0][:, :], xs).then_inc(hid_full, 1)
                pe.wait_ge(y_out, i * 2 + 2)
                product(i, 1, HID_BANK[1][:, :], xs).then_inc(hid_full, 1)
                pe.wait_ge(sc_out, i + 1)
                scatter_out()
                product(i, 2, HID_BANK[2][:, :], xs).then_inc(hid_full, 1)
                product(i, 3, HID_BANK[3][:, :], xs).then_inc(hid_full, 1)
                pe.wait_ge(hid_out, i * 4 + 2)
                gather(i + 1)
                pe.wait_ge(hid_out, i * 4 + 3)
                pe.wait_ge(weigh_ok, i + 1)
                for t in range(LAT_TT):
                    ins = pe.transpose(bank[4][:, t * P:(t + 1) * P], weigh[:, t, :], ident[:, :])
                ins.then_inc(sc_full, 1)
                pe.wait_ge(hid_out, i * 4 + 4)
                for part in (1, 0):
                    if part == 0:
                        pe.wait_ge(sc_out, i + 2)
                    for j in range(FF // P):
                        cols = hid[:, j * 2 * P:(j + 1) * 2 * P].rearrange("s (m two) -> s two m", two=2)[:, part, :]
                        ins = pe.matmul(bank[4 + part][:, j * SLOTS:(j + 1) * SLOTS], cols, fold[:, :], start=True, stop=True)
                    ins.then_inc(ht_full, 1)
                pe.wait_ge(hs_ok, i + 1)
                for n in range(2):
                    pe.wait_ge(xs_out, i * 2 + (3 + n))
                    product(i, 4 + n, bank[6 + n][:, :], hs).then_inc(y_full, 1)
            pe.wait_ge(y_out, items_pe * 2 + 2)
            scatter_out(last=True).then_inc(acc_full, 1)

        @block.sync
        def _(sp):
            def bcast(row):
                return row.partition_broadcast(P)

            row0 = 0
            for vec in (g_mix_norm[0], g_ffn_norm[0], b_dw[0], g_conv_ln[0], b_conv_ln[0],
                        b_alpha[0].rearrange("a b -> (a b)"), c[0], c_ctx, b_ada[0]):
                rows = vec.rearrange("(r p) -> r p", p=P)
                n = min(rows.shape[0], 112 - row0)
                sp.dma_start(vec_rows[row0:row0 + n, :], rows[0:n, :]).then_inc(vec_in, 16)
                row0 += n
            sp.dma_start(wdw_rows[:, :], w_dw[0]).then_inc(rows_in, 16)
            sp.dma_start(tokens[:, 0:CTX_TT, :], ctx_tokens[0].rearrange("(t p) d -> p t d", p=P)).then_inc(tok_in, 16)
            sp.dma_start(tokens[:, CTX_TT:TT, :], x[0].rearrange("(t p) d -> p t d", p=P)).then_inc(tok_in, 16)
            for n in range(NRING):
                sp.dma_start(ring[n][:, :, :], stream[n]).then_inc(landed[n], 16)
            sp.dma_start(b1_rows[:, :], b_exp_in[0]).then_inc(rows_in, 16)
            sp.dma_start(a_lr_w[:, :, :], w_in[0].rearrange("(t p) n -> p t n", p=P)[:, :, c0["a_lr"]:c0["gate_conv"]]).then_inc(bias_in, 16)
            sp.dma_start(wal[:, :, :], w_alpha[0].rearrange("d r k -> r d k")).then_inc(bias_in, 16)
            sp.dma_start(wr[:, :, :], w_router[0].rearrange("(t p) n -> p t n", p=P)).then_inc(bias_in, 16)
            sp.dma_start(gla_g[:, :], bcast(g_gla_norm)).then_inc(bias_in, 16)
            for n in range(NRING, NSTREAM):
                sp.wait_ge(*chunk_used[n - NRING])
                sp.dma_start(ring[n % NRING][:, :, :], stream[n]).then_inc(landed[n % NRING], 16)
                if n == n_proj + NRING - 1:
                    sp.dma_start(b_ada_b[:, :], bcast(b_ada[0:1, 2 * D:6 * D])).then_inc(b_ada_in, 16)
                if n == n_proj + 8 + NRING - 1:
                    sp.wait_ge(mod_ok, 9)
                    sp.dma_start(x1[:, :, :], x[0].rearrange("(t p) d -> p t d", p=P)).then_inc(x_again_in, 16)
                    sp.dma_start(b2_rows[:, :], b_exp_out[0]).then_inc(late_in, 16)
                    sp.dma_start(g_ffn_b[:, :], bcast(g_ffn_norm)).then_inc(late_in, 16)
                    sp.dma_start(b_router_b[:, :], bcast(b_router)).then_inc(late_in, 16)
            items = item_count(sp)
            for n in range(NSTREAM - NRING, NSTREAM):
                sp.wait_ge(*chunk_used[n])
            with sp.Fori(0, items) as i:
                e = sp.value_load(item_expert[0:1, bass.ds(i, 1)], min_val=0, max_val=E - 1)
                w1 = w_exp_in[0][bass.ds(e, 1)].rearrange("a (t p) n -> (a p) t n", p=P)
                w2 = w_exp_out[0][bass.ds(e, 1)].rearrange("a (t p) n -> (a p) t n", p=P)
                for j in range(CPI):
                    src = w1[:, :, j * NF:(j + 1) * NF] if j < 2 * FF // NF else \
                        w2[:, :, (j - 2 * FF // NF) * NF:(j - 2 * FF // NF + 1) * NF]
                    s = (NSTREAM + j) % NRING
                    sp.wait_ge(lo_ok, i * (2 * CPI) + (LO_PRIME + 2 * (j - NRING + 1)))
                    sp.dma_start(ring[s][:, :, :], src).then_inc(landed[s], 16)
            sp.dma_start(g_final_b[:, :], bcast(g_final.rearrange("(a d) -> a d", a=1))).then_inc(g_final_in, 16)
            sp.wait_ge(out_ok, LAT_TT)
            sp.dma_start(out[0].rearrange("(t p) d -> p t d", p=P), out_sb[:, :, :]).then_inc(stored, 16)
            sp.wait_ge(stored, 16)

        @block.gpsimd
        def _(pool):
            done = Tally(const_ok)

            def wait_own():
                pool.wait_ge(const_ok, done.n)

            done.sign(pool.memset(ident[:, :], 0.0))
            done.sign(pool.memset(ones[:, :], 1.0))
            done.sign(pool.memset(mask_f[:, :], 1.0))
            done.sign(pool.memset(mask_b[:, :], 1.0))
            done.sign(pool.memset(scan_keep[:, :], 1.0))
            done.sign(pool.memset(fold[:, :], 0.0))
            done.sign(pool.memset(neg_half[:, :], -0.5))
            done.sign(pool.memset(u[:, :, :, :], 0.0))
            done.sign(pool.iota(slot_of_col[:, :], [[0, 2], [1, SLOTS]], base=0, channel_multiplier=0,
                                allow_small_or_imprecise_dtypes=True))
            wait_own()
            done.sign(pool.affine_select(out=ident[:, :], in_=ident[:, :], compare_op=ALU.not_equal, fill=1.0, base=0,
                                         pattern=[[-1, P]], channel_multiplier=1))
            done.sign(pool.affine_select(out=before[:, :], in_=ones[:, :], compare_op=ALU.is_gt, fill=0.0, base=0,
                                         pattern=[[1, P]], channel_multiplier=-1))
            keep = scan_keep[:, :].rearrange("p (c t) -> p c t", t=CHUNK)
            done.sign(pool.memset(keep[:, :, 0:1], 0.0))
            for half in range(2):
                wait_own()
                done.sign(pool.affine_select(out=fold[:, :], in_=fold[:, :], compare_op=ALU.not_equal, fill=1.0,
                                             base=-half * SLOTS, pattern=[[-1, SLOTS]], channel_multiplier=1))
            for b in range(P // CHUNK):
                cols = slice(b * CHUNK, (b + 1) * CHUNK)
                for mask in (mask_f, mask_b):
                    wait_own()
                    sign = 1 if mask is mask_f else -1
                    done.sign(pool.affine_select(out=mask[:, cols], in_=mask[:, cols], compare_op=ALU.is_ge, fill=0.0,
                                                 base=sign * b * CHUNK, pattern=[[sign, CHUNK]], channel_multiplier=-sign))
                    wait_own()
                    if mask is mask_f:
                        done.sign(pool.affine_select(out=mask[:, cols], in_=mask[:, cols], compare_op=ALU.is_ge, fill=0.0,
                                                     base=-b * CHUNK, pattern=[[0, CHUNK]], channel_multiplier=1))
                    else:
                        done.sign(pool.affine_select(out=mask[:, cols], in_=mask[:, cols], compare_op=ALU.is_ge, fill=0.0,
                                                     base=(b + 1) * CHUNK - 1, pattern=[[0, CHUNK]], channel_multiplier=-1))
            assert done.n == N_CONST, done.n
            steps = Tally(pool_ok)

            def rstd_of(sums, count, n, gate, gate_n, signal):
                pool.wait_ge(gate, gate_n)
                steps.sign(pool.tensor_scalar(sums, sums, 1.0 / count, EPS, ALU.mult, ALU.add))
                pool.wait_ge(pool_ok, steps.n)
                pool.tensor_tensor(sums, sums, neg_half[:, 0:n], ALU.pow).then_inc(signal, 1)

            wait_own()
            rstd_of(stat[:, 0:TT], D, TT, sums_ok, TT, pow_ok)
            for n in range(LAT_TT * HEADS):
                rstd_of(stat[:, 8 + n:9 + n], DV, 1, oss_ok, n + 1, orstd_ok)
            pool.wait_ge(ln_var_ok, 1)
            steps.sign(pool.tensor_scalar(rstd[:, :], var[:, :], EPS, 1.0, ALU.add, ALU.mult))
            pool.wait_ge(pool_ok, steps.n)
            pool.tensor_tensor(rstd[:, :], rstd[:, :], neg_half[:, 0:SEQ], ALU.pow).then_inc(ln_rstd_ok, 1)
            rstd_of(stat[:, 16:16 + LAT_TT], D, LAT_TT, x1_sum, LAT_TT, x1_pow)
            pool.wait_ge(ms_free, 1)
            pool.iota(item_no[:, :], [[1, ITEM_COLS]], base=0, channel_multiplier=0,
                      allow_small_or_imprecise_dtypes=True).then_inc(const_ok, 1)
            pool.iota(ecol[:, 2:3], [[0, 1]], base=0, channel_multiplier=1,
                      allow_small_or_imprecise_dtypes=True).then_inc(const_ok, 1)
            rstd_of(stat[:, 20:20 + LAT_TT], D, LAT_TT, fin_sum, LAT_TT, fin_pow)

        @block.scalar
        def _(act):
            groups = [0]

            def a_bank():
                groups[0] += 1
                act.wait_ge(a_full, groups[0])
                return A_BANKS[(groups[0] - 1) % 4]

            act.wait_ge(dve_ok, 1)
            act.activation(sc_act[:, :], vecT[:, 48:48 + 2 * KT], ACT.Sigmoid).then_inc(sc_sig, 1)
            act.wait_ge(tok_in, 32)
            for t in range(TT):
                if t >= 1:
                    act.wait_ge(sums_ok, t)
                act.activation(sq_junk[:, :], tokens[:, t, :], ACT.Square,
                               accum_out=stat[:, t:t + 1]).then_inc(sums_ok, 1)
            for n in range(4):
                b = a_bank()
                act.activation(mod_rows[:, n * NF:(n + 1) * NF], b[0:2, :], ACT.Copy).then_inc(a_empty, 1)
            act.wait_ge(mod_ok, 1)
            for kt in range(KT):
                b = a_bank()
                for s, (lo, hi) in enumerate(((LCTX, T), (0, LCTX))):
                    ins = act.activation(hT[:, kt, lo:hi], b[:, lo:hi], ACT.Identity, bias=modT[:, kt, s:s + 1],
                                         scale=modT[:, KT + kt, s:s + 1])
                ins.then_inc(a_empty, 1)
            for d in range(2):
                b = a_bank()
                act.activation(a_lrT[:, d, :], b[0:RANK, :], ACT.Copy).then_inc(a_empty, 1)
            for h in range(HEADS):
                b = a_bank()
                act.activation(kT[:, h, :], b[:, :], ACT.Copy).then_inc(a_empty, 1)
            for h in range(HEADS):
                b = a_bank()
                act.activation(qT[:, h, :], b[:, 0:SEQ], ACT.Copy, scale=float(DK) ** -0.5).then_inc(a_empty, 1)

            def conv_input(n):
                for g in (2 * n, 2 * n + 1):
                    half, r = divmod(g, KT)
                    is_b, ct = r // 4, half * 4 + r % 4
                    b = a_bank()
                    if is_b:
                        act.activation(yT[:, ct, :], b[:, 0:SEQ], ACT.Sigmoid).then_inc(a_empty, 1)
                    else:
                        act.activation(u[:, ct, :, PAD:PAD + GRID_W], b[:, 0:SEQ].rearrange("p (r w) -> p r w", w=GRID_W),
                                       ACT.Copy).then_inc(a_empty, 1)

            for it in range(HD + 1):
                if it < HD:
                    act.wait_ge(z_ok, it + 1)
                    act.activation(e_t[:, :], e_t[:, :], ACT.Exp).then_inc(act_ok, 1)
                    act.wait_ge(act_ok, it + 1)
                    act.activation(e_t[:, :], e_t[:, :], ACT.Ln, bias=1.0).then_inc(ln_ok, 1)
                    conv_input(it)
                    act.wait_ge(te_ok, it + 1)
                    act.activation(la_t[:, 0:SEQ], z_t[:, 0:SEQ], ACT.Exp, scale=1.0 / TAU)
                    act.activation(e_t[:, 0:SEQ], z_t[:, 0:SEQ], ACT.Exp, scale=-1.0 / TAU)
                    act.activation(decay[:, it, :], pre_t[:, :].rearrange("p (c t) -> p c t", t=CHUNK)[:, :, CHUNK - 1],
                                   ACT.Exp, scale=1.0 / TAU)
                    act.activation(et_t[:, :], te_t[:, :], ACT.Exp, scale=1.0 / TAU).then_inc(et_ok, 1)
                if it >= 1:
                    b = a_bank()
                    act.activation(k_end[:, it - 1, :, :], b[:, :].rearrange("p (t k) -> p t k", k=P), ACT.Copy).then_inc(a_empty, 1)
            for n in range(2):
                for t in range(TT):
                    b = a_bank()
                    act.activation(v[:, t, n * NF:(n + 1) * NF], b[:, :], ACT.Copy).then_inc(a_empty, 1)
            act.wait_ge(kte_ok, HD)
            for dst, fn in ((sgn, ACT.Silu), (sg_conv, ACT.Sigmoid), (sg_gla, ACT.Sigmoid)):
                for n in range(2):
                    for t in range(LAT_TT):
                        b = a_bank()
                        ins = act.activation(dst[:, t, n * NF:(n + 1) * NF], b[:, :], fn)
                        ins.then_inc(a_empty, 1)
            for n in range(LAT_TT * HEADS):
                act.wait_ge(d_full, mark["before_o"] + n + 1)
                if n >= 1:
                    act.wait_ge(oss_ok, n)
                act.activation(o_junk[:, :], D_BANKS[(mark["before_o"] + n) % 4][:, 0:DV], ACT.Square,
                               accum_out=stat[:, 8 + n:9 + n]).then_inc(oss_ok, 1)
            for g in range(4):
                b = a_bank()
                act.activation(oT[:, 2 * g:2 * g + 2, :], b[:, :].rearrange("p (k t) -> p k t", k=2), ACT.Copy).then_inc(a_empty, 1)
            act.wait_ge(conv_ok, KT)
            for ct in range(KT):
                act.activation(ysq[:, ct, :], yT[:, ct, :], ACT.Square).then_inc(ysq_ok, 1)
            for ct in range(KT):
                act.wait_ge(ln_in, ct + 1)
                act.activation(yT[:, ct, :], ln_t[:, ct, :], ACT.Silu, scale=vecT[:, 24 + ct:25 + ct],
                               bias=vecT[:, 32 + ct:33 + ct]).then_inc(act_conv_ok, 1)
            for g in range(4):
                b = a_bank()
                act.activation(mT[:, 2 * g:2 * g + 2, :], b[:, :].rearrange("p (k t) -> p k t", k=2), ACT.Copy).then_inc(a_empty, 1)
            for t in range(LAT_TT):
                act.wait_ge(x1_ok, 1)
                act.activation(h2[:, t, :], x1[:, t, :], ACT.Square, accum_out=stat[:, 16 + t:17 + t]).then_inc(x1_sum, 1)
            for g in range(4):
                b = a_bank()
                act.activation(h2T[:, 2 * g:2 * g + 2, :], b[:, :].rearrange("p (k t) -> p k t", k=2), ACT.Copy).then_inc(a_empty, 1)
            act.wait_ge(max_ok, 1)
            for t in range(LAT_TT):
                act.activation(expo[:, t, :], logits[:, t, :], ACT.Exp, bias=need[:, t, 3:4]).then_inc(exp_ok, 1)

            items = item_count(act)
            HALF = KT // 2

            def split_hi(i, j):
                act.wait_ge(*item_landed(i, j))
                if j < 2:
                    act.wait_ge(y_full, i * 2 + (j + 1))
                else:
                    act.wait_ge(hid_full, i * 4 + (j - 1))
                for half in range(2):
                    ks = slice(half * HALF, (half + 1) * HALF)
                    act.activation(w_hi[j % NPART][:, ks, :], ring[(NSTREAM + j) % NRING][:, ks, :], ACT.Copy).then_inc(hi_ok, 1)

            def hid_copy(i, n):
                act.wait_ge(hid_full, i * 4 + (n + 1))
                act.activation(hid[:, n * NF:(n + 1) * NF], HID_BANK[n][:, :], ACT.Copy).then_inc(hid_out, 1)

            with act.Fori(0, items) as i:
                split_hi(i, 0)
                split_hi(i, 1)
                hid_copy(i, 0)
                split_hi(i, 2)
                hid_copy(i, 1)
                split_hi(i, 3)
                hid_copy(i, 2)
                split_hi(i, 4)
                hid_copy(i, 3)
                act.wait_ge(sc_full, i + 1)
                act.activation(scatter[:, :, :], bank[4][:, 0:LAT_TT * P].rearrange("p (t c) -> p t c", c=P), ACT.Copy).then_inc(sc_out, 1)
                split_hi(i, 5)
                act.wait_ge(glu_ok, i + 1)
                act.activation(sig[:, :, :], glu[:, :, :], ACT.Sigmoid, scale=ALPHA).then_inc(sig_ok, 1)
                for n in range(2):
                    act.wait_ge(y_full, i * 2 + (n + 3))
                    act.activation(y[:, n * NF:(n + 1) * NF], bank[6 + n][:, :], ACT.Copy).then_inc(y_out, 1)
            for t in range(LAT_TT):
                act.wait_ge(x2_ok, t + 1)
                act.activation(out_sb[:, t, :], x1[:, t, :], ACT.Square, accum_out=stat[:, 20 + t:21 + t]).then_inc(fin_sum, 1)

        @block.vector
        def _(dve):
            step = Tally(dve_ok)
            groups = [0]

            def d_bank():
                groups[0] += 1
                dve.wait_ge(d_full, groups[0])
                return D_BANKS[(groups[0] - 1) % 4]

            def own():
                dve.wait_ge(dve_ok, step.n)

            b = d_bank()
            dve.tensor_copy(vecT[:, :], b[:, 0:112]).then_inc(d_empty, 1)
            dve.wait_ge(d_empty, 1)
            step.sign(dve.memset(stat[:, :], 0.0))
            b = d_bank()
            dve.tensor_copy(wdwT[:, :, :], b[:, 0:KT * TAPS].rearrange("p (k w) -> p k w", w=TAPS)).then_inc(d_empty, 1)
            b = d_bank()
            dve.tensor_copy(b1T[:, :, :].rearrange("p e j -> p j e"), b[:, :].rearrange("p (j e) -> p j e", e=E)).then_inc(d_empty, 1)
            dve.wait_ge(sc_sig, 1)
            dve.tensor_tensor(scT[:, :, :].rearrange("p k s -> p s k"), vecT[:, 48:48 + 2 * KT].rearrange("p (s k) -> p s k", s=2),
                              sc_act[:, :].rearrange("p (s k) -> p s k", s=2), ALU.mult).then_inc(sc_ok, 1)
            dve.wait_ge(pow_ok, 1)
            for t in range(TT):
                dve.tensor_scalar(tokens[:, t, :], tokens[:, t, :], stat[:, t:t + 1], None, ALU.mult).then_inc(norm_ok, 1)
            b = d_bank()
            bias = vecT[:, 64:64 + 2 * KT].unsqueeze(2).to_broadcast([P, 2 * KT, 2])
            dve.tensor_tensor(modT[:, :, :], b[:, 0:4 * KT].rearrange("p (k s) -> p k s", s=2), bias, ALU.add).then_inc(d_empty, 1)
            dve.wait_ge(d_empty, groups[0])
            gmix = vecT[:, 0:KT].unsqueeze(2).to_broadcast([P, KT, 2])
            dve.scalar_tensor_tensor(modT[:, KT:2 * KT, :], modT[:, KT:2 * KT, :], 1.0, gmix, ALU.add, ALU.mult).then_inc(mod_ok, 1)

            dve.wait_ge(const_ok, N_CONST)
            per_chunk = lambda t: t[:, :].rearrange("p (c t) -> p c t", t=CHUNK)
            for it in range(HD + 1):
                d, h = divmod(it, HEADS)
                if it < HD:
                    b = d_bank()
                    dve.tensor_scalar(z_t[:, :], b[:, :], vecT[:, 40 + it:41 + it], None, ALU.add).then_inc(d_empty, 1)
                    dve.wait_ge(d_empty, groups[0])
                    dve.scalar_tensor_tensor(e_t[:, :], z_t[:, :], -1.0, z_t[:, :], ALU.mult, ALU.min).then_inc(z_ok, 1)
                if it >= 1:
                    pd, ph = divmod(it - 1, HEADS)
                    b = d_bank()
                    sc2 = b[:, 0:SEQ].rearrange("p (t c) -> p t c", c=P)
                    mask = (mask_f, mask_b)[pd][:, :].unsqueeze(1).to_broadcast([P, LAT_TT, P])
                    if pd == 0:
                        dve.tensor_tensor(scores[:, ph, :, :], sc2, mask, ALU.mult).then_inc(d_empty, 1)
                    else:
                        dve.tensor_tensor(kte_t[:, 0:SEQ].rearrange("p (t c) -> p t c", c=P), sc2, mask, ALU.mult).then_inc(d_empty, 1)
                        dve.wait_ge(d_empty, groups[0])
                        step.sign(dve.tensor_tensor(scores[:, ph, :, :], scores[:, ph, :, :],
                                                    kte_t[:, 0:SEQ].rearrange("p (t c) -> p t c", c=P), ALU.add))
                if it < HD:
                    dve.wait_ge(ln_ok, it + 1)
                    step.sign(dve.scalar_tensor_tensor(la_t[:, :], z_t[:, :], 0.0, e_t[:, :], ALU.min, ALU.subtract))
                    own()
                    step.sign(dve.tensor_tensor_scan(pre_t[:, :], scan_keep[:, :], la_t[:, :], 0.0, ALU.mult, ALU.add))
                    own()
                    total = per_chunk(pre_t)[:, :, CHUNK - 1:CHUNK].to_broadcast([P, NCHUNK, CHUNK])
                    if d == 0:
                        dve.tensor_copy(z_t[:, 0:SEQ], pre_t[:, LCTX:T])
                        dve.tensor_tensor(per_chunk(te_t), total, per_chunk(pre_t), ALU.subtract).then_inc(te_ok, 1)
                    else:
                        step.sign(dve.tensor_tensor(te_t[:, :], pre_t[:, :], la_t[:, :], ALU.subtract))
                        own()
                        nl = LCTX // CHUNK
                        dve.tensor_tensor(z_t[:, 0:SEQ].rearrange("p (c t) -> p c t", t=CHUNK), total[:, nl:NCHUNK, :],
                                          per_chunk(te_t)[:, nl:NCHUNK, :], ALU.subtract).then_inc(te_ok, 1)
                    dve.wait_ge(et_ok, it + 1)
                    step.sign(dve.tensor_tensor(q_dec[:, it, :], qT[:, h, :], la_t[:, 0:SEQ], ALU.mult))
                    step.sign(dve.tensor_tensor(te_t[:, 0:SEQ], kT[:, h, LCTX:T], e_t[:, 0:SEQ], ALU.mult))
                    dve.tensor_tensor(kte_t[:, :], kT[:, h, :], et_t[:, :], ALU.mult).then_inc(kte_ok, 1)

            dve.wait_ge(a_empty, mark["conv_in"])
            for ct in range(KT):
                rows = lambda k: u[:, ct, :, k:k + GRID_W]
                yv = yT[:, ct, :].rearrange("p (r w) -> p r w", w=GRID_W)
                step.sign(dve.tensor_tensor(rows(PAD), rows(PAD), yv, ALU.mult))
                own()
                step.sign(dve.tensor_scalar(yv, rows(0), wdwT[:, ct, 0:1], vecT[:, 16 + ct:17 + ct], ALU.mult, ALU.add))
                for k in range(1, TAPS):
                    own()
                    ins = dve.scalar_tensor_tensor(yv, rows(k), wdwT[:, ct, k:k + 1], yv, ALU.mult, ALU.add)
                    if k < TAPS - 1:
                        step.sign(ins)
                    else:
                        ins.then_inc(conv_ok, 1)

            first_store = LCTX // CHUNK
            for s in range(NCHUNK - 1):
                src, dst = max(s - first_store, 0), max(s + 1 - first_store, 0)
                for hd in range(HD):
                    b = d_bank()
                    if s == 0:
                        dve.tensor_copy(state[:, 0, hd, :], b[:, 0:DV]).then_inc(d_empty, 1)
                    else:
                        dve.wait_ge(d_empty, groups[0] - HD)
                        dve.scalar_tensor_tensor(state[:, dst, hd, :], state[:, src, hd, :],
                                                 decay[:, hd, CHUNK_OF(hd // HEADS, s):CHUNK_OF(hd // HEADS, s) + 1],
                                                 b[:, 0:DV], ALU.mult, ALU.add).then_inc(d_empty, 1)
            dve.wait_ge(a_empty, mark["g"])
            for t in range(LAT_TT):
                for h in range(HEADS):
                    step.sign(dve.tensor_tensor(sgn[:, t, h * DV:(h + 1) * DV], sgn[:, t, h * DV:(h + 1) * DV], gla_g[:, :], ALU.mult))
            own()
            assert groups[0] == mark["before_o"], groups
            for n in range(LAT_TT * HEADS):
                t, h = divmod(n, HEADS)
                b = d_bank()
                dve.wait_ge(orstd_ok, n + 1)
                dve.scalar_tensor_tensor(o_sb[:, t, h * DV:(h + 1) * DV], b[:, 0:DV], stat[:, 8 + n:9 + n],
                                         sgn[:, t, h * DV:(h + 1) * DV], ALU.mult, ALU.mult).then_inc(d_empty, 1)
            for kt in range(KT):
                ins = dve.tensor_copy(sc_wide[:, kt, :], scT[:, kt, 0:1].to_broadcast([P, P]))
            ins.then_inc(wide_ok, 1)
            dve.wait_ge(b_ada_in, 16)
            for part, dst in enumerate((gt1, sh2, a2, gt2)):
                for n in range(2):
                    b = d_bank()
                    dve.tensor_tensor(dst[:, n * NF:(n + 1) * NF], b[:, :],
                                      b_ada_b[:, part * D + n * NF:part * D + (n + 1) * NF], ALU.add).then_inc(d_empty, 1)
                    dve.wait_ge(d_empty, groups[0])
                    dve.sem_inc(mod_ok, 1)
            for n in range(2):
                for t in range(LAT_TT):
                    b = d_bank()
                    cs = slice(n * NF, (n + 1) * NF)
                    dve.tensor_tensor(m[:, t, cs], b[:, :], sg_gla[:, t, cs], ALU.mult).then_inc(d_empty, 1)
            b = d_bank()
            step.sign(dve.tensor_scalar(mu[:, :], b[:, 0:SEQ], 1.0 / D, None, ALU.mult))
            own()
            step.sign(dve.tensor_tensor(musq[:, :], mu[:, :], mu[:, :], ALU.mult))
            own()
            dve.scalar_tensor_tensor(var[:, :], b[:, SEQ:2 * SEQ], 1.0 / D, musq[:, :], ALU.mult, ALU.subtract).then_inc(d_empty, 1)
            dve.wait_ge(d_empty, groups[0])
            step.sign(dve.tensor_scalar(var[:, :], var[:, :], 0.0, None, ALU.max))
            own()
            dve.sem_inc(ln_var_ok, 1)
            for ct in range(KT):
                step.sign(dve.tensor_tensor(ln_t[:, ct, :], yT[:, ct, :], mu[:, :], ALU.subtract))
            own()
            dve.wait_ge(ln_rstd_ok, 1)
            for ct in range(KT):
                dve.tensor_tensor(ln_t[:, ct, :], ln_t[:, ct, :], rstd[:, :], ALU.mult).then_inc(ln_in, 1)
            for n in range(2):
                for t in range(LAT_TT):
                    b = d_bank()
                    cs = slice(n * NF, (n + 1) * NF)
                    dve.tensor_tensor(gated[:, :], b[:, :], sg_conv[:, t, cs], ALU.mult).then_inc(d_empty, 1)
                    dve.wait_ge(d_empty, groups[0])
                    step.sign(dve.tensor_tensor(m[:, t, cs], m[:, t, cs], gated[:, :], ALU.add))
                    own()
                    dve.sem_inc(m_ok, 1)
            dve.wait_ge(x_again_in, 16)
            for n in range(2):
                for t in range(LAT_TT):
                    b = d_bank()
                    cs = slice(n * NF, (n + 1) * NF)
                    dve.tensor_tensor(gated[:, :], b[:, :], gt1[:, cs], ALU.mult).then_inc(d_empty, 1)
                    dve.wait_ge(d_empty, groups[0])
                    step.sign(dve.tensor_tensor(x1[:, t, cs], x1[:, t, cs], gated[:, :], ALU.add))
                    own()
            dve.sem_inc(x1_ok, 1)
            dve.sem_inc(ms_free, 1)
            dve.wait_ge(late_in, 48)
            step.sign(dve.scalar_tensor_tensor(a2[:, :], a2[:, :], 1.0, g_ffn_b[:, :], ALU.add, ALU.mult))
            own()
            dve.wait_ge(x1_pow, 1)
            for t in range(LAT_TT):
                step.sign(dve.scalar_tensor_tensor(h2[:, t, :], x1[:, t, :], stat[:, 16 + t:17 + t], a2[:, :], ALU.mult, ALU.mult))
            own()
            for t in range(LAT_TT):
                dve.tensor_tensor(h2[:, t, :], h2[:, t, :], sh2[:, :], ALU.add).then_inc(h2_ok, 1)
            dve.wait_ge(h2_ok, LAT_TT)
            step.sign(dve.tensor_copy(h2_hi[:, :, :], h2[:, :, :]))
            own()
            step.sign(dve.tensor_tensor(h2_lo[:, :, :], h2[:, :, :], h2_hi[:, :, :].bitcast(F32), ALU.subtract))

            b = d_bank()
            for t in range(LAT_TT):
                ins = dve.tensor_tensor(logits[:, t, :], b[:, t * E:(t + 1) * E], b_router_b[:, :], ALU.add)
            ins.then_inc(d_empty, 1)
            dve.wait_ge(d_empty, groups[0])
            for t in range(LAT_TT):
                step.sign(dve.max(top8[:, t, :], logits[:, t, :]))
            own()
            for t in range(LAT_TT):
                step.sign(dve.tensor_scalar(need[:, t, 3:4], top8[:, t, 0:1], -1.0, None, ALU.mult))
            own()
            dve.sem_inc(max_ok, 1)
            for t in range(LAT_TT):
                kth = top8[:, t, TOPK - 1:TOPK]
                step.sign(dve.tensor_scalar(above[:, t, :], logits[:, t, :], kth, None, ALU.is_gt))
                step.sign(dve.tensor_scalar(equal[:, t, :], logits[:, t, :], kth, None, ALU.is_equal))
            own()
            for t in range(LAT_TT):
                step.sign(dve.tensor_reduce(need[:, t, 0:1], above[:, t, :], AX_X, ALU.add))
                step.sign(dve.tensor_tensor_scan(nth[:, t, :], ones[:, 0:E], equal[:, t, :], 0.0, ALU.mult, ALU.add))
            own()
            for t in range(LAT_TT):
                step.sign(dve.tensor_scalar(need[:, t, 1:2], need[:, t, 0:1], -1.0, float(TOPK), ALU.mult, ALU.add))
            own()
            for t in range(LAT_TT):
                step.sign(dve.scalar_tensor_tensor(sel[:, t, :], nth[:, t, :], need[:, t, 1:2], equal[:, t, :], ALU.is_le, ALU.mult))
            own()
            step.sign(dve.tensor_tensor(sel[:, :, :], sel[:, :, :], above[:, :, :], ALU.add))
            own()
            dve.sem_inc(sel_ok, 1)
            dve.wait_ge(exp_ok, LAT_TT)
            step.sign(dve.tensor_tensor(expo[:, :, :], expo[:, :, :], sel[:, :, :], ALU.mult))
            own()
            step.sign(dve.tensor_reduce(need[:, :, 2], expo[:, :, :], AX_X, ALU.add))
            own()
            step.sign(dve.reciprocal(need[:, :, 2], need[:, :, 2]))
            own()
            for t in range(LAT_TT):
                step.sign(dve.tensor_scalar(prob[:, t, :], expo[:, t, :], need[:, t, 2:3], None, ALU.mult))
            b = d_bank()
            step.sign(dve.tensor_copy(rank[:, :, :], b[:, 0:LAT_TT * E].rearrange("p (t e) -> p t e", e=E)))
            for j in range(4):
                step.sign(dve.tensor_scalar(blocks[:, j, :], b[:, LAT_TT * E:(LAT_TT + 1) * E], float(j * SLOTS), None, ALU.is_gt))
            own()
            dve.tensor_tensor(blocks[:, 0:2, :], blocks[:, 0:2, :], blocks[:, 2:4, :], ALU.add).then_inc(d_empty, 1)
            dve.wait_ge(d_empty, groups[0])
            step.sign(dve.tensor_tensor(blocks[:, 0, :], blocks[:, 0, :], blocks[:, 1, :], ALU.add))
            own()
            step.sign(dve.tensor_tensor_scan(ends[:, 1, :], ones[:, 0:E], blocks[:, 0, :], 0.0, ALU.mult, ALU.add))
            own()
            step.sign(dve.tensor_tensor(ends[:, 0, :], ends[:, 1, :], blocks[:, 0, :], ALU.subtract))
            step.sign(dve.tensor_scalar(above[:, :, :], sel[:, :, :], -BIG, BIG, ALU.mult, ALU.add))
            own()
            step.sign(dve.tensor_tensor(rank[:, :, :], rank[:, :, :], above[:, :, :], ALU.add))
            own()
            first_item = ends[:, 0, :].unsqueeze(1).to_broadcast([P, LAT_TT, E])
            step.sign(dve.scalar_tensor_tensor(rank[:, :, :], first_item, float(SLOTS), rank[:, :, :], ALU.mult, ALU.add))
            own()
            dve.sem_inc(rank_ok, 1)
            b = d_bank()
            step.sign(dve.tensor_copy(rankT[:, :, :], b[0:E, 0:LAT_TT * P].rearrange("p (t c) -> p t c", c=P)))
            dve.tensor_copy(probT[:, :, :], b[0:E, LAT_TT * P:2 * LAT_TT * P].rearrange("p (t c) -> p t c", c=P)).then_inc(d_empty, 1)
            b = d_bank()
            dve.tensor_copy(ecol[:, 0:1], b[0:E, 0:1])
            dve.tensor_copy(ecol[:, 1:2], b[0:E, P:P + 1]).then_inc(d_empty, 1)
            dve.wait_ge(d_empty, groups[0])
            dve.wait_ge(const_ok, N_CONST + 2)
            step.sign(dve.tensor_scalar(one_item[:, :], item_no[0:E, :], ecol[:, 1:2], None, ALU.is_lt))
            own()
            step.sign(dve.scalar_tensor_tensor(one_item[:, :], item_no[0:E, :], ecol[:, 0:1], one_item[:, :], ALU.is_ge, ALU.mult))
            own()
            dve.sem_inc(one_item_ok, 1)
            b = d_bank()
            for t in range(LAT_TT):
                step.sign(dve.scalar_tensor_tensor(slot_tok[:, t, :], item_no[:, :], -float(SLOTS), b[:, t * ITEM_COLS:(t + 1) * ITEM_COLS],
                                                   ALU.mult, ALU.add))
            step.sign(dve.tensor_copy(item_expert[0:1, ITEM_COLS:ITEM_COLS + 1], ends[0:1, 1, E - 1:E]))
            dve.tensor_copy(prob_tok[:, :, :], b[:, LAT_TT * ITEM_COLS:2 * LAT_TT * ITEM_COLS].rearrange("p (t i) -> p t i", i=ITEM_COLS))
            dve.tensor_copy(item_expert[0:1, 0:ITEM_COLS], b[0:1, 2 * LAT_TT * ITEM_COLS:(2 * LAT_TT + 1) * ITEM_COLS]).then_inc(d_empty, 1)
            dve.wait_ge(d_empty, groups[0])
            own()
            dve.sem_inc(items_ok, 1)

            items = item_count(dve)
            HALF = KT // 2
            dve.wait_ge(y_full, 2)
            step.sign(dve.memset(y[:, :], 0.0))
            step.sign(dve.memset(scatter[:, :, :], 0.0))
            own()
            dve.sem_inc(y_out, 2)
            dve.sem_inc(sc_out, 1)
            dve.sem_inc(lo_ok, LO_PRIME)

            def make_pick(i):
                for t in range(LAT_TT):
                    ins = dve.tensor_scalar(pick[:, t, :], slot_of_col[:, 0:SLOTS], slot_tok[:, t, bass.ds(i, 1)], None, ALU.is_equal)
                ins.then_inc(pick_ok, 1)

            def take_xs(i):
                for half in range(2):
                    dve.wait_ge(xs_full, i * 2 + (half + 1))
                    dve.tensor_copy(xs[:, half * HALF:(half + 1) * HALF, :], bank[6 + half][:, :].rearrange("p (k c) -> p k c", c=P)).then_inc(xs_out, 1)

            def split_lo(i, j):
                for half in range(2):
                    ks = slice(half * HALF, (half + 1) * HALF)
                    dve.wait_ge(hi_ok, i * (2 * CPI) + (2 * j + half + 1))
                    raw = ring[(NSTREAM + j) % NRING][:, ks, :]
                    dve.tensor_tensor(w_lo[j % NPART][:, ks, :], raw, w_hi[j % NPART][:, ks, :].bitcast(F32), ALU.subtract).then_inc(lo_ok, 1)

            make_pick(0)
            take_xs(0)
            LOOP_STEPS = 4
            with dve.Fori(0, items) as i:
                e = dve.value_load(item_expert[0:1, bass.ds(i, 1)], min_val=0, max_val=E - 1)
                steps = [0]

                def link(ins):
                    ins.then_inc(loop_step, 1)
                    steps[0] += 1
                    dve.wait_ge(loop_step, i * LOOP_STEPS + steps[0])

                for t in range(LAT_TT):
                    ins = dve.tensor_scalar(weigh[:, t, :], slot_of_col[:, :], slot_tok[:, t, bass.ds(i, 1)],
                                            prob_tok[:, t, bass.ds(i, 1)], ALU.is_equal, ALU.mult)
                ins.then_inc(weigh_ok, 1)
                split_lo(i, 0)
                split_lo(i, 1)
                make_pick(i + 1)
                split_lo(i, 2)
                split_lo(i, 3)
                split_lo(i, 4)
                take_xs(i + 1)
                b1 = lambda part: b1T[:, bass.ds(e, 1), part * (FF // P):(part + 1) * (FF // P)] \
                    .rearrange("p a j -> p (a j)").unsqueeze(2).to_broadcast([P, FF // P, SLOTS])
                dve.wait_ge(ht_full, i * 2 + 1)
                dve.tensor_tensor(lin[:, :, :], bank[5][:, :].rearrange("p (j c) -> p j c", c=SLOTS), b1(1), ALU.add).then_inc(ht_out, 1)
                dve.wait_ge(ht_full, i * 2 + 2)
                dve.tensor_tensor(glu[:, :, :], bank[4][:, :].rearrange("p (j c) -> p j c", c=SLOTS), b1(0), ALU.add).then_inc(ht_out, 1)
                dve.wait_ge(ht_out, i * 2 + 2)
                dve.tensor_scalar(glu[:, :, :], glu[:, :, :], LIMIT, None, ALU.min).then_inc(glu_ok, 1)
                link(dve.tensor_scalar(lin[:, :, :], lin[:, :, :], LIMIT, -LIMIT, ALU.min, ALU.max))
                dve.wait_ge(glu_ok, i + 1)
                link(dve.scalar_tensor_tensor(lin[:, :, :], lin[:, :, :], 1.0, glu[:, :, :], ALU.add, ALU.mult))
                dve.wait_ge(sig_ok, i + 1)
                link(dve.tensor_tensor(hf[:, :, :], lin[:, :, :], sig[:, :, :], ALU.mult))
                link(dve.tensor_copy(hs[:, :, 0:SLOTS], hf[:, :, :]))
                dve.tensor_tensor(hs[:, :, SLOTS:2 * SLOTS], hf[:, :, :], hs[:, :, 0:SLOTS].bitcast(F32), ALU.subtract).then_inc(hs_ok, 1)
                split_lo(i, 5)
                assert steps[0] == LOOP_STEPS
            dve.wait_ge(acc_full, 1)
            for t in range(LAT_TT):
                for n in range(2):
                    cs = slice(n * NF, (n + 1) * NF)
                    step.sign(dve.tensor_tensor(hid[:, (2 * t + n) * NF:(2 * t + n + 1) * NF], bank[2 * t + n][:, :], gt2[:, cs], ALU.mult))
            own()
            for t in range(LAT_TT):
                step.sign(dve.tensor_tensor(x1[:, t, :], x1[:, t, :], hid[:, t * D:(t + 1) * D], ALU.add))
                own()
                dve.sem_inc(x2_ok, 1)
            dve.wait_ge(g_final_in, 16)
            dve.wait_ge(fin_pow, 1)
            for t in range(LAT_TT):
                dve.scalar_tensor_tensor(out_sb[:, t, :], x1[:, t, :], stat[:, 20 + t:21 + t], g_final_b[:, :], ALU.mult, ALU.mult).then_inc(out_ok, 1)



_INS = ["x", "c", "ctx", "c_ctx", "w_ada", "b_ada", "g_mix_norm", "w_in", "w_dw", "b_dw", "g_conv_ln", "b_conv_ln",
        "w_conv_out", "w_alpha", "b_alpha", "g_gla_norm", "w_gla_out", "w_out", "g_ffn_norm", "w_router", "b_router",
        "w_exp_in", "b_exp_in", "w_exp_out", "b_exp_out", "g_final"]


def kernel(**inputs):
    import numpy as np
    import concourse.bacc as bacc
    from concourse.bass_utils import run_bass_kernel_spmd

    nc = bacc.Bacc("TRN2", target_bir_lowering=False, num_devices=1)
    arrays, args = {}, []
    for name in _INS:
        a = np.ascontiguousarray(inputs[name])
        arrays[f"in_{name}"] = a
        args.append(nc.dram_tensor(f"in_{name}", a.shape, mybir.dt.from_np(a.dtype), kind="ExternalInput").ap())
    out = nc.dram_tensor("out_0", inputs["x"].shape, F32, kind="ExternalOutput").ap()
    build(nc, *args, out)
    r = run_bass_kernel_spmd(nc, [arrays], core_ids=[0])
    return r.results[0]["out_0"]
```

```python
from contextlib import ExitStack

import concourse.bass as bass
from concourse import mybir

F32 = mybir.dt.float32
F32R = mybir.dt.float32r
I32 = mybir.dt.int32
ALU = mybir.AluOpType
ACT = mybir.ActivationFunctionType
AX_X = mybir.AxisListType.X

P = 128
EPS = 1e-6
TAU = 16.0
ALPHA = 1.702
LIMIT = 7.0
BIG = 65536.0


class Tally:

    def __init__(self, sem):
        self.sem, self.n = sem, 0

    def sign(self, ins):
        ins.then_inc(self.sem, 1)
        self.n += 1


def build(nc, x, c, ctx_tokens, c_ctx, w_ada, b_ada, g_mix_norm, w_in, w_dw, b_dw, g_conv_ln, b_conv_ln,
          w_conv_out, w_alpha, b_alpha, g_gla_norm, w_gla_out, w_out, g_ffn_norm, w_router, b_router,
          w_exp_in, b_exp_in, w_exp_out, b_exp_out, g_final, out, debug=None):
    _, SEQ, D = x.shape
    LCTX = ctx_tokens.shape[1]
    T = LCTX + SEQ
    KT = D // P
    CTX_TT, LAT_TT = LCTX // P, SEQ // P
    TT = CTX_TT + LAT_TT
    TAPS = w_dw.shape[1]
    PAD = TAPS // 2
    GRID_W = 64
    ROWS = SEQ // GRID_W
    RANK, KD = w_alpha.shape[2], w_alpha.shape[3]
    DK = P
    HEADS = KD // DK
    DV = g_gla_norm.shape[1]
    CHUNK = 64
    NCHUNK = T // CHUNK
    E, FF = w_exp_in.shape[1], w_exp_out.shape[2]
    TOPK = 4
    HALF_P = P // 2
    SLOTS = 2 * HALF_P
    NF = 512
    ITEMS_MAX = (SEQ * TOPK + E * (SLOTS - 1)) // SLOTS
    ITEMS_OF_ONE = (SEQ + SLOTS - 1) // SLOTS
    ITEM_COLS = ITEMS_MAX + 1
    QUAD = 32
    QUADS = P // QUAD
    HD = 2 * HEADS
    c0 = dict(conv_a=0, conv_b=D, q=2 * D, k=2 * D + KD, v=2 * D + 2 * KD)
    c0["g"] = c0["v"] + HEADS * DV
    c0["a_lr"] = c0["g"] + HEADS * DV
    c0["gate_conv"] = c0["a_lr"] + 2 * RANK
    c0["gate_gla"] = c0["gate_conv"] + D

    def chunked(w, col):
        return w.rearrange("(t p) n -> p t n", p=P)[:, :, col:col + NF]

    stream = []
    ada = lambda part: [chunked(w_ada[0], part * D + n * NF) for n in range(D // NF)]
    proj = lambda name, n: chunked(w_in[0], c0[name] + n * NF)
    stream += ada(0) + ada(1)
    stream += [proj("k", 0), proj("q", 0), proj("conv_a", 0), proj("conv_b", 0), proj("conv_a", 1), proj("conv_b", 1)]
    stream += [proj(name, n) for name in ("v", "g", "gate_conv", "gate_gla") for n in range(2)]
    n_proj = len(stream)
    dense = lambda w: [chunked(w[0], n * NF) for n in range(D // NF)]
    stream += dense(w_gla_out) + dense(w_conv_out)
    stream += ada(2) + ada(3) + ada(4)
    stream += dense(w_out) + ada(5)
    NSTREAM = len(stream)
    NRING = 3
    UK, UN = 2, 2 * NF
    UPP = KT // UK
    PAIRS = 2 * FF // UN
    UPI = UPP * (PAIRS + 1)
    JH = FF // P // 2

    base = (nc.sbuf_base + 511) // 512 * 512
    KB = 1024

    def at(name, kb, shape, dt=F32):
        return nc.alloc_sbuf_tensor_at(name, list(shape), dt, offset=base + int(kb * KB))

    class Bump:

        def __init__(self, kb, end):
            self.kb, self.end = kb, end

        def __call__(self, name, shape, dt=F32):
            size = 4
            for s in shape[1:]:
                size *= s
            t = at(name, self.kb, shape, dt)
            self.kb += (size + 63) // 64 * 64 / KB
            assert self.kb <= self.end, name
            return t

    ring = [at(f"weights{s}", 16 * s, [P, KT, NF]) for s in range(NRING)]
    small = Bump(48, 68)
    ident = small("ident", [P, P])
    ones = small("ones", [P, P])
    slot_no = small("slot_no", [P, SLOTS])
    slot_twice = small("slot_twice", [P, 2, 2, HALF_P])
    mask_f = small("mask_f", [P, P])
    mask_b = small("mask_b", [P, P])
    before = small("before", [P, P])
    scan_keep = small("scan_keep", [P, T])
    vecT = small("vecT", [P, 112])
    wdwT = small("wdwT", [P, KT, TAPS])
    decay = small("decay", [P, HD, NCHUNK])
    stat = small("stat", [P, 32])
    a_lr_w = small("a_lr_w", [P, KT, 2 * RANK])
    wal = small("wal", [QUAD + RANK, KD])
    wr = small("wr", [P, KT, E])
    sc_act = small("sc_act", [P, 2 * KT])
    scT = small("scT", [P, KT, QUAD])
    tile_sum = small("tile_sum", [P, 2])
    tile_sum_all = small("tile_sum_all", [P, P])
    modT = small("modT", [P, 2 * KT, 2])
    b1T = small("b1T", [P, E, 2 * FF // P])
    slot_tok = small("slot_tok", [P, LAT_TT, ITEM_COLS])
    prob_tok = small("prob_tok", [P, LAT_TT, ITEM_COLS])
    item_expert = small("item_expert", [1, ITEM_COLS + 1], I32)
    item_wide = small("item_wide", [1, ITEM_COLS], I32)
    neg_half = small("neg_half", [P, 8])
    x1 = at("x1", 68, [P, LAT_TT, D])
    gt2 = at("gt2", 76, [P, D])
    h2 = at("h2", 80, [P, LAT_TT, D])
    b2_rows = at("b2_rows", 88, [E, D])
    tokens = at("tokens", 68, [P, TT, D])
    sq_junk = at("sq_junk", 116, [P, D])
    o_junk = at("o_junk", 188, [P, DV])
    mod_part = at("mod_part", 84, [P, 2 * D])
    b1_rows = at("b1_rows", 92, [E, 2 * FF])
    vec_rows = at("vec_rows", 100, [112, P])
    wdw_rows = at("wdw_rows", 132, [TAPS, D])
    hT = at("hT", 100, [P, KT, T])
    a_lrT = at("a_lrT", 92, [QUAD + RANK, T])
    k_end = at("k_end", 116, [P, HD, TT, P])
    q_dec = at("q_dec", 132, [P, HD, SEQ])
    scores = at("scores", 140, [P, HEADS, LAT_TT, P])
    yT = at("yT", 144, [P, KT, SEQ])
    u = at("u", 152, [P, KT, ROWS, GRID_W + 2 * PAD])
    kT = at("kT", 164, [P, HEADS, T])
    qT = at("qT", 172, [P, HEADS, SEQ])
    z_t = at("z_t", 176, [P, T])
    e_t = at("e_t", 178, [P, T])
    la_t = at("la_t", 180, [P, T])
    pre_t = at("pre_t", 182, [P, T])
    te_t = at("te_t", 184, [P, T])
    et_t = at("et_t", 186, [P, T])
    kte_t = at("kte_t", 188, [P, T])
    v = at("v", 190, [P, TT, HEADS * DV])
    state = at("state", 68, [P, 4, HD, DV])
    sgn = at("sgn", 164, [P, LAT_TT, HEADS * DV])
    sg_conv = at("sg_conv", 172, [P, LAT_TT, D])
    sg_gla = at("sg_gla", 180, [P, LAT_TT, D])
    gla_g = at("gla_g", 206, [P, DV])
    o_sb = at("o_sb", 116, [P, LAT_TT, HEADS * DV])
    oT = at("oT", 124, [P, KT, SEQ])
    b_ada_b = at("b_ada_b", 100, [P, 4 * D])
    late_part = at("late_part", 92, [P, 2, NF])
    gt1 = at("gt1", 96, [P, D])
    sh2 = at("sh2", 202, [P, D])
    a2 = at("a2", 198, [P, D])
    ysq = at("ysq", 152, [P, KT, SEQ])
    ln_wide = at("ln_wide", 160, [P, 2, LAT_TT, P])
    m = at("m", 152, [P, LAT_TT, D])
    gated = at("gated", 164, [P, NF])
    mT = at("mT", 124, [P, KT, SEQ])
    g_ffn_b = at("g_ffn_b", 190, [P, D])
    b_router_b = at("b_router_b", 194, [P, E])
    h2T = at("h2T", 132, [P, KT, SEQ])
    rt = Bump(152, 164)
    logits = rt("logits", [P, LAT_TT, E])
    top8 = rt("top8", [P, LAT_TT, 8])
    above = rt("above", [P, LAT_TT, E])
    equal = rt("equal", [P, LAT_TT, E])
    nth = rt("nth", [P, LAT_TT, E])
    need = rt("need", [P, LAT_TT, 4])
    sel = rt("sel", [P, LAT_TT, E])
    expo = rt("expo", [P, LAT_TT, E])
    prob = rt("prob", [P, LAT_TT, E])
    rank = rt("rank", [P, LAT_TT, E])
    blocks = rt("blocks", [P, ITEMS_OF_ONE, E])
    ends = rt("ends", [P, 3, E])
    ecol = rt("ecol", [E, 4])
    one_item = rt("one_item", [E, ITEM_COLS])
    spill = rt("spill", [1, ITEM_COLS])
    item_no = rt("item_no", [P, ITEM_COLS])
    rankT = rt("rankT", [E, LAT_TT, P])
    probT = rt("probT", [E, LAT_TT, P])
    unit = [at(f"unit{n}", 8 * n if n < 6 else 100 + 8 * (n - 6), [P, UK, UN]) for n in range(UPI)]
    hid = at("hid", 164, [P, 2, PAIRS, NF])
    xs = at("xs", 172, [P, KT, SLOTS])
    hs = at("hs", 176, [P, 2, 2 * JH, HALF_P])
    y = at("y", 180, [P, 2, NF])
    scatter = at("scatter", 184, [P, LAT_TT, 2, P])
    pick = at("pick", 186, [P, LAT_TT, SLOTS])
    weigh = at("weigh", 187, [P, LAT_TT, 2, P])
    swi = at("swi", 189, [P, 2, 2, 2 * JH, HALF_P])
    sig = at("sig", 197, [P, 2, 2 * JH, HALF_P])
    g_final_b = at("g_final_b", 201, [P, D])
    sums = at("sums", 148, [P, LAT_TT, D])
    out_sb = at("out_sb", 100, [P, LAT_TT, D])

    stack = ExitStack()
    with stack:
        def sem(name):
            return stack.enter_context(nc.semaphore(name))

        bank = [stack.enter_context(nc.psum_tensor(f"bank{i}", [P, NF], F32)) for i in range(8)]
        A_BANKS, D_BANKS = bank[0:4], bank[4:8]

        landed = [sem(f"weights_landed{s}") for s in range(NRING)]
        vec_in, tok_in, bias_in, rows_in = sem("vec_in"), sem("tok_in"), sem("bias_in"), sem("rows_in")
        b_ada_in, x_again_in, late_in = sem("b_ada_in"), sem("x_again_in"), sem("late_in")
        const_ok = sem("const_ok")
        a_full, a_empty = sem("a_bank_full"), sem("a_bank_empty")
        d_full, d_empty = sem("d_bank_full"), sem("d_bank_empty")
        dve_ok, act_ok, pool_ok = sem("dve_step"), sem("act_step"), sem("pool_step")
        sums_ok, pow_ok = sem("squares_summed"), sem("rstd_ok")
        sc_sig, sc_ok, norm_ok, mod_ok = sem("c_sigmoid"), sem("silu_c_ok"), sem("tokens_normed"), sem("mod_ok")
        z_ok, ln_ok, te_ok, et_ok, kte_ok = sem("z_ok"), sem("ln_ok"), sem("te_ok"), sem("et_ok"), sem("kte_ok")
        conv_ok, ysq_ok, act_conv_ok = sem("conv_ok"), sem("ysq_ok"), sem("act_conv_ok")
        oss_ok, orstd_ok, ln_cols_ok, hT_ok = sem("o_squares"), sem("o_rstd"), sem("ln_columns"), sem("hT_ok")
        ln_var_ok, ln_rstd_ok, ln_in, ln_sig = sem("ln_var"), sem("ln_rstd"), sem("ln_in"), sem("ln_sig")
        x1_ok, x1_sum, x1_pow, h2_ok, exp_ok = sem("x1_ok"), sem("x1_sum"), sem("x1_rstd"), sem("h2_ok"), sem("exp_ok")
        m_ok, ms_free, max_ok, sel_ok, rank_ok = sem("m_ok"), sem("m_unused"), sem("max_ok"), sem("sel_ok"), sem("rank_ok")
        one_item_ok, items_ok, x2_ok, g_final_in = sem("one_item_ok"), sem("items_ok"), sem("x2_ok"), sem("g_final_in")
        def both(name):
            return [sem(name + "_a"), sem(name + "_b")]

        unit_landed = [sem(f"unit_landed{n}") for n in range(UPI)]
        unit_used, items_done = sem("unit_used"), sem("items_done")
        hid_out, ht_full, ht_out, y_out = both("hid_out"), both("hidT_full"), both("hidT_out"), both("y_out")
        glu_ok, sig_ok, hs_ok = both("glu_ok"), both("sig_ok"), both("hs_ok")
        xs_full, xs_out = sem("xs_full"), sem("xs_out")
        sc_full, sc_out = sem("scatter_full"), sem("scatter_out")
        pick_ok, weigh_ok = sem("pick_ok"), sem("weigh_ok")
        swi_step = sem("swiglu_step")
        acc_full, fin_sum, fin_pow, out_ok, stored = sem("acc_full"), sem("fin_sum"), sem("fin_pow"), sem("out_ok"), sem("stored")

        block = stack.enter_context(nc.Block())
        N_IDENT = 4
        N_CONST = 31
        A, B = 0, 1

        def CHUNK_OF(direction, s):
            n_ctx = LCTX // CHUNK
            return s if direction == 0 else n_ctx - 1 - s if s < n_ctx else NCHUNK - 1 + n_ctx - s

        def item_count(eng):
            eng.wait_ge(items_ok, 1)
            return eng.value_load(item_expert[0:1, ITEM_COLS:ITEM_COLS + 1], min_val=1, max_val=ITEMS_MAX)

        def front_landed(n):
            return landed[n % NRING], 16 * (n // NRING + 1)

        def item_of(eng, i):
            return eng.value_load(item_wide[0:1, bass.ds(i, 1)], min_val=0, max_val=1)

        def hid_tile(slot):
            g, half = divmod(slot, 2)
            return (NF // P) * (g // 2) + 2 * half + g % 2

        chunk_used = []
        mark = {}

        @block.tensor
        def _(pe):
            na, nd, taken = [0], [0], [0]

            def a_open():
                if na[0] >= 4:
                    pe.wait_ge(a_empty, na[0] - 3)
                na[0] += 1
                return A_BANKS[(na[0] - 1) % 4]

            def d_open():
                if nd[0] >= 4:
                    pe.wait_ge(d_empty, nd[0] - 3)
                nd[0] += 1
                return D_BANKS[(nd[0] - 1) % 4]

            def next_chunk():
                n = taken[0]
                pe.wait_ge(*front_landed(n))
                taken[0] += 1
                return ring[n % NRING]

            def accumulate(dst, lhs, rhs):
                for k in range(KT):
                    ins = pe.matmul(dst, lhs(k), rhs(k), start=(k == 0), stop=(k == KT - 1))
                return ins

            def used_by_a():
                chunk_used.append((a_full, na[0]))

            def used_by_d():
                chunk_used.append((d_full, nd[0]))

            def transposed(src):
                for g in range(KT // 2):
                    b = a_open()
                    for kk in range(2):
                        for t in range(LAT_TT):
                            kt = 2 * g + kk
                            ins = pe.transpose(b[:, (kk * LAT_TT + t) * P:(kk * LAT_TT + t + 1) * P],
                                               src[:, t, kt * P:(kt + 1) * P], ident[:, :])
                    ins.then_inc(a_full, 1)

            def ada_chunk():
                w = next_chunk()
                b = a_open()
                for r in range(KT // QUADS):
                    for q in range(QUADS):
                        k = r * QUADS + q
                        ins = pe.matmul(b[q * QUAD:(q + 1) * QUAD, :], scT[:, k, :], w[:, k, :], start=(r == 0),
                                        stop=(r == KT // QUADS - 1), skip_group_check=True)
                ins.then_inc(a_full, 1)
                used_by_a()

            pe.wait_ge(const_ok, N_IDENT)
            pe.wait_ge(vec_in, 9 * 16)
            pe.transpose(d_open()[:, 0:112], vec_rows[:, :], ident[0:112, 0:112]).then_inc(d_full, 1)
            pe.wait_ge(sc_ok, 1)
            ada_chunk()
            ada_chunk()
            pe.wait_ge(norm_ok, TT)
            for kt in range(KT):
                b = a_open()
                for t in range(TT):
                    ins = pe.transpose(b[:, t * P:(t + 1) * P], tokens[:, t, kt * P:(kt + 1) * P], ident[:, :])
                ins.then_inc(a_full, 1)
            ada_chunk()
            ada_chunk()
            pe.wait_ge(const_ok, N_CONST)
            pe.wait_ge(rows_in, 32)
            b = d_open()
            for kt in range(KT):
                ins = pe.transpose(b[:, kt * TAPS:(kt + 1) * TAPS], wdw_rows[:, kt * P:(kt + 1) * P], ident[0:TAPS, 0:TAPS])
            ins.then_inc(d_full, 1)
            pe.wait_ge(a_empty, na[0])
            b = d_open()
            for j in range(2 * KT):
                ins = pe.matmul(b[:, 2 * j:2 * j + 2], mod_part[:, j * P:(j + 1) * P], tile_sum[:, :], start=True, stop=True)
            ins.then_inc(d_full, 1)
            b = d_open()
            for part in range(2):
                for slot in range(FF // P):
                    j = hid_tile(slot)
                    cols = b1_rows[:, j * 2 * P:(j + 1) * 2 * P].rearrange("e (m two) -> e two m", two=2)[:, part, :]
                    g = part * (FF // P) + slot
                    ins = pe.transpose(b[:, g * E:(g + 1) * E], cols, ident[0:E, 0:E])
            ins.then_inc(d_full, 1)
            pe.wait_ge(hT_ok, KT)
            pe.wait_ge(bias_in, 5 * 16)
            b = a_open()
            for k in range(KT):
                for d in range(2):
                    ins = pe.matmul(b[d * QUAD:d * QUAD + RANK, :], a_lr_w[:, k, d * RANK:(d + 1) * RANK], hT[:, k, :],
                                    start=(k == 0), stop=(k == KT - 1), skip_group_check=True)
            ins.then_inc(a_full, 1)
            n_a_lr = na[0]
            w = next_chunk()
            for h in range(HEADS):
                b = a_open()
                accumulate(b[:, :], lambda k: w[:, k, h * P:(h + 1) * P], lambda k: hT[:, k, :]).then_inc(a_full, 1)
            used_by_a()
            w = next_chunk()
            for h in range(HEADS):
                b = a_open()
                accumulate(b[:, 0:SEQ], lambda k: w[:, k, h * P:(h + 1) * P], lambda k: hT[:, k, LCTX:T]).then_inc(a_full, 1)
            used_by_a()
            pe.wait_ge(a_empty, n_a_lr)
            def v_chunk():
                w = next_chunk()
                for t in range(TT):
                    b = a_open()
                    accumulate(b[:, :], lambda k: hT[:, k, t * P:(t + 1) * P], lambda k: w[:, k, :]).then_inc(a_full, 1)
                used_by_a()

            for it in range(HD + 1):
                if it < HD:
                    d, h = divmod(it, HEADS)
                    b = d_open()
                    r = slice(d * QUAD, d * QUAD + RANK)
                    pe.matmul(b[:, :], wal[r, h * P:(h + 1) * P], a_lrT[r, :], start=True, stop=True).then_inc(d_full, 1)
                    for g in (2 * it, 2 * it + 1):
                        if g % 4 == 0:
                            w = next_chunk()
                        b = a_open()
                        cs = slice((g % 4) * P, (g % 4 + 1) * P)
                        accumulate(b[:, 0:SEQ], lambda k: w[:, k, cs], lambda k: hT[:, k, LCTX:T]).then_inc(a_full, 1)
                        if g % 4 == 3:
                            used_by_a()
                if it == HD:
                    mark["conv_in"] = na[0]
                    v_chunk()
                if it >= 1:
                    pe.wait_ge(kte_ok, it)
                    b = a_open()
                    for t in range(TT):
                        ins = pe.transpose(b[:, t * P:(t + 1) * P], kte_t[:, t * P:(t + 1) * P], ident[:, :])
                    ins.then_inc(a_full, 1)
                    b = d_open()
                    for t in range(LAT_TT):
                        ins = pe.matmul(b[:, t * P:(t + 1) * P], te_t[:, t * P:(t + 1) * P],
                                        q_dec[:, it - 1, t * P:(t + 1) * P], start=True, stop=True)
                    ins.then_inc(d_full, 1)
            v_chunk()
            mark["v"] = na[0]
            for n in range(6):
                w = next_chunk()
                for t in range(LAT_TT):
                    b = a_open()
                    accumulate(b[:, :], lambda k: hT[:, k, LCTX + t * P:LCTX + (t + 1) * P], lambda k: w[:, k, :]).then_inc(a_full, 1)
                used_by_a()
                if n == 1:
                    mark["g"] = na[0]
            pe.wait_ge(ysq_ok, KT)
            b = d_open()
            for n, src in enumerate((yT, ysq)):
                for t in range(LAT_TT):
                    ins = accumulate(b[:, n * LAT_TT + t:n * LAT_TT + t + 1], lambda k: src[:, k, t * P:(t + 1) * P],
                                     lambda k: ones[:, 0:1])
            ins.then_inc(d_full, 1)
            pe.wait_ge(a_empty, mark["v"])
            for s in range(NCHUNK - 1):
                for hd in range(HD):
                    ck = CHUNK_OF(hd // HEADS, s)
                    r = slice((ck % 2) * CHUNK, (ck % 2 + 1) * CHUNK)
                    h = hd % HEADS
                    b = d_open()
                    pe.matmul(b[:, 0:DV], k_end[r, hd, ck // 2, :], v[r, ck // 2, h * DV:(h + 1) * DV],
                              start=True, stop=True).then_inc(d_full, 1)
            pe.wait_ge(d_empty, nd[0])
            mark["before_o"] = nd[0]
            for t in range(LAT_TT):
                for h in range(HEADS):
                    b = d_open()
                    pe.matmul(b[:, 0:DV], scores[:, h, t, :], v[:, CTX_TT + t, h * DV:(h + 1) * DV], start=True, stop=False,
                              skip_group_check=True)
                    for d in range(2):
                        for half in range(2):
                            ck = 2 * (CTX_TT + t) + half
                            s = ck if d == 0 else NCHUNK - 1 + LCTX // CHUNK - ck
                            hd = d * HEADS + h
                            q0 = t * P + half * CHUNK
                            ins = pe.matmul(b[half * CHUNK:(half + 1) * CHUNK, 0:DV], q_dec[:, hd, q0:q0 + CHUNK],
                                            state[:, s - LCTX // CHUNK, hd, :], start=False, stop=(d == 1), skip_group_check=True)
                    ins.then_inc(d_full, 1)
            mark["o"] = nd[0]
            pe.wait_ge(ln_cols_ok, 1)
            b = d_open()
            for n in range(2):
                for t in range(LAT_TT):
                    ins = pe.matmul(b[:, (n * LAT_TT + t) * P:(n * LAT_TT + t + 1) * P], ln_wide[:, n, t, :], ident[:, :],
                                    start=True, stop=True)
            ins.then_inc(d_full, 1)
            pe.wait_ge(d_empty, mark["o"])
            transposed(o_sb)

            def token_rows(src):
                for n in range(2):
                    w = next_chunk()
                    for t in range(LAT_TT):
                        b = d_open()
                        accumulate(b[:, :], lambda k: src[:, k, t * P:(t + 1) * P], lambda k: w[:, k, :]).then_inc(d_full, 1)
                    used_by_d()

            pe.wait_ge(a_empty, na[0])
            token_rows(oT)
            pe.wait_ge(act_conv_ok, KT)
            token_rows(yT)

            def late_rows(chunks):
                for n in range(chunks + 1):
                    if n < chunks:
                        ada_chunk()
                    if n >= 1:
                        b = d_open()
                        late = late_done[0]
                        pe.wait_ge(a_empty, na[0] - (1 if n < chunks else 0))
                        pe.matmul(b[:, :], tile_sum_all[:, :], late_part[:, late % 2, :], start=True, stop=True).then_inc(d_full, 1)
                        late_done[0] += 1

            late_done = [0]
            mark["late"] = nd[0]
            late_rows(6)
            pe.wait_ge(m_ok, 4)
            transposed(m)
            pe.wait_ge(a_empty, na[0])
            token_rows(mT)
            mark["late2"] = nd[0]
            late_rows(2)
            pe.wait_ge(h2_ok, LAT_TT)
            transposed(h2)
            pe.wait_ge(a_empty, na[0])
            b = d_open()
            for t in range(LAT_TT):
                ins = accumulate(b[:, t * E:(t + 1) * E], lambda k: h2T[:, k, t * P:(t + 1) * P], lambda k: wr[:, k, :])
            ins.then_inc(d_full, 1)
            pe.wait_ge(sel_ok, 1)
            b = d_open()
            pe.matmul(b[:, 0:E], before[:, :], sel[:, 0, :], start=True, stop=True)
            pe.matmul(b[:, E:2 * E], ones[:, :], sel[:, 0, :], start=True, stop=False)
            pe.matmul(b[:, E:2 * E], before[:, :], sel[:, 1, :], start=False, stop=True)
            pe.matmul(b[:, 2 * E:3 * E], ones[:, :], sel[:, 0, :], start=True, stop=False)
            pe.matmul(b[:, 2 * E:3 * E], ones[:, :], sel[:, 1, :], start=False, stop=True).then_inc(d_full, 1)
            pe.wait_ge(rank_ok, 1)
            b = d_open()
            for t in range(LAT_TT):
                pe.transpose(b[0:E, t * P:(t + 1) * P], rank[:, t, :], ident[:, :])
                ins = pe.transpose(b[0:E, (LAT_TT + t) * P:(LAT_TT + t + 1) * P], prob[:, t, :], ident[:, :])
            ins.then_inc(d_full, 1)
            b = d_open()
            pe.transpose(b[0:E, 0:P], ends[:, 0, :], ident[:, :])
            pe.transpose(b[0:E, P:2 * P], ends[:, 1, :], ident[:, :])
            pe.transpose(b[0:E, 2 * P:3 * P], ends[:, 2, :], ident[:, :]).then_inc(d_full, 1)
            pe.wait_ge(one_item_ok, 1)
            b = d_open()
            for t in range(LAT_TT):
                pe.matmul(b[:, t * ITEM_COLS:(t + 1) * ITEM_COLS], rankT[:, t, :], one_item[:, :], start=True, stop=True)
                pe.matmul(b[:, (LAT_TT + t) * ITEM_COLS:(LAT_TT + t + 1) * ITEM_COLS], probT[:, t, :], one_item[:, :], start=True, stop=True)
            for n in range(2):
                ins = pe.matmul(b[0:1, (2 * LAT_TT + n) * ITEM_COLS:(2 * LAT_TT + n + 1) * ITEM_COLS], ecol[:, 2 + n:3 + n],
                                one_item[:, :], start=True, stop=True)
            ins.then_inc(d_full, 1)
            def gather(i):
                pe.wait_ge(pick_ok, i + 1)
                for k in range(KT):
                    half, kk = divmod(k, KT // 2)
                    for t in range(LAT_TT):
                        ins = pe.matmul(bank[6 + half][:, kk * SLOTS:(kk + 1) * SLOTS], h2[:, t, k * P:(k + 1) * P], pick[:, t, :],
                                        start=(t == 0), stop=(t == LAT_TT - 1))
                    if kk == KT // 2 - 1:
                        ins.then_inc(xs_full, 1)

            pe.wait_ge(d_empty, nd[0])
            gather(0)
            pe.wait_ge(late_in, 48)
            for t in range(LAT_TT):
                for n in range(2):
                    pe.matmul(bank[2 * t + n][:, :], probT[:, t, :], b2_rows[:, n * NF:(n + 1) * NF], start=True, stop=False,
                              skip_group_check=True)

            def product(i, n, blocks, dst, tokens_of):
                for m in range(UPP):
                    w = unit[n * UPP + m]
                    pe.wait_ge(unit_landed[n * UPP + m], i * 16 + 16)
                    for kk in range(UK):
                        k = m * UK + kk
                        for blk in blocks:
                            for half in range(2):
                                ins = pe.matmul(dst[blk][half * HALF_P:(half + 1) * HALF_P, :], tokens_of(blk, k),
                                                w[:, kk, half * NF:(half + 1) * NF],
                                                start=(k == 0), stop=(k == KT - 1), skip_group_check=True)
                    ins.then_inc(unit_used, 1)

            def scatter_block(blk, last=False):
                for t in range(LAT_TT):
                    for half in range(2):
                        rows = slice(half * HALF_P, (half + 1) * HALF_P)
                        ins = pe.matmul(bank[2 * t + half][:, :], scatter[rows, t, blk, :], y[rows, blk, :], start=False, stop=last,
                                        skip_group_check=True)
                return ins

            def transpose_hid(i, blk):
                pe.wait_ge(hid_out[blk], i * 2 + 2)
                dst = bank[6:8] if blk == B else bank[4:6]
                for part in range(2):
                    for g in range(JH):
                        pair, jj = divmod(g, 2)
                        cols = hid[:, blk, pair, jj * 2 * P:(jj + 1) * 2 * P].rearrange("s (m two) -> s two m", two=2)[:, part, :]
                        ins = pe.transpose(dst[part][:, g * P:(g + 1) * P], cols, ident[:, :])
                    ins.then_inc(ht_full[blk], 1)

            def item_pe(i, blocks):
                wide = B in blocks
                pe.wait_ge(xs_out, i * 2 + 2)
                if wide:
                    pe.wait_ge(sc_out, i + 1)
                    pe.wait_ge(y_out[A], i + 1)
                for n in range(PAIRS):
                    product(i, n, blocks, {A: bank[4 + n], B: bank[6 + n]},
                            lambda blk, k: xs[:, k, blk * HALF_P:(blk + 1) * HALF_P])
                if wide:
                    transpose_hid(i, B)
                    transpose_hid(i, A)
                    pe.wait_ge(ht_out[B], i * 2 + 2)
                    gather(i + 1)
                else:
                    pe.sem_inc(ht_full[B], 2)
                    pe.wait_ge(sc_out, i + 1)
                    pe.wait_ge(y_out[A], i + 1)
                    gather(i + 1)
                    transpose_hid(i, A)
                scatter_block(A)
                pe.wait_ge(xs_out, i * 2 + 3)
                pe.wait_ge(weigh_ok, i + 1)
                for t in range(LAT_TT):
                    for blk in range(2):
                        ins = pe.transpose(bank[6][:, (2 * t + blk) * P:(2 * t + blk + 1) * P], weigh[:, t, blk, :], ident[:, :])
                ins.then_inc(sc_full, 1)
                pe.wait_ge(xs_out, i * 2 + 4)
                for blk in blocks:
                    pe.wait_ge(hs_ok[blk], i + 1)
                place = {hid_tile(slot): slot for slot in range(FF // P)}
                product(i, PAIRS, blocks, {A: bank[7], B: bank[5]}, lambda blk, k: hs[:, blk, place[k], :])
                if wide:
                    pe.wait_ge(y_out[B], i + 1)
                    pe.wait_ge(sc_out, i + 2)
                    scatter_block(B)

            items_pe = item_count(pe)
            with pe.Fori(0, items_pe) as i:
                wide = item_of(pe, i)
                with pe.If(wide == 0):
                    item_pe(i, [A])
                with pe.Else():
                    item_pe(i, [B, A])
                pe.sem_inc(items_done, 1)
            pe.wait_ge(y_out[A], items_pe + 1)
            pe.wait_ge(sc_out, items_pe + 1)
            scatter_block(A, last=True).then_inc(acc_full, 1)

        @block.sync
        def _(sp):
            def bcast(row):
                return row.partition_broadcast(P)

            row0 = 0
            for vec in (g_mix_norm[0], g_ffn_norm[0], b_dw[0], g_conv_ln[0], b_conv_ln[0],
                        b_alpha[0].rearrange("a b -> (a b)"), c[0], c_ctx, b_ada[0]):
                rows = vec.rearrange("(r p) -> r p", p=P)
                n = min(rows.shape[0], 112 - row0)
                sp.dma_start(vec_rows[row0:row0 + n, :], rows[0:n, :]).then_inc(vec_in, 16)
                row0 += n
            sp.dma_start(ring[0][:, :, :], stream[0]).then_inc(landed[0], 16)
            sp.dma_start(tokens[:, 0:CTX_TT, :], ctx_tokens[0].rearrange("(t p) d -> p t d", p=P)).then_inc(tok_in, 16)
            sp.dma_start(tokens[:, CTX_TT:TT, :], x[0].rearrange("(t p) d -> p t d", p=P)).then_inc(tok_in, 16)
            for n in range(1, NRING):
                sp.dma_start(ring[n][:, :, :], stream[n]).then_inc(landed[n], 16)

            def small_loads():
                sp.dma_start(wdw_rows[:, :], w_dw[0]).then_inc(rows_in, 16)
                sp.dma_start(b1_rows[:, :], b_exp_in[0]).then_inc(rows_in, 16)
                sp.dma_start(a_lr_w[:, :, :], w_in[0].rearrange("(t p) n -> p t n", p=P)[:, :, c0["a_lr"]:c0["gate_conv"]]) \
                    .then_inc(bias_in, 16)
                for d in range(2):
                    sp.dma_start(wal[d * QUAD:d * QUAD + RANK, :], w_alpha[0, d]).then_inc(bias_in, 16)
                sp.dma_start(wr[:, :, :], w_router[0].rearrange("(t p) n -> p t n", p=P)).then_inc(bias_in, 16)
                sp.dma_start(gla_g[:, :], bcast(g_gla_norm)).then_inc(bias_in, 16)

            for n in range(NRING, NSTREAM):
                sp.wait_ge(*chunk_used[n - NRING])
                sp.dma_start(ring[n % NRING][:, :, :], stream[n]).then_inc(landed[n % NRING], 16)
                if n == NRING:
                    small_loads()
                if n == n_proj + NRING - 1:
                    sp.dma_start(b_ada_b[:, :], bcast(b_ada[0:1, 2 * D:6 * D])).then_inc(b_ada_in, 16)
                if n == n_proj + NRING:
                    sp.dma_start(x1[:, :, :], x[0].rearrange("(t p) d -> p t d", p=P)).then_inc(x_again_in, 16)
                    sp.dma_start(b2_rows[:, :], b_exp_out[0]).then_inc(late_in, 16)
                    sp.dma_start(g_ffn_b[:, :], bcast(g_ffn_norm)).then_inc(late_in, 16)
                    sp.dma_start(b_router_b[:, :], bcast(b_router)).then_inc(late_in, 16)
            items = item_count(sp)
            for n in range(NSTREAM - NRING, NSTREAM):
                sp.wait_ge(*chunk_used[n])
            def item_weights(i, first):
                e = sp.value_load(item_expert[0:1, bass.ds(i, 1)], min_val=0, max_val=E - 1)
                w1 = w_exp_in[0][bass.ds(e, 1)].rearrange("a (t p) n -> (a p) t n", p=P)
                w2 = w_exp_out[0][bass.ds(e, 1)].rearrange("a (t p) n -> (a p) t n", p=P)
                for n in range(UPI):
                    pair, m = divmod(n, UPP)
                    src = w1[:, m * UK:(m + 1) * UK, pair * UN:(pair + 1) * UN] if pair < PAIRS else w2[:, m * UK:(m + 1) * UK, :]
                    if not first:
                        sp.wait_ge(unit_used, i * UPI + (n + 1 - UPI))
                    sp.dma_start(unit[n][:, :, :], src).then_inc(unit_landed[n], 16)

            item_weights(0, True)
            with sp.Fori(1, items) as i:
                item_weights(i, False)
            sp.dma_start(g_final_b[:, :], bcast(g_final.rearrange("(a d) -> a d", a=1))).then_inc(g_final_in, 16)
            sp.wait_ge(out_ok, LAT_TT)
            sp.dma_start(out[0].rearrange("(t p) d -> p t d", p=P), out_sb[:, :, :]).then_inc(stored, 16)
            sp.wait_ge(stored, 16)

        @block.gpsimd
        def _(pool):
            done = Tally(const_ok)

            def wait_own():
                pool.wait_ge(const_ok, done.n)

            done.sign(pool.memset(ident[:, :], 0.0))
            done.sign(pool.memset(scT[:, :, :], 0.0))
            wait_own()
            done.sign(pool.affine_select(out=ident[:, :], in_=ident[:, :], compare_op=ALU.not_equal, fill=1.0, base=0,
                                         pattern=[[-1, P]], channel_multiplier=1))
            done.sign(pool.memset(neg_half[:, :], -0.5))
            assert done.n == N_IDENT
            done.sign(pool.memset(ones[:, :], 1.0))
            done.sign(pool.memset(tile_sum[:, :], 0.0))
            done.sign(pool.memset(tile_sum_all[:, :], 0.0))
            done.sign(pool.memset(mask_f[:, :], 1.0))
            done.sign(pool.memset(mask_b[:, :], 1.0))
            done.sign(pool.memset(scan_keep[:, :], 1.0))
            for q in range(QUADS):
                wait_own()
                done.sign(pool.affine_select(out=tile_sum[:, :], in_=tile_sum[:, :], compare_op=ALU.not_equal, fill=1.0,
                                             base=-q * QUAD, pattern=[[-1, 2]], channel_multiplier=1))
                done.sign(pool.affine_select(out=tile_sum_all[:, :], in_=tile_sum_all[:, :], compare_op=ALU.not_equal, fill=1.0,
                                             base=-q * QUAD, pattern=[[0, P]], channel_multiplier=1))
            done.sign(pool.iota(slot_no[:, :], [[1, SLOTS]], base=0, channel_multiplier=0,
                                allow_small_or_imprecise_dtypes=True))
            done.sign(pool.iota(slot_twice[:, :, :, :], [[HALF_P, 2], [0, 2], [1, HALF_P]], base=0, channel_multiplier=0,
                                allow_small_or_imprecise_dtypes=True))
            wait_own()
            done.sign(pool.affine_select(out=before[:, :], in_=ones[:, :], compare_op=ALU.is_gt, fill=0.0, base=0,
                                         pattern=[[1, P]], channel_multiplier=-1))
            keep = scan_keep[:, :].rearrange("p (c t) -> p c t", t=CHUNK)
            done.sign(pool.memset(keep[:, :, 0:1], 0.0))
            for b in range(P // CHUNK):
                cols = slice(b * CHUNK, (b + 1) * CHUNK)
                for mask in (mask_f, mask_b):
                    wait_own()
                    sign = 1 if mask is mask_f else -1
                    done.sign(pool.affine_select(out=mask[:, cols], in_=mask[:, cols], compare_op=ALU.is_ge, fill=0.0,
                                                 base=sign * b * CHUNK, pattern=[[sign, CHUNK]], channel_multiplier=-sign))
                    wait_own()
                    if mask is mask_f:
                        done.sign(pool.affine_select(out=mask[:, cols], in_=mask[:, cols], compare_op=ALU.is_ge, fill=0.0,
                                                     base=-b * CHUNK, pattern=[[0, CHUNK]], channel_multiplier=1))
                    else:
                        done.sign(pool.affine_select(out=mask[:, cols], in_=mask[:, cols], compare_op=ALU.is_ge, fill=0.0,
                                                     base=(b + 1) * CHUNK - 1, pattern=[[0, CHUNK]], channel_multiplier=-1))
            done.sign(pool.memset(u[:, :, :, :], 0.0))
            assert done.n == N_CONST, done.n
            steps = Tally(pool_ok)

            def rstd_of(sums, count, n, gate, gate_n, signal):
                pool.wait_ge(gate, gate_n)
                steps.sign(pool.tensor_scalar(sums, sums, 1.0 / count, EPS, ALU.mult, ALU.add))
                pool.wait_ge(pool_ok, steps.n)
                pool.tensor_tensor(sums, sums, neg_half[:, 0:n], ALU.pow).then_inc(signal, 1)

            rstd_of(stat[:, 0:TT], D, TT, sums_ok, TT, pow_ok)
            rstd_of(stat[:, 26:26 + LAT_TT], 1, LAT_TT, ln_var_ok, 1, ln_rstd_ok)
            for n in range(LAT_TT * HEADS):
                rstd_of(stat[:, 8 + n:9 + n], DV, 1, oss_ok, n + 1, orstd_ok)
            rstd_of(stat[:, 16:16 + LAT_TT], D, LAT_TT, x1_sum, LAT_TT, x1_pow)
            pool.wait_ge(ms_free, 1)
            pool.iota(item_no[:, :], [[1, ITEM_COLS]], base=0, channel_multiplier=0,
                      allow_small_or_imprecise_dtypes=True).then_inc(const_ok, 1)
            pool.iota(ecol[:, 2:3], [[0, 1]], base=0, channel_multiplier=1,
                      allow_small_or_imprecise_dtypes=True).then_inc(const_ok, 1)
            rstd_of(stat[:, 20:20 + LAT_TT], D, LAT_TT, fin_sum, LAT_TT, fin_pow)

        @block.scalar
        def _(act):
            groups = [0]

            def a_bank():
                groups[0] += 1
                act.wait_ge(a_full, groups[0])
                return A_BANKS[(groups[0] - 1) % 4]

            act.wait_ge(dve_ok, 1)
            act.activation(sc_act[:, :], vecT[:, 48:48 + 2 * KT], ACT.Sigmoid).then_inc(sc_sig, 1)
            act.wait_ge(tok_in, 32)
            for t in range(TT):
                if t >= 1:
                    act.wait_ge(sums_ok, t)
                act.activation(sq_junk[:, :], tokens[:, t, :], ACT.Square,
                               accum_out=stat[:, t:t + 1]).then_inc(sums_ok, 1)
            def mod_copy(n):
                b = a_bank()
                act.activation(mod_part[:, n * NF:(n + 1) * NF], b[:, :], ACT.Copy).then_inc(a_empty, 1)

            mod_copy(0)
            mod_copy(1)
            for kt in range(KT):
                b = a_bank()
                act.activation(hT[:, kt, :], b[:, :], ACT.Copy).then_inc(a_empty, 1)
            raw = groups[0]
            mod_copy(2)
            mod_copy(3)
            act.wait_ge(mod_ok, 1)
            act.wait_ge(a_empty, raw)
            for kt in range(KT // 2, KT):
                for s, (lo, hi) in enumerate(((LCTX, T), (0, LCTX))):
                    ins = act.activation(hT[:, kt, lo:hi], hT[:, kt, lo:hi], ACT.Identity, bias=modT[:, kt, s:s + 1],
                                         scale=modT[:, KT + kt, s:s + 1])
                ins.then_inc(hT_ok, 1)
            b = a_bank()
            for d in range(2):
                r = slice(d * QUAD, d * QUAD + RANK)
                ins = act.activation(a_lrT[r, :], b[r, :], ACT.Copy)
            ins.then_inc(a_empty, 1)
            for h in range(HEADS):
                b = a_bank()
                act.activation(kT[:, h, :], b[:, :], ACT.Copy).then_inc(a_empty, 1)
            for h in range(HEADS):
                b = a_bank()
                act.activation(qT[:, h, :], b[:, 0:SEQ], ACT.Copy, scale=float(DK) ** -0.5).then_inc(a_empty, 1)

            def conv_input(n):
                for g in (2 * n, 2 * n + 1):
                    half, r = divmod(g, KT)
                    is_b, ct = r // 4, half * 4 + r % 4
                    b = a_bank()
                    if is_b:
                        act.activation(yT[:, ct, :], b[:, 0:SEQ], ACT.Sigmoid).then_inc(a_empty, 1)
                    else:
                        act.activation(u[:, ct, :, PAD:PAD + GRID_W], b[:, 0:SEQ].rearrange("p (r w) -> p r w", w=GRID_W),
                                       ACT.Copy).then_inc(a_empty, 1)

            def v_copies(n):
                for t in range(TT):
                    b = a_bank()
                    act.activation(v[:, t, n * NF:(n + 1) * NF], b[:, :], ACT.Copy).then_inc(a_empty, 1)

            for it in range(HD + 1):
                if it < HD:
                    act.wait_ge(z_ok, it + 1)
                    act.activation(e_t[:, :], e_t[:, :], ACT.Exp).then_inc(act_ok, 1)
                    act.wait_ge(act_ok, it + 1)
                    act.activation(e_t[:, :], e_t[:, :], ACT.Ln, bias=1.0).then_inc(ln_ok, 1)
                    conv_input(it)
                    act.wait_ge(te_ok, it + 1)
                    act.activation(la_t[:, 0:SEQ], z_t[:, 0:SEQ], ACT.Exp, scale=1.0 / TAU)
                    act.activation(e_t[:, 0:SEQ], z_t[:, 0:SEQ], ACT.Exp, scale=-1.0 / TAU)
                    act.activation(decay[:, it, :], pre_t[:, :].rearrange("p (c t) -> p c t", t=CHUNK)[:, :, CHUNK - 1],
                                   ACT.Exp, scale=1.0 / TAU)
                    act.activation(et_t[:, :], te_t[:, :], ACT.Exp, scale=1.0 / TAU).then_inc(et_ok, 1)
                if it == HD:
                    v_copies(0)
                if it >= 1:
                    b = a_bank()
                    act.activation(k_end[:, it - 1, :, :], b[:, :].rearrange("p (t k) -> p t k", k=P), ACT.Copy).then_inc(a_empty, 1)
            v_copies(1)
            act.wait_ge(kte_ok, HD)
            for dst, fn in ((sgn, ACT.Silu), (sg_conv, ACT.Sigmoid), (sg_gla, ACT.Sigmoid)):
                for n in range(2):
                    for t in range(LAT_TT):
                        b = a_bank()
                        ins = act.activation(dst[:, t, n * NF:(n + 1) * NF], b[:, :], fn)
                        ins.then_inc(a_empty, 1)
            act.wait_ge(conv_ok, KT)
            for ct in range(KT):
                act.activation(ysq[:, ct, :], yT[:, ct, :], ACT.Square).then_inc(ysq_ok, 1)
            for n in range(LAT_TT * HEADS):
                act.wait_ge(d_full, mark["before_o"] + n + 1)
                if n >= 1:
                    act.wait_ge(oss_ok, n)
                act.activation(o_junk[:, :], D_BANKS[(mark["before_o"] + n) % 4][:, 0:DV], ACT.Square,
                               accum_out=stat[:, 8 + n:9 + n]).then_inc(oss_ok, 1)
            for g in range(4):
                b = a_bank()
                act.activation(oT[:, 2 * g:2 * g + 2, :], b[:, :].rearrange("p (k t) -> p k t", k=2), ACT.Copy).then_inc(a_empty, 1)
            for ct in range(KT):
                act.wait_ge(ln_in, ct + 1)
                act.activation(yT[:, ct, :], yT[:, ct, :], ACT.Silu, scale=vecT[:, 24 + ct:25 + ct],
                               bias=vecT[:, 32 + ct:33 + ct]).then_inc(act_conv_ok, 1)

            def late_copies(chunks):
                for _ in range(chunks):
                    b = a_bank()
                    n = late_done[0]
                    if n >= 2:
                        act.wait_ge(d_full, late_summed(n - 2))
                    act.activation(late_part[:, n % 2, :], b[:, :], ACT.Copy).then_inc(a_empty, 1)
                    late_done[0] += 1

            def late_summed(n):
                return mark["late"] + n + 1 if n < 6 else mark["late2"] + n - 6 + 1

            late_done = [0]
            late_copies(6)
            for g in range(4):
                b = a_bank()
                act.activation(mT[:, 2 * g:2 * g + 2, :], b[:, :].rearrange("p (k t) -> p k t", k=2), ACT.Copy).then_inc(a_empty, 1)
            late_copies(2)
            for t in range(LAT_TT):
                act.wait_ge(x1_ok, 1)
                act.activation(h2[:, t, :], x1[:, t, :], ACT.Square, accum_out=stat[:, 16 + t:17 + t]).then_inc(x1_sum, 1)
            for g in range(4):
                b = a_bank()
                act.activation(h2T[:, 2 * g:2 * g + 2, :], b[:, :].rearrange("p (k t) -> p k t", k=2), ACT.Copy).then_inc(a_empty, 1)
            act.wait_ge(max_ok, 1)
            for t in range(LAT_TT):
                act.activation(expo[:, t, :], logits[:, t, :], ACT.Exp, bias=need[:, t, 3:4]).then_inc(exp_ok, 1)

            items = item_count(act)

            def take_xs(i):
                for half in range(2):
                    act.wait_ge(xs_full, i * 2 + (half + 1))
                    act.activation(xs[:, half * (KT // 2):(half + 1) * (KT // 2), :],
                                   bank[6 + half][:, :].rearrange("p (k c) -> p k c", c=SLOTS), ACT.Copy).then_inc(xs_out, 1)

            def item_act(i, blocks):
                wide = B in blocks
                for n in range(PAIRS):
                    act.wait_ge(unit_used, i * UPI + (n + 1) * UPP)
                    for blk in blocks:
                        act.activation(hid[:, blk, n, :], bank[(6 if blk == B else 4) + n][:, :], ACT.Copy).then_inc(hid_out[blk], 1)
                if not wide:
                    take_xs(i + 1)
                for blk in blocks:
                    act.wait_ge(glu_ok[blk], i + 1)
                    act.activation(sig[:, blk, :, :], swi[:, blk, 0, :, :], ACT.Sigmoid, scale=ALPHA).then_inc(sig_ok[blk], 1)
                if wide:
                    take_xs(i + 1)
                act.wait_ge(sc_full, i + 1)
                act.activation(scatter[:, :, :, :], bank[6][:, :].rearrange("p (t b c) -> p t b c", t=LAT_TT, b=2), ACT.Copy).then_inc(sc_out, 1)
                act.wait_ge(unit_used, i * UPI + UPI)
                if wide:
                    act.activation(y[:, B, :], bank[5][:, :], ACT.Copy).then_inc(y_out[B], 1)
                else:
                    act.sem_inc(hid_out[B], 2)
                    act.sem_inc(sig_ok[B], 1)
                    act.sem_inc(y_out[B], 1)

            take_xs(0)
            with act.Fori(0, items) as i:
                wide = item_of(act, i)
                with act.If(wide == 0):
                    item_act(i, [A])
                with act.Else():
                    item_act(i, [B, A])
                act.activation(y[:, A, :], bank[7][:, :], ACT.Copy).then_inc(y_out[A], 1)
            for t in range(LAT_TT):
                act.wait_ge(x2_ok, t + 1)
                act.activation(out_sb[:, t, :], x1[:, t, :], ACT.Square, accum_out=stat[:, 20 + t:21 + t]).then_inc(fin_sum, 1)

        @block.vector
        def _(dve):
            step = Tally(dve_ok)
            groups = [0]

            def d_bank():
                groups[0] += 1
                dve.wait_ge(d_full, groups[0])
                return D_BANKS[(groups[0] - 1) % 4]

            def own():
                dve.wait_ge(dve_ok, step.n)

            b = d_bank()
            dve.tensor_copy(vecT[:, :], b[:, 0:112]).then_inc(d_empty, 1)
            dve.wait_ge(d_empty, 1)
            step.sign(dve.memset(stat[:, :], 0.0))
            dve.wait_ge(sc_sig, 1)
            dve.wait_ge(const_ok, N_IDENT)
            dve.tensor_tensor(scT[:, :, 0:2].rearrange("p k s -> p s k"), vecT[:, 48:48 + 2 * KT].rearrange("p (s k) -> p s k", s=2),
                              sc_act[:, :].rearrange("p (s k) -> p s k", s=2), ALU.mult).then_inc(sc_ok, 1)
            dve.wait_ge(pow_ok, 1)
            for t in range(TT):
                dve.tensor_scalar(tokens[:, t, :], tokens[:, t, :], stat[:, t:t + 1], None, ALU.mult).then_inc(norm_ok, 1)
            b = d_bank()
            dve.tensor_copy(wdwT[:, :, :], b[:, 0:KT * TAPS].rearrange("p (k w) -> p k w", w=TAPS)).then_inc(d_empty, 1)
            b = d_bank()
            bias = vecT[:, 64:64 + 2 * KT].unsqueeze(2).to_broadcast([P, 2 * KT, 2])
            dve.tensor_tensor(modT[:, :, :], b[:, 0:4 * KT].rearrange("p (k s) -> p k s", s=2), bias, ALU.add).then_inc(d_empty, 1)
            dve.wait_ge(d_empty, groups[0])
            gmix = vecT[:, 0:KT].unsqueeze(2).to_broadcast([P, KT, 2])
            dve.scalar_tensor_tensor(modT[:, KT:2 * KT, :], modT[:, KT:2 * KT, :], 1.0, gmix, ALU.add, ALU.mult).then_inc(mod_ok, 1)
            dve.wait_ge(mod_ok, 1)
            dve.wait_ge(a_empty, 2 + KT)
            for kt in range(KT // 2):
                for sample, (lo, hi) in enumerate(((LCTX, T), (0, LCTX))):
                    ins = dve.tensor_scalar(hT[:, kt, lo:hi], hT[:, kt, lo:hi], modT[:, KT + kt, sample:sample + 1],
                                            modT[:, kt, sample:sample + 1], ALU.mult, ALU.add)
                ins.then_inc(hT_ok, 1)
            b = d_bank()
            dve.tensor_copy(b1T[:, :, :].rearrange("p e j -> p j e"), b[:, :].rearrange("p (j e) -> p j e", e=E)).then_inc(d_empty, 1)

            dve.wait_ge(const_ok, N_CONST)
            per_chunk = lambda t: t[:, :].rearrange("p (c t) -> p c t", t=CHUNK)
            def masked_scores(chain):
                pd, ph = divmod(chain, HEADS)
                b = d_bank()
                sc2 = b[:, 0:SEQ].rearrange("p (t c) -> p t c", c=P)
                mask = (mask_f, mask_b)[pd][:, :].unsqueeze(1).to_broadcast([P, LAT_TT, P])
                if pd == 0:
                    dve.tensor_tensor(scores[:, ph, :, :], sc2, mask, ALU.mult).then_inc(d_empty, 1)
                else:
                    dve.tensor_tensor(kte_t[:, 0:SEQ].rearrange("p (t c) -> p t c", c=P), sc2, mask, ALU.mult).then_inc(d_empty, 1)
                    dve.wait_ge(d_empty, groups[0])
                    step.sign(dve.tensor_tensor(scores[:, ph, :, :], scores[:, ph, :, :],
                                                kte_t[:, 0:SEQ].rearrange("p (t c) -> p t c", c=P), ALU.add))

            for it in range(HD):
                d, h = divmod(it, HEADS)
                if it < HD:
                    b = d_bank()
                    dve.tensor_scalar(z_t[:, :], b[:, :], vecT[:, 40 + it:41 + it], None, ALU.add).then_inc(d_empty, 1)
                    dve.wait_ge(d_empty, groups[0])
                    dve.scalar_tensor_tensor(e_t[:, :], z_t[:, :], -1.0, z_t[:, :], ALU.mult, ALU.min).then_inc(z_ok, 1)
                if it >= 1:
                    masked_scores(it - 1)
                if it < HD:
                    dve.wait_ge(ln_ok, it + 1)
                    step.sign(dve.scalar_tensor_tensor(la_t[:, :], z_t[:, :], 0.0, e_t[:, :], ALU.min, ALU.subtract))
                    own()
                    step.sign(dve.tensor_tensor_scan(pre_t[:, :], scan_keep[:, :], la_t[:, :], 0.0, ALU.mult, ALU.add))
                    own()
                    total = per_chunk(pre_t)[:, :, CHUNK - 1:CHUNK].to_broadcast([P, NCHUNK, CHUNK])
                    if d == 0:
                        dve.tensor_copy(z_t[:, 0:SEQ], pre_t[:, LCTX:T])
                        dve.tensor_tensor(per_chunk(te_t), total, per_chunk(pre_t), ALU.subtract).then_inc(te_ok, 1)
                    else:
                        step.sign(dve.tensor_tensor(te_t[:, :], pre_t[:, :], la_t[:, :], ALU.subtract))
                        own()
                        nl = LCTX // CHUNK
                        dve.tensor_tensor(z_t[:, 0:SEQ].rearrange("p (c t) -> p c t", t=CHUNK), total[:, nl:NCHUNK, :],
                                          per_chunk(te_t)[:, nl:NCHUNK, :], ALU.subtract).then_inc(te_ok, 1)
                    dve.wait_ge(et_ok, it + 1)
                    step.sign(dve.tensor_tensor(q_dec[:, it, :], qT[:, h, :], la_t[:, 0:SEQ], ALU.mult))
                    step.sign(dve.tensor_tensor(te_t[:, 0:SEQ], kT[:, h, LCTX:T], e_t[:, 0:SEQ], ALU.mult))
                    dve.tensor_tensor(kte_t[:, :], kT[:, h, :], et_t[:, :], ALU.mult).then_inc(kte_ok, 1)

            dve.wait_ge(a_empty, mark["conv_in"])
            for ct in range(KT):
                rows = lambda k: u[:, ct, :, k:k + GRID_W]
                yv = yT[:, ct, :].rearrange("p (r w) -> p r w", w=GRID_W)
                step.sign(dve.tensor_tensor(rows(PAD), rows(PAD), yv, ALU.mult))
                own()
                step.sign(dve.tensor_scalar(yv, rows(0), wdwT[:, ct, 0:1], vecT[:, 16 + ct:17 + ct], ALU.mult, ALU.add))
                for k in range(1, TAPS):
                    own()
                    ins = dve.scalar_tensor_tensor(yv, rows(k), wdwT[:, ct, k:k + 1], yv, ALU.mult, ALU.add)
                    if k < TAPS - 1:
                        step.sign(ins)
                    else:
                        ins.then_inc(conv_ok, 1)
            masked_scores(HD - 1)
            mean, var = stat[:, 24:24 + LAT_TT], stat[:, 26:26 + LAT_TT]
            b = d_bank()
            step.sign(dve.tensor_scalar(mean, b[:, 0:LAT_TT], 1.0 / D, None, ALU.mult))
            own()
            step.sign(dve.tensor_tensor(stat[:, 28:28 + LAT_TT], mean, mean, ALU.mult))
            own()
            dve.scalar_tensor_tensor(var, b[:, LAT_TT:2 * LAT_TT], 1.0 / D, stat[:, 28:28 + LAT_TT], ALU.mult,
                                     ALU.subtract).then_inc(d_empty, 1)
            dve.wait_ge(d_empty, groups[0])
            step.sign(dve.tensor_scalar(var, var, 0.0, None, ALU.max))
            own()
            dve.sem_inc(ln_var_ok, 1)

            first_store = LCTX // CHUNK
            for s in range(NCHUNK - 1):
                src, dst = max(s - first_store, 0), max(s + 1 - first_store, 0)
                for hd in range(HD):
                    b = d_bank()
                    if s == 0:
                        dve.tensor_copy(state[:, 0, hd, :], b[:, 0:DV]).then_inc(d_empty, 1)
                    else:
                        dve.wait_ge(d_empty, groups[0] - HD)
                        dve.scalar_tensor_tensor(state[:, dst, hd, :], state[:, src, hd, :],
                                                 decay[:, hd, CHUNK_OF(hd // HEADS, s):CHUNK_OF(hd // HEADS, s) + 1],
                                                 b[:, 0:DV], ALU.mult, ALU.add).then_inc(d_empty, 1)
            dve.wait_ge(ln_rstd_ok, 1)
            for n, cols in enumerate((mean, var)):
                for t in range(LAT_TT):
                    ins = dve.tensor_scalar(ln_wide[:, n, t, :], ones[:, :], cols[:, t:t + 1], None, ALU.mult)
            ins.then_inc(ln_cols_ok, 1)
            dve.wait_ge(a_empty, mark["g"])
            for t in range(LAT_TT):
                for h in range(HEADS):
                    step.sign(dve.tensor_tensor(sgn[:, t, h * DV:(h + 1) * DV], sgn[:, t, h * DV:(h + 1) * DV], gla_g[:, :], ALU.mult))
            own()
            assert groups[0] == mark["before_o"], groups
            for n in range(LAT_TT * HEADS):
                t, h = divmod(n, HEADS)
                b = d_bank()
                dve.wait_ge(orstd_ok, n + 1)
                dve.scalar_tensor_tensor(o_sb[:, t, h * DV:(h + 1) * DV], b[:, 0:DV], stat[:, 8 + n:9 + n],
                                         sgn[:, t, h * DV:(h + 1) * DV], ALU.mult, ALU.mult).then_inc(d_empty, 1)
            b = d_bank()
            for ct in range(KT):
                step.sign(dve.tensor_tensor(yT[:, ct, :], yT[:, ct, :], b[:, 0:SEQ], ALU.subtract))
            own()
            for ct in range(KT):
                dve.tensor_tensor(yT[:, ct, :], yT[:, ct, :], b[:, SEQ:2 * SEQ], ALU.mult).then_inc(ln_in, 1)
            dve.wait_ge(ln_in, KT)
            dve.sem_inc(d_empty, 1)
            for n in range(2):
                for t in range(LAT_TT):
                    b = d_bank()
                    cs = slice(n * NF, (n + 1) * NF)
                    dve.tensor_tensor(m[:, t, cs], b[:, :], sg_gla[:, t, cs], ALU.mult).then_inc(d_empty, 1)
            for n in range(2):
                for t in range(LAT_TT):
                    b = d_bank()
                    cs = slice(n * NF, (n + 1) * NF)
                    dve.tensor_tensor(gated[:, :], b[:, :], sg_conv[:, t, cs], ALU.mult).then_inc(d_empty, 1)
                    dve.wait_ge(d_empty, groups[0])
                    step.sign(dve.tensor_tensor(m[:, t, cs], m[:, t, cs], gated[:, :], ALU.add))
                    own()
                    dve.sem_inc(m_ok, 1)

            def late_add(dst, part):
                for n in range(2):
                    b = d_bank()
                    dve.tensor_tensor(dst[:, n * NF:(n + 1) * NF], b[:, :],
                                      b_ada_b[:, part * D + n * NF:part * D + (n + 1) * NF], ALU.add).then_inc(d_empty, 1)

            dve.wait_ge(b_ada_in, 16)
            for part, dst in enumerate((gt1, sh2, a2)):
                late_add(dst, part)
            dve.wait_ge(d_empty, groups[0])
            dve.wait_ge(x_again_in, 16)
            for n in range(2):
                for t in range(LAT_TT):
                    b = d_bank()
                    cs = slice(n * NF, (n + 1) * NF)
                    dve.tensor_tensor(gated[:, :], b[:, :], gt1[:, cs], ALU.mult).then_inc(d_empty, 1)
                    dve.wait_ge(d_empty, groups[0])
                    step.sign(dve.tensor_tensor(x1[:, t, cs], x1[:, t, cs], gated[:, :], ALU.add))
                    own()
            dve.sem_inc(x1_ok, 1)
            dve.sem_inc(ms_free, 1)
            late_add(gt2, 3)
            dve.wait_ge(late_in, 48)
            step.sign(dve.scalar_tensor_tensor(a2[:, :], a2[:, :], 1.0, g_ffn_b[:, :], ALU.add, ALU.mult))
            own()
            dve.wait_ge(x1_pow, 1)
            for t in range(LAT_TT):
                step.sign(dve.scalar_tensor_tensor(h2[:, t, :], x1[:, t, :], stat[:, 16 + t:17 + t], a2[:, :], ALU.mult, ALU.mult))
            own()
            for t in range(LAT_TT):
                dve.tensor_tensor(h2[:, t, :], h2[:, t, :], sh2[:, :], ALU.add).then_inc(h2_ok, 1)

            b = d_bank()
            for t in range(LAT_TT):
                ins = dve.tensor_tensor(logits[:, t, :], b[:, t * E:(t + 1) * E], b_router_b[:, :], ALU.add)
            ins.then_inc(d_empty, 1)
            dve.wait_ge(d_empty, groups[0])
            for t in range(LAT_TT):
                step.sign(dve.max(top8[:, t, :], logits[:, t, :]))
            own()
            for t in range(LAT_TT):
                step.sign(dve.tensor_scalar(need[:, t, 3:4], top8[:, t, 0:1], -1.0, None, ALU.mult))
            own()
            dve.sem_inc(max_ok, 1)
            for t in range(LAT_TT):
                kth = top8[:, t, TOPK - 1:TOPK]
                step.sign(dve.tensor_scalar(above[:, t, :], logits[:, t, :], kth, None, ALU.is_gt))
                step.sign(dve.tensor_scalar(equal[:, t, :], logits[:, t, :], kth, None, ALU.is_equal))
            own()
            for t in range(LAT_TT):
                step.sign(dve.tensor_reduce(need[:, t, 0:1], above[:, t, :], AX_X, ALU.add))
                step.sign(dve.tensor_tensor_scan(nth[:, t, :], ones[:, 0:E], equal[:, t, :], 0.0, ALU.mult, ALU.add))
            own()
            for t in range(LAT_TT):
                step.sign(dve.tensor_scalar(need[:, t, 1:2], need[:, t, 0:1], -1.0, float(TOPK), ALU.mult, ALU.add))
            own()
            for t in range(LAT_TT):
                step.sign(dve.scalar_tensor_tensor(sel[:, t, :], nth[:, t, :], need[:, t, 1:2], equal[:, t, :], ALU.is_le, ALU.mult))
            own()
            step.sign(dve.tensor_tensor(sel[:, :, :], sel[:, :, :], above[:, :, :], ALU.add))
            own()
            dve.sem_inc(sel_ok, 1)
            dve.wait_ge(exp_ok, LAT_TT)
            step.sign(dve.tensor_tensor(expo[:, :, :], expo[:, :, :], sel[:, :, :], ALU.mult))
            own()
            step.sign(dve.tensor_reduce(need[:, :, 2], expo[:, :, :], AX_X, ALU.add))
            own()
            step.sign(dve.reciprocal(need[:, :, 2], need[:, :, 2]))
            own()
            for t in range(LAT_TT):
                step.sign(dve.tensor_scalar(prob[:, t, :], expo[:, t, :], need[:, t, 2:3], None, ALU.mult))
            b = d_bank()
            step.sign(dve.tensor_copy(rank[:, :, :], b[:, 0:LAT_TT * E].rearrange("p (t e) -> p t e", e=E)))
            counts = b[:, LAT_TT * E:(LAT_TT + 1) * E]
            for j in range(ITEMS_OF_ONE):
                step.sign(dve.tensor_scalar(blocks[:, j, :], counts, float(j * SLOTS), None, ALU.is_gt))
            own()
            for j in range(1, ITEMS_OF_ONE):
                step.sign(dve.tensor_tensor(blocks[:, 0, :], blocks[:, 0, :], blocks[:, j, :], ALU.add))
            own()
            step.sign(dve.tensor_tensor_scan(ends[:, 1, :], ones[:, 0:E], blocks[:, 0, :], 0.0, ALU.mult, ALU.add))
            own()
            step.sign(dve.tensor_tensor(ends[:, 0, :], ends[:, 1, :], blocks[:, 0, :], ALU.subtract))
            own()
            dve.scalar_tensor_tensor(ends[:, 2, :], ends[:, 0, :], float(SLOTS), counts, ALU.mult, ALU.add).then_inc(d_empty, 1)
            step.sign(dve.tensor_scalar(above[:, :, :], sel[:, :, :], -BIG, BIG, ALU.mult, ALU.add))
            own()
            step.sign(dve.tensor_tensor(rank[:, :, :], rank[:, :, :], above[:, :, :], ALU.add))
            own()
            first_item = ends[:, 0, :].unsqueeze(1).to_broadcast([P, LAT_TT, E])
            step.sign(dve.scalar_tensor_tensor(rank[:, :, :], first_item, float(SLOTS), rank[:, :, :], ALU.mult, ALU.add))
            own()
            dve.wait_ge(d_empty, groups[0])
            dve.sem_inc(rank_ok, 1)
            b = d_bank()
            step.sign(dve.tensor_copy(rankT[:, :, :], b[0:E, 0:LAT_TT * P].rearrange("p (t c) -> p t c", c=P)))
            dve.tensor_copy(probT[:, :, :], b[0:E, LAT_TT * P:2 * LAT_TT * P].rearrange("p (t c) -> p t c", c=P)).then_inc(d_empty, 1)
            b = d_bank()
            dve.tensor_copy(ecol[:, 0:1], b[0:E, 0:1])
            dve.wait_ge(const_ok, N_CONST + 2)
            dve.tensor_copy(ecol[:, 3:4], b[0:E, 2 * P:2 * P + 1])
            dve.tensor_copy(ecol[:, 1:2], b[0:E, P:P + 1]).then_inc(d_empty, 1)
            dve.wait_ge(d_empty, groups[0])
            step.sign(dve.tensor_scalar(one_item[:, :], item_no[0:E, :], ecol[:, 1:2], None, ALU.is_lt))
            own()
            step.sign(dve.scalar_tensor_tensor(one_item[:, :], item_no[0:E, :], ecol[:, 0:1], one_item[:, :], ALU.is_ge, ALU.mult))
            own()
            dve.sem_inc(one_item_ok, 1)
            b = d_bank()
            for t in range(LAT_TT):
                step.sign(dve.scalar_tensor_tensor(slot_tok[:, t, :], item_no[:, :], -float(SLOTS), b[:, t * ITEM_COLS:(t + 1) * ITEM_COLS],
                                                   ALU.mult, ALU.add))
            step.sign(dve.scalar_tensor_tensor(spill[:, :], item_no[0:1, :], -float(SLOTS),
                                               b[0:1, (2 * LAT_TT + 1) * ITEM_COLS:(2 * LAT_TT + 2) * ITEM_COLS], ALU.mult, ALU.add))
            own()
            step.sign(dve.tensor_scalar(item_wide[:, :], spill[:, :], float(HALF_P), None, ALU.is_gt))
            step.sign(dve.tensor_copy(item_expert[0:1, ITEM_COLS:ITEM_COLS + 1], ends[0:1, 1, E - 1:E]))
            dve.tensor_copy(prob_tok[:, :, :], b[:, LAT_TT * ITEM_COLS:2 * LAT_TT * ITEM_COLS].rearrange("p (t i) -> p t i", i=ITEM_COLS))
            dve.tensor_copy(item_expert[0:1, 0:ITEM_COLS], b[0:1, 2 * LAT_TT * ITEM_COLS:(2 * LAT_TT + 1) * ITEM_COLS]).then_inc(d_empty, 1)
            dve.wait_ge(d_empty, groups[0])
            own()
            dve.sem_inc(items_ok, 1)

            items = item_count(dve)

            def make_pick(i):
                for t in range(LAT_TT):
                    ins = dve.tensor_scalar(pick[:, t, :], slot_no[:, :], slot_tok[:, t, bass.ds(i, 1)], None, ALU.is_equal)
                ins.then_inc(pick_ok, 1)

            STEPS = 2

            def swiglu(i, blk, before):
                own_steps = i * (2 * STEPS) + before
                banks = bank[6:8] if blk == B else bank[4:6]
                for part in range(2):
                    dve.wait_ge(ht_full[blk], i * 2 + (part + 1))
                    b1 = b1T[:, bass.ds(e, 1), part * (FF // P):(part + 1) * (FF // P)].rearrange("p a j -> p (a j)") \
                        .unsqueeze(2).to_broadcast([P, FF // P, HALF_P])
                    dve.tensor_tensor(swi[:, blk, part, :, :], banks[part][:, :].rearrange("p (j c) -> p j c", c=HALF_P), b1,
                                      ALU.add).then_inc(ht_out[blk], 1)
                glu, lin = swi[:, blk, 0, :, :], swi[:, blk, 1, :, :]
                dve.wait_ge(ht_out[blk], i * 2 + 2)
                dve.tensor_scalar(glu, glu, LIMIT, None, ALU.min).then_inc(glu_ok[blk], 1)
                dve.tensor_scalar(lin, lin, LIMIT, -LIMIT, ALU.min, ALU.max).then_inc(swi_step, 1)
                dve.wait_ge(swi_step, own_steps + 1)
                dve.wait_ge(glu_ok[blk], i + 1)
                dve.scalar_tensor_tensor(lin, lin, 1.0, glu, ALU.add, ALU.mult).then_inc(swi_step, 1)
                dve.wait_ge(swi_step, own_steps + 2)
                dve.wait_ge(sig_ok[blk], i + 1)
                dve.tensor_tensor(hs[:, blk, :, :], lin, sig[:, blk, :, :], ALU.mult).then_inc(hs_ok[blk], 1)

            step.sign(dve.memset(y[:, A, :], 0.0))
            step.sign(dve.memset(scatter[:, :, :, :], 0.0))
            own()
            dve.sem_inc(y_out[A], 1)
            dve.sem_inc(sc_out, 1)
            make_pick(0)
            with dve.Fori(0, items) as i:
                e = dve.value_load(item_expert[0:1, bass.ds(i, 1)], min_val=0, max_val=E - 1)
                wide = item_of(dve, i)
                dve.wait_ge(xs_full, i * 2 + 2)
                make_pick(i + 1)
                dve.wait_ge(unit_used, i * UPI + 1)
                for t in range(LAT_TT):
                    ins = dve.tensor_scalar(weigh[:, t, :, :].rearrange("p b (d c) -> p b d c", d=2), slot_twice[:, :, :, :],
                                            slot_tok[:, t, bass.ds(i, 1)], prob_tok[:, t, bass.ds(i, 1)], ALU.is_equal, ALU.mult)
                ins.then_inc(weigh_ok, 1)
                with dve.If(wide == 0):
                    dve.sem_inc(swi_step, STEPS)
                    for done in (glu_ok[B], hs_ok[B]):
                        dve.sem_inc(done, 1)
                    dve.sem_inc(ht_out[B], 2)
                with dve.Else():
                    swiglu(i, B, 0)
                swiglu(i, A, STEPS)
            dve.wait_ge(acc_full, 1)
            for t in range(LAT_TT):
                for n in range(2):
                    cs = slice(n * NF, (n + 1) * NF)
                    step.sign(dve.tensor_tensor(sums[:, t, cs], bank[2 * t + n][:, :], gt2[:, cs], ALU.mult))
            own()
            for t in range(LAT_TT):
                step.sign(dve.tensor_tensor(x1[:, t, :], x1[:, t, :], sums[:, t, :], ALU.add))
                own()
                dve.sem_inc(x2_ok, 1)
            dve.wait_ge(g_final_in, 16)
            dve.wait_ge(fin_pow, 1)
            for t in range(LAT_TT):
                dve.scalar_tensor_tensor(out_sb[:, t, :], x1[:, t, :], stat[:, 20 + t:21 + t], g_final_b[:, :], ALU.mult, ALU.mult).then_inc(out_ok, 1)



_INS = ["x", "c", "ctx", "c_ctx", "w_ada", "b_ada", "g_mix_norm", "w_in", "w_dw", "b_dw", "g_conv_ln", "b_conv_ln",
        "w_conv_out", "w_alpha", "b_alpha", "g_gla_norm", "w_gla_out", "w_out", "g_ffn_norm", "w_router", "b_router",
        "w_exp_in", "b_exp_in", "w_exp_out", "b_exp_out", "g_final"]


def kernel(**inputs):
    import numpy as np
    import concourse.bacc as bacc
    from concourse.bass_utils import run_bass_kernel_spmd

    nc = bacc.Bacc("TRN2", target_bir_lowering=False, num_devices=1)
    arrays, args = {}, []
    for name in _INS:
        a = np.ascontiguousarray(inputs[name])
        arrays[f"in_{name}"] = a
        args.append(nc.dram_tensor(f"in_{name}", a.shape, mybir.dt.from_np(a.dtype), kind="ExternalInput").ap())
    out = nc.dram_tensor("out_0", inputs["x"].shape, F32, kind="ExternalOutput").ap()
    build(nc, *args, out)
    r = run_bass_kernel_spmd(nc, [arrays], core_ids=[0])
    return r.results[0]["out_0"]
```

```python
from contextlib import ExitStack

import concourse.bass as bass
from concourse import mybir

F32 = mybir.dt.float32
F32R = mybir.dt.float32r
I32 = mybir.dt.int32
ALU = mybir.AluOpType
ACT = mybir.ActivationFunctionType
AX_X = mybir.AxisListType.X

P = 128
EPS = 1e-6
TAU = 16.0
ALPHA = 1.702
LIMIT = 7.0
BIG = 65536.0


class Tally:

    def __init__(self, sem):
        self.sem, self.n = sem, 0

    def sign(self, ins):
        ins.then_inc(self.sem, 1)
        self.n += 1


def build(nc, x, c, ctx_tokens, c_ctx, w_ada, b_ada, g_mix_norm, w_in, w_dw, b_dw, g_conv_ln, b_conv_ln,
          w_conv_out, w_alpha, b_alpha, g_gla_norm, w_gla_out, w_out, g_ffn_norm, w_router, b_router,
          w_exp_in, b_exp_in, w_exp_out, b_exp_out, g_final, out, debug=None):
    _, SEQ, D = x.shape
    LCTX = ctx_tokens.shape[1]
    T = LCTX + SEQ
    KT = D // P
    CTX_TT, LAT_TT = LCTX // P, SEQ // P
    TT = CTX_TT + LAT_TT
    TAPS = w_dw.shape[1]
    PAD = TAPS // 2
    GRID_W = 64
    ROWS = SEQ // GRID_W
    RANK, KD = w_alpha.shape[2], w_alpha.shape[3]
    DK = P
    HEADS = KD // DK
    DV = g_gla_norm.shape[1]
    CHUNK = 64
    NCHUNK = T // CHUNK
    E, FF = w_exp_in.shape[1], w_exp_out.shape[2]
    TOPK = 4
    HALF_P = P // 2
    SLOTS = 2 * HALF_P
    NF = 512
    ITEMS_MAX = (SEQ * TOPK + E * (SLOTS - 1)) // SLOTS
    ITEMS_MIN = SEQ * TOPK // SLOTS
    ITEMS_OF_ONE = (SEQ + SLOTS - 1) // SLOTS
    ITEM_COLS = ITEMS_MAX + 1
    QUAD = 32
    QUADS = P // QUAD
    HD = 2 * HEADS
    c0 = dict(conv_a=0, conv_b=D, q=2 * D, k=2 * D + KD, v=2 * D + 2 * KD)
    c0["g"] = c0["v"] + HEADS * DV
    c0["a_lr"] = c0["g"] + HEADS * DV
    c0["gate_conv"] = c0["a_lr"] + 2 * RANK
    c0["gate_gla"] = c0["gate_conv"] + D

    def chunked(w, col):
        return w.rearrange("(t p) n -> p t n", p=P)[:, :, col:col + NF]

    stream = []
    ada = lambda part: [chunked(w_ada[0], part * D + n * NF) for n in range(D // NF)]
    proj = lambda name, n: chunked(w_in[0], c0[name] + n * NF)
    stream += ada(0) + ada(1)
    stream += [proj("k", 0), proj("q", 0), proj("conv_a", 0), proj("conv_b", 0), proj("conv_a", 1), proj("conv_b", 1)]
    stream += [proj(name, n) for name in ("v", "g", "gate_conv", "gate_gla") for n in range(2)]
    n_proj = len(stream)
    dense = lambda w: [chunked(w[0], n * NF) for n in range(D // NF)]
    dense = lambda w: [chunked(w[0], n * NF) for n in range(D // NF)]
    late = ada(2) + ada(3) + ada(4) + ada(5)
    LATE_AFTER = dict(gla_out=(1, 1), conv_out=(1, 2), out=(1, 2))
    for name, w in (("gla_out", w_gla_out), ("conv_out", w_conv_out), ("out", w_out)):
        for n in range(D // NF):
            stream.append(dense(w)[n])
            for _ in range(LATE_AFTER[name][n]):
                stream.append(late.pop(0))
    NSTREAM = len(stream)
    NRING = 3
    MOD_DVE = 5
    UK, UN = 2, 2 * NF
    UPP = KT // UK
    PAIRS = 2 * FF // UN
    UPI = UPP * (PAIRS + 1)
    JH = FF // P // 2

    base = (nc.sbuf_base + 511) // 512 * 512
    KB = 1024

    def at(name, kb, shape, dt=F32):
        return nc.alloc_sbuf_tensor_at(name, list(shape), dt, offset=base + int(kb * KB))

    class Bump:

        def __init__(self, kb, end):
            self.kb, self.end = kb, end

        def __call__(self, name, shape, dt=F32):
            size = 4
            for s in shape[1:]:
                size *= s
            t = at(name, self.kb, shape, dt)
            self.kb += (size + 63) // 64 * 64 / KB
            assert self.kb <= self.end, name
            return t

    ring = [at(f"weights{s}", 16 * s, [P, KT, NF]) for s in range(NRING)]
    small = Bump(48, 68)
    ident = small("ident", [P, P])
    ones = small("ones", [P, P])
    slot_no = small("slot_no", [P, SLOTS])
    slot_twice = small("slot_twice", [P, 2, 2, HALF_P])
    mask_f = small("mask_f", [P, P])
    mask_b = small("mask_b", [P, P])
    before = small("before", [P, P])
    scan_keep = small("scan_keep", [P, T])
    vecT = small("vecT", [P, 112])
    wdwT = small("wdwT", [P, KT, TAPS])
    decay = small("decay", [P, HD, NCHUNK])
    stat = small("stat", [P, 48])
    quad_fold = small("quad_fold", [P, QUAD])
    a_lr_w = small("a_lr_w", [P, KT, 2 * RANK])
    wal = small("wal", [QUAD + RANK, KD])
    wr = small("wr", [P, KT, E])
    sc_act = small("sc_act", [P, 2 * KT])
    scT = small("scT", [P, KT, QUAD])
    tile_sum = small("tile_sum", [P, 2])
    tile_sum_all = small("tile_sum_all", [P, P])
    modT = small("modT", [P, 2 * KT, 2])
    b1T = small("b1T", [P, E, 2 * FF // P])
    slot_tok = small("slot_tok", [P, LAT_TT, ITEM_COLS])
    prob_tok = small("prob_tok", [P, LAT_TT, ITEM_COLS])
    item_expert = small("item_expert", [1, ITEM_COLS + 1], I32)
    item_wide = small("item_wide", [1, ITEM_COLS], I32)
    neg_half = small("neg_half", [P, 8])
    x1 = at("x1", 68, [P, LAT_TT, D])
    gt2 = at("gt2", 76, [P, D])
    h2 = at("h2", 80, [P, LAT_TT, D])
    b2_rows = at("b2_rows", 148, [E, D])
    tokens = at("tokens", 68, [P, TT, D])
    sq_junk = at("sq_junk", 116, [P, D])
    o_junk = at("o_junk", 188, [P, DV])
    mod_part = at("mod_part", 84, [P, 2 * D])
    b1_rows = at("b1_rows", 92, [E, 2 * FF])
    vec_rows = at("vec_rows", 100, [112, P])
    wdw_rows = at("wdw_rows", 132, [TAPS, D])
    hT = at("hT", 100, [P, KT, T])
    a_lrT = at("a_lrT", 92, [QUAD + RANK, T])
    k_end = at("k_end", 116, [P, HD, TT, P])
    q_dec = at("q_dec", 132, [P, HD, SEQ])
    scores = at("scores", 140, [P, HEADS, LAT_TT, P])
    yT = at("yT", 144, [P, KT, SEQ])
    u = at("u", 152, [P, KT, ROWS, GRID_W + 2 * PAD])
    kT = at("kT", 164, [P, HEADS, T])
    qT = at("qT", 172, [P, HEADS, SEQ])
    z_t = at("z_t", 176, [P, T])
    e_t = at("e_t", 178, [P, T])
    la_t = at("la_t", 180, [P, T])
    pre_t = at("pre_t", 182, [P, T])
    te_t = at("te_t", 184, [P, T])
    et_t = at("et_t", 186, [P, T])
    kte_t = at("kte_t", 188, [P, T])
    v = at("v", 190, [P, TT, HEADS * DV])
    state = at("state", 68, [P, 4, HD, DV])
    sgn = at("sgn", 164, [P, LAT_TT, HEADS * DV])
    sg_conv = at("sg_conv", 172, [P, LAT_TT, D])
    sg_gla = at("sg_gla", 180, [P, LAT_TT, D])
    gla_g = at("gla_g", 206, [P, DV])
    o_sb = at("o_sb", 116, [P, LAT_TT, HEADS * DV])
    oT = at("oT", 124, [P, KT, SEQ])
    b_ada_b = at("b_ada_b", 100, [P, 4 * D])
    late_part = at("late_part", 92, [P, 2, NF])
    gt1 = at("gt1", 96, [P, D])
    sh2 = at("sh2", 202, [P, D])
    a2 = at("a2", 198, [P, D])
    ysq = at("ysq", 152, [P, KT, SEQ])
    ln_wide = at("ln_wide", 160, [P, 2, LAT_TT, P])
    m = at("m", 152, [P, LAT_TT, D])
    gated = at("gated", 164, [P, NF])
    mT = at("mT", 124, [P, KT, SEQ])
    g_ffn_b = at("g_ffn_b", 190, [P, D])
    b_router_b = at("b_router_b", 194, [P, E])
    sq_x1 = at("sq_x1", 180, [P, LAT_TT, D])
    h2T = at("h2T", 172, [P, KT, SEQ])
    rt = Bump(152, 160)
    logits = rt("logits", [P, LAT_TT, E])
    logit_part = rt("logit_part", [P, SEQ])
    top8 = rt("top8", [P, LAT_TT, 8])
    above = rt("above", [P, LAT_TT, E])
    equal = rt("equal", [P, LAT_TT, E])
    nth = rt("nth", [P, LAT_TT, E])
    need = rt("need", [P, LAT_TT, 4])
    sel = rt("sel", [P, LAT_TT, E])
    expo = rt("expo", [P, LAT_TT, E])
    prob = rt("prob", [P, LAT_TT, E])
    rank = rt("rank", [P, LAT_TT, E])
    blocks = rt("blocks", [P, ITEMS_OF_ONE, E])
    ends = rt("ends", [P, 3, E])
    ecol = rt("ecol", [E, 4])
    one_item = rt("one_item", [E, ITEM_COLS])
    spill = rt("spill", [1, ITEM_COLS])
    item_no = rt("item_no", [P, ITEM_COLS])
    rankT = rt("rankT", [E, LAT_TT, P])
    probT = rt("probT", [E, LAT_TT, P])
    unit = [at(f"unit{n}", 8 * n if n < 6 else 100 + 8 * (n - 6), [P, UK, UN]) for n in range(UPI)]
    hid = at("hid", 164, [P, 2, PAIRS, NF])
    xs = at("xs", 172, [P, KT, SLOTS])
    hs = at("hs", 176, [P, 2, 2 * JH, HALF_P])
    y_hi = at("y_hi", 180, [P, 2, NF], F32R)
    y_lo = at("y_lo", 88, [P, 2, NF], F32R)
    scatter = at("scatter", 184, [P, 2, LAT_TT, P], F32R)
    weighT = at("weighT", 160, [P, 2, LAT_TT, P])
    slot_prob = at("slot_prob", 162, [P, 2])
    pick = at("pick", 186, [P, LAT_TT, SLOTS])
    weigh = at("weigh", 187, [P, LAT_TT, 2, P])
    swi = at("swi", 189, [P, 2, 2, 2 * JH, HALF_P])
    sig = at("sig", 197, [P, 2, 2 * JH, HALF_P])
    g_final_b = at("g_final_b", 201, [P, D])
    sums = at("sums", 148, [P, LAT_TT, D])
    out_sb = at("out_sb", 100, [P, LAT_TT, D])
    fin_junk = at("fin_junk", 108, [P, LAT_TT, D])

    stack = ExitStack()
    with stack:
        def sem(name):
            return stack.enter_context(nc.semaphore(name))

        bank = [stack.enter_context(nc.psum_tensor(f"bank{i}", [P, NF], F32)) for i in range(8)]
        A_BANKS, D_BANKS = bank[0:4], bank[4:8]

        landed = [sem(f"weights_landed{s}") for s in range(NRING)]
        vec_in, tok_in, bias_in, rows_in = sem("vec_in"), sem("tok_in"), sem("bias_in"), sem("rows_in")
        b_ada_in, x_again_in, late_in = sem("b_ada_in"), sem("x_again_in"), sem("late_in")
        const_ok = sem("const_ok")
        a_full, a_empty = sem("a_bank_full"), sem("a_bank_empty")
        d_full, d_empty = sem("d_bank_full"), sem("d_bank_empty")
        dve_ok, act_ok, pool_ok = sem("dve_step"), sem("act_step"), sem("pool_step")
        sums_ok, pow_ok = sem("squares_summed"), sem("rstd_ok")
        sc_sig, sc_ok, norm_ok, mod_ok = sem("c_sigmoid"), sem("silu_c_ok"), sem("tokens_normed"), sem("mod_ok")
        z_ok, ln_ok, te_ok, et_ok, kte_ok = sem("z_ok"), sem("ln_ok"), sem("te_ok"), sem("et_ok"), sem("kte_ok")
        conv_ok, ysq_ok, act_conv_ok = sem("conv_ok"), sem("ysq_ok"), sem("act_conv_ok")
        oss_ok, orstd_ok, ln_cols_ok, hT_ok = sem("o_squares"), sem("o_rstd"), sem("ln_columns"), sem("hT_ok")
        hT_hi_ok, sq_ok = sem("hT_upper_ok"), sem("x1_squares")
        ln_var_ok, ln_rstd_ok, ln_in = sem("ln_var"), sem("ln_rstd"), sem("ln_in")
        x1_ok, x1_sum, x1_pow, h2_ok, exp_ok = sem("x1_ok"), sem("x1_sum"), sem("x1_rstd"), sem("h2_ok"), sem("exp_ok")
        m_ok, ms_free, max_ok, sel_ok, rank_ok = sem("m_ok"), sem("m_unused"), sem("max_ok"), sem("sel_ok"), sem("rank_ok")
        one_item_ok, items_ok, x2_ok, g_final_in = sem("one_item_ok"), sem("items_ok"), sem("x2_ok"), sem("g_final_in")
        def both(name):
            return [sem(name + "_a"), sem(name + "_b")]

        unit_landed = [sem(f"unit_landed{n}") for n in range(UPI)]
        unit_used, items_done = sem("unit_used"), sem("items_done")
        hid_out, ht_full, ht_out, y_out = both("hid_out"), both("hidT_full"), both("hidT_out"), both("y_out")
        glu_ok, sig_ok, hs_ok = both("glu_ok"), both("sig_ok"), both("hs_ok")
        xs_full, xs_out = sem("xs_full"), sem("xs_out")
        sc_full, sc_out = sem("scatter_full"), sem("scatter_out")
        pick_ok, weigh_ok = sem("pick_ok"), sem("weigh_ok")
        swi_step = sem("swiglu_step")
        weighT_ok, yh_ok = sem("weighT_ok"), both("y_hi_ok")
        fin_sq, scaled_ok, scaled_last_ok, out_act_ok = sem("fin_squares"), sem("scaled_ok"), sem("scaled_last_ok"), sem("out_act_ok")
        scattered, b2_in, yb_full = sem("scattered"), sem("b2_in"), sem("y_full_b")
        acc_full, fin_sum, fin_pow, out_ok, stored = sem("acc_full"), sem("fin_sum"), sem("fin_pow"), sem("out_ok"), sem("stored")

        block = stack.enter_context(nc.Block())
        N_IDENT = 4
        N_CONST = 37
        A, B = 0, 1

        def CHUNK_OF(direction, s):
            n_ctx = LCTX // CHUNK
            return s if direction == 0 else n_ctx - 1 - s if s < n_ctx else NCHUNK - 1 + n_ctx - s

        def item_count(eng):
            eng.wait_ge(items_ok, 1)
            return eng.value_load(item_expert[0:1, ITEM_COLS:ITEM_COLS + 1], min_val=1, max_val=ITEMS_MAX)

        def front_landed(n):
            return landed[n % NRING], 16 * (n // NRING + 1)

        def item_of(eng, i):
            return eng.value_load(item_wide[0:1, bass.ds(i, 1)], min_val=0, max_val=1)

        def hid_tile(slot):
            g, half = divmod(slot, 2)
            return (NF // P) * (g // 2) + 2 * half + g % 2

        chunk_used = []
        mark = {}

        @block.tensor
        def _(pe):
            na, nd, taken = [0], [0], [0]

            def a_open():
                if na[0] >= 4:
                    pe.wait_ge(a_empty, na[0] - 3)
                na[0] += 1
                return A_BANKS[(na[0] - 1) % 4]

            def d_open():
                if nd[0] >= 4:
                    pe.wait_ge(d_empty, nd[0] - 3)
                nd[0] += 1
                return D_BANKS[(nd[0] - 1) % 4]

            def next_chunk():
                n = taken[0]
                pe.wait_ge(*front_landed(n))
                taken[0] += 1
                return ring[n % NRING]

            def accumulate(dst, lhs, rhs):
                for k in range(KT):
                    ins = pe.matmul(dst, lhs(k), rhs(k), start=(k == 0), stop=(k == KT - 1))
                return ins

            def used_by_a():
                chunk_used.append((a_full, na[0]))

            def used_by_d():
                chunk_used.append((d_full, nd[0]))

            def transposed(src):
                for g in range(KT // 2):
                    b = a_open()
                    for kk in range(2):
                        for t in range(LAT_TT):
                            kt = 2 * g + kk
                            ins = pe.transpose(b[:, (kk * LAT_TT + t) * P:(kk * LAT_TT + t + 1) * P],
                                               src[:, t, kt * P:(kt + 1) * P], ident[:, :])
                    ins.then_inc(a_full, 1)

            def ada_chunk():
                w = next_chunk()
                b = a_open()
                for r in range(KT // QUADS):
                    for q in range(QUADS):
                        k = r * QUADS + q
                        ins = pe.matmul(b[q * QUAD:(q + 1) * QUAD, :], scT[:, k, :], w[:, k, :], start=(r == 0),
                                        stop=(r == KT // QUADS - 1), skip_group_check=True)
                ins.then_inc(a_full, 1)
                used_by_a()

            pe.wait_ge(const_ok, N_IDENT)
            pe.wait_ge(vec_in, 9 * 16)
            pe.transpose(d_open()[:, 0:112], vec_rows[:, :], ident[0:112, 0:112]).then_inc(d_full, 1)
            pe.wait_ge(sc_ok, 1)
            ada_chunk()
            ada_chunk()
            pe.wait_ge(norm_ok, TT)
            for kt in range(KT):
                b = a_open()
                for t in range(TT):
                    ins = pe.transpose(b[:, t * P:(t + 1) * P], tokens[:, t, kt * P:(kt + 1) * P], ident[:, :])
                ins.then_inc(a_full, 1)
            ada_chunk()

            def mod_columns(n):
                for j in range(n * (NF // P), (n + 1) * (NF // P)):
                    ins = pe.matmul(mod_bank[:, 2 * j:2 * j + 2], mod_part[:, j * P:(j + 1) * P], tile_sum[:, :], start=True, stop=True)
                return ins

            pe.wait_ge(const_ok, N_CONST)
            mod_bank = d_open()
            pe.wait_ge(a_empty, 2)
            mod_columns(0)
            mod_columns(1)
            ada_chunk()
            pe.wait_ge(a_empty, na[0] - 1)
            mod_columns(2)
            pe.wait_ge(a_empty, na[0])
            mod_columns(3).then_inc(d_full, 1)
            pe.wait_ge(rows_in, 32)
            b = d_open()
            for kt in range(KT):
                ins = pe.transpose(b[:, kt * TAPS:(kt + 1) * TAPS], wdw_rows[:, kt * P:(kt + 1) * P], ident[0:TAPS, 0:TAPS])
            ins.then_inc(d_full, 1)
            b = d_open()
            for part in range(2):
                for slot in range(FF // P):
                    j = hid_tile(slot)
                    cols = b1_rows[:, j * 2 * P:(j + 1) * 2 * P].rearrange("e (m two) -> e two m", two=2)[:, part, :]
                    g = part * (FF // P) + slot
                    ins = pe.transpose(b[:, g * E:(g + 1) * E], cols, ident[0:E, 0:E])
            ins.then_inc(d_full, 1)
            pe.wait_ge(bias_in, 5 * 16)
            b = a_open()
            for k in range(KT):
                pe.wait_ge(*((hT_ok, k + 1) if k < MOD_DVE else (hT_hi_ok, k + 1 - MOD_DVE)))
                for d in range(2):
                    ins = pe.matmul(b[d * QUAD:d * QUAD + RANK, :], a_lr_w[:, k, d * RANK:(d + 1) * RANK], hT[:, k, :],
                                    start=(k == 0), stop=(k == KT - 1), skip_group_check=True)
            ins.then_inc(a_full, 1)
            n_a_lr = na[0]
            w = next_chunk()
            for h in range(HEADS):
                b = a_open()
                accumulate(b[:, :], lambda k: w[:, k, h * P:(h + 1) * P], lambda k: hT[:, k, :]).then_inc(a_full, 1)
            used_by_a()
            w = next_chunk()
            for h in range(HEADS):
                b = a_open()
                accumulate(b[:, 0:SEQ], lambda k: w[:, k, h * P:(h + 1) * P], lambda k: hT[:, k, LCTX:T]).then_inc(a_full, 1)
            used_by_a()
            pe.wait_ge(a_empty, n_a_lr)
            def v_chunk():
                w = next_chunk()
                for t in range(TT):
                    b = a_open()
                    accumulate(b[:, :], lambda k: hT[:, k, t * P:(t + 1) * P], lambda k: w[:, k, :]).then_inc(a_full, 1)
                used_by_a()

            for it in range(HD + 1):
                if it < HD:
                    d, h = divmod(it, HEADS)
                    b = d_open()
                    r = slice(d * QUAD, d * QUAD + RANK)
                    pe.matmul(b[:, :], wal[r, h * P:(h + 1) * P], a_lrT[r, :], start=True, stop=True).then_inc(d_full, 1)
                    for g in (2 * it, 2 * it + 1):
                        if g % 4 == 0:
                            w = next_chunk()
                        b = a_open()
                        cs = slice((g % 4) * P, (g % 4 + 1) * P)
                        accumulate(b[:, 0:SEQ], lambda k: w[:, k, cs], lambda k: hT[:, k, LCTX:T]).then_inc(a_full, 1)
                        if g % 4 == 3:
                            used_by_a()
                if it == HD:
                    mark["conv_in"] = na[0]
                    v_chunk()
                if it >= 1:
                    pe.wait_ge(kte_ok, it)
                    b = a_open()
                    for t in range(TT):
                        ins = pe.transpose(b[:, t * P:(t + 1) * P], kte_t[:, t * P:(t + 1) * P], ident[:, :])
                    ins.then_inc(a_full, 1)
                    b = d_open()
                    for t in range(LAT_TT):
                        ins = pe.matmul(b[:, t * P:(t + 1) * P], te_t[:, t * P:(t + 1) * P],
                                        q_dec[:, it - 1, t * P:(t + 1) * P], start=True, stop=True)
                    ins.then_inc(d_full, 1)
            v_chunk()
            mark["v"] = na[0]
            for n in range(6):
                w = next_chunk()
                for t in range(LAT_TT):
                    b = a_open()
                    accumulate(b[:, :], lambda k: hT[:, k, LCTX + t * P:LCTX + (t + 1) * P], lambda k: w[:, k, :]).then_inc(a_full, 1)
                used_by_a()
                if n == 1:
                    mark["g"] = na[0]
            pe.wait_ge(a_empty, mark["v"])
            for hd in range(HD):
                b = d_open()
                h = hd % HEADS
                for t in range(CTX_TT):
                    ins = pe.matmul(b[:, 0:DV], k_end[:, hd, t, :], v[:, t, h * DV:(h + 1) * DV], start=(t == 0), stop=(t == CTX_TT - 1))
                ins.then_inc(d_full, 1)
            for s in range(LCTX // CHUNK, NCHUNK - 1):
                for hd in range(HD):
                    ck = CHUNK_OF(hd // HEADS, s)
                    r = slice((ck % 2) * CHUNK, (ck % 2 + 1) * CHUNK)
                    h = hd % HEADS
                    b = d_open()
                    pe.matmul(b[:, 0:DV], k_end[r, hd, ck // 2, :], v[r, ck // 2, h * DV:(h + 1) * DV],
                              start=True, stop=True).then_inc(d_full, 1)
            pe.wait_ge(ysq_ok, KT)
            b = d_open()
            for n, src in enumerate((yT, ysq)):
                for t in range(LAT_TT):
                    ins = accumulate(b[:, n * LAT_TT + t:n * LAT_TT + t + 1], lambda k: src[:, k, t * P:(t + 1) * P],
                                     lambda k: ones[:, 0:1])
            ins.then_inc(d_full, 1)
            pe.wait_ge(d_empty, nd[0] - 1)
            mark["before_o"] = nd[0]
            for t in range(LAT_TT):
                for h in range(HEADS):
                    b = d_open()
                    pe.matmul(b[:, 0:DV], scores[:, h, t, :], v[:, CTX_TT + t, h * DV:(h + 1) * DV], start=True, stop=False,
                              skip_group_check=True)
                    for d in range(2):
                        for half in range(2):
                            ck = 2 * (CTX_TT + t) + half
                            s = ck if d == 0 else NCHUNK - 1 + LCTX // CHUNK - ck
                            hd = d * HEADS + h
                            q0 = t * P + half * CHUNK
                            ins = pe.matmul(b[half * CHUNK:(half + 1) * CHUNK, 0:DV], q_dec[:, hd, q0:q0 + CHUNK],
                                            state[:, s - LCTX // CHUNK, hd, :], start=False, stop=(d == 1), skip_group_check=True)
                    ins.then_inc(d_full, 1)
            mark["o"] = nd[0]
            pe.wait_ge(ln_cols_ok, 1)
            b = d_open()
            for n in range(2):
                for t in range(LAT_TT):
                    ins = pe.matmul(b[:, (n * LAT_TT + t) * P:(n * LAT_TT + t + 1) * P], ln_wide[:, n, t, :], ident[:, :],
                                    start=True, stop=True)
            ins.then_inc(d_full, 1)
            pe.wait_ge(d_empty, mark["o"])
            transposed(o_sb)

            def flush_late():
                while len(late_done) < len(na_of_late):
                    n = len(late_done)
                    pe.wait_ge(a_empty, na_of_late[n])
                    b = d_open()
                    pe.matmul(b[:, :], tile_sum_all[:, :], late_part[:, n % 2, :], start=True, stop=True).then_inc(d_full, 1)
                    late_done.append(nd[0])

            na_of_late, late_done = [], []

            def scatter_block(blk, first=False, last=False):
                for t in range(LAT_TT):
                    for half in range(2):
                        rows = slice(half * HALF_P, (half + 1) * HALF_P)
                        for part in (y_hi, y_lo):
                            ins = pe.matmul(bank[2 * t + half][:, :], scatter[rows, blk, t, :], part[rows, blk, :], start=first and part is y_hi,
                                            stop=last and part is y_lo, skip_group_check=True)
                    if last:
                        ins.then_inc(acc_full, 1)
                if blk == A and not first and not last:
                    ins.then_inc(scattered, 1)

            def token_rows(src, name):
                for n in range(2):
                    w = next_chunk()
                    for t in range(LAT_TT):
                        b = d_open()
                        accumulate(b[:, :], lambda k: src[:, k, t * P:(t + 1) * P], lambda k: w[:, k, :]).then_inc(d_full, 1)
                        if t == 0:
                            flush_late()
                    used_by_d()
                    if (name, n) != ("out", 1):
                        late_chunks(LATE_AFTER[name][n])

            def late_chunks(count):
                for _ in range(count):
                    ada_chunk()
                    na_of_late.append(na[0])

            pe.wait_ge(a_empty, na[0])
            token_rows(oT, "gla_out")
            mark["oT_read"] = chunk_used[-1 - LATE_AFTER["gla_out"][1]]
            pe.wait_ge(act_conv_ok, KT)
            token_rows(yT, "conv_out")
            mark["yT_read"] = chunk_used[-1 - LATE_AFTER["conv_out"][1]]
            pe.wait_ge(m_ok, 4)
            transposed(m)
            pe.wait_ge(a_empty, na[0])
            token_rows(mT, "out")
            mark["mT_read"] = chunk_used[-1]

            def transposed_h2(t):
                pe.wait_ge(h2_ok, t + 1)
                for g in range(2):
                    b = a_open()
                    for kk in range(KT // 2):
                        k = g * (KT // 2) + kk
                        ins = pe.transpose(b[:, kk * P:(kk + 1) * P], h2[:, t, k * P:(k + 1) * P], ident[:, :])
                    ins.then_inc(a_full, 1)

            transposed_h2(0)
            late_chunks(LATE_AFTER["out"][1])
            transposed_h2(1)
            pe.wait_ge(a_empty, na[0])
            b = d_open()
            for r in range(KT // QUADS):
                for q in range(QUADS):
                    k = r * QUADS + q
                    ins = pe.matmul(b[q * QUAD:(q + 1) * QUAD, 0:SEQ], wr[:, k, :], h2T[:, k, :], start=(r == 0),
                                    stop=(r == KT // QUADS - 1), skip_group_check=True)
            ins.then_inc(d_full, 1)
            pe.wait_ge(d_empty, nd[0])
            b = d_open()
            for t in range(LAT_TT):
                ins = pe.matmul(b[:, t * E:(t + 1) * E], logit_part[:, t * P:(t + 1) * P], quad_fold[:, :], start=True, stop=True)
            ins.then_inc(d_full, 1)
            flush_late()
            mark["b_ada_b_read"] = (d_empty, nd[0])
            mark["late"] = late_done
            pe.wait_ge(y_out[A], 1)
            scatter_block(A, first=True)
            pe.wait_ge(sel_ok, 1)
            b = d_open()
            pe.matmul(b[:, 0:E], before[:, :], sel[:, 0, :], start=True, stop=True)
            pe.matmul(b[:, E:2 * E], ones[:, :], sel[:, 0, :], start=True, stop=False)
            pe.matmul(b[:, E:2 * E], before[:, :], sel[:, 1, :], start=False, stop=True)
            pe.matmul(b[:, 2 * E:3 * E], ones[:, :], sel[:, 0, :], start=True, stop=False)
            pe.matmul(b[:, 2 * E:3 * E], ones[:, :], sel[:, 1, :], start=False, stop=True).then_inc(d_full, 1)

            def gather(halves=(0, 1), banks=(bank[7], bank[6])):
                for half in halves:
                    for kk in range(KT // 2):
                        k = half * (KT // 2) + kk
                        for t in range(LAT_TT):
                            ins = pe.matmul(banks[half][:, kk * SLOTS:(kk + 1) * SLOTS], h2[:, t, k * P:(k + 1) * P], pick[:, t, :],
                                            start=(t == 0), stop=(t == LAT_TT - 1))
                    ins.then_inc(xs_full, 1)

            pe.wait_ge(rank_ok, 1)
            b = d_open()
            xs0_banks = (D_BANKS[(nd[0] - 2) % 4], b)
            mark["xs0_banks"] = xs0_banks
            for t in range(LAT_TT):
                pe.transpose(b[0:E, t * P:(t + 1) * P], rank[:, t, :], ident[:, :])
                ins = pe.transpose(b[0:E, (LAT_TT + t) * P:(LAT_TT + t + 1) * P], prob[:, t, :], ident[:, :])
            ins.then_inc(d_full, 1)
            b = d_open()
            pe.transpose(b[0:E, 0:P], ends[:, 0, :], ident[:, :])
            pe.transpose(b[0:E, P:2 * P], ends[:, 1, :], ident[:, :])
            pe.transpose(b[0:E, 2 * P:3 * P], ends[:, 2, :], ident[:, :]).then_inc(d_full, 1)
            pe.wait_ge(pick_ok, 1)
            gather((0,), xs0_banks)
            pe.wait_ge(one_item_ok, 1)
            b = d_open()
            for t in range(LAT_TT):
                pe.matmul(b[:, t * ITEM_COLS:(t + 1) * ITEM_COLS], rankT[:, t, :], one_item[:, :], start=True, stop=True)
                pe.matmul(b[:, (LAT_TT + t) * ITEM_COLS:(LAT_TT + t + 1) * ITEM_COLS], probT[:, t, :], one_item[:, :], start=True, stop=True)
            for n in range(2):
                ins = pe.matmul(b[0:1, (2 * LAT_TT + n) * ITEM_COLS:(2 * LAT_TT + n + 1) * ITEM_COLS], ecol[:, 2 + n:3 + n],
                                one_item[:, :], start=True, stop=True)
            ins.then_inc(d_full, 1)

            gather((1,), xs0_banks)
            pe.wait_ge(d_empty, nd[0])

            def product(i, n, blocks, dst, tokens_of, uses=True):
                for m in range(UPP):
                    w = unit[n * UPP + m]
                    pe.wait_ge(unit_landed[n * UPP + m], i * 16 + 32)
                    for kk in range(UK):
                        k = m * UK + kk
                        for blk in blocks:
                            for half in range(2):
                                ins = pe.matmul(dst[blk][half * HALF_P:(half + 1) * HALF_P, :], tokens_of(blk, k),
                                                w[:, kk, half * NF:(half + 1) * NF],
                                                start=(k == 0), stop=(k == KT - 1), skip_group_check=True)
                    if uses:
                        ins.then_inc(unit_used, 1)
                return ins

            def transpose_hid(i, blk):
                pe.wait_ge(hid_out[blk], i * 2 + 2)
                dst = bank[6:8] if blk == B else bank[4:6]
                for part in range(2):
                    for g in range(JH):
                        pair, jj = divmod(g, 2)
                        cols = hid[:, blk, pair, jj * 2 * P:(jj + 1) * 2 * P].rearrange("s (m two) -> s two m", two=2)[:, part, :]
                        ins = pe.transpose(dst[part][:, g * P:(g + 1) * P], cols, ident[:, :])
                    ins.then_inc(ht_full[blk], 1)

            def transpose_weigh(i, dst):
                pe.wait_ge(weigh_ok, i + 1)
                for blk in range(2):
                    for t in range(LAT_TT):
                        ins = pe.transpose(dst[:, (2 * blk + t) * P:(2 * blk + t + 1) * P], weigh[:, t, blk, :], ident[:, :])
                ins.then_inc(sc_full, 1)

            def item_pe(i, blocks):
                wide = B in blocks
                pe.wait_ge(xs_out, i * 2 + 2)
                if wide:
                    pe.wait_ge(sc_out, i + 1)
                for n in range(PAIRS):
                    if wide and n == 1:
                        pe.wait_ge(y_out[A], i + 1)
                    product(i, n, blocks, {A: bank[4 + n], B: bank[6 + n]},
                            lambda blk, k: xs[:, k, blk * HALF_P:(blk + 1) * HALF_P])
                if wide:
                    scatter_block(A)
                    transpose_hid(i, B)
                    transpose_hid(i, A)
                    pe.wait_ge(ht_out[B], i * 2 + 2)
                    pe.wait_ge(pick_ok, i + 2)
                    gather()
                    pe.wait_ge(ht_out[A], i * 2 + 2)
                    transpose_weigh(i, bank[4])
                else:
                    pe.sem_inc(ht_full[B], 2)
                    pe.sem_inc(yb_full, 1)
                    transpose_weigh(i, bank[6])
                    transpose_hid(i, A)
                    pe.wait_ge(y_out[A], i + 1)
                    pe.wait_ge(pick_ok, i + 2)
                    gather((0,))
                    pe.wait_ge(weighT_ok, i + 1)
                    gather((1,))
                    pe.wait_ge(sc_out, i + 1)
                    scatter_block(A)
                place = {hid_tile(slot): slot for slot in range(FF // P)}
                hs_of = lambda blk, k: hs[:, blk, place[k], :]
                if wide:
                    pe.wait_ge(hs_ok[B], i + 1)
                    product(i, PAIRS, [B], {B: bank[5]}, hs_of, uses=False).then_inc(yb_full, 1)
                pe.wait_ge(xs_out, i * 2 + 3)
                pe.wait_ge(hs_ok[A], i + 1)
                product(i, PAIRS, [A], {A: bank[7]}, hs_of)
                if wide:
                    pe.wait_ge(y_out[B], i + 1)
                    pe.wait_ge(sc_out, i + 2)
                    scatter_block(B)

            pe.wait_ge(b2_in, 16)
            items_pe = item_count(pe)
            with pe.Fori(0, items_pe) as i:
                wide = item_of(pe, i)
                with pe.If(wide == 0):
                    item_pe(i, [A])
                with pe.Else():
                    item_pe(i, [B, A])
                with pe.If(i == ITEMS_MIN - 1):
                    for t in range(LAT_TT):
                        for n in range(2):
                            pe.matmul(bank[2 * t + n][:, :], probT[:, t, :], b2_rows[:, n * NF:(n + 1) * NF], start=False, stop=False,
                                      skip_group_check=True)
                pe.sem_inc(items_done, 1)
            pe.wait_ge(y_out[A], items_pe + 1)
            pe.wait_ge(sc_out, items_pe + 1)
            scatter_block(A, last=True)

        @block.sync
        def _(sp):
            def bcast(row):
                return row.partition_broadcast(P)

            sp.dma_start(ring[0][:, :, :], stream[0]).then_inc(landed[0], 16)
            row0 = 0
            for vec in (g_mix_norm[0], g_ffn_norm[0], b_dw[0], g_conv_ln[0], b_conv_ln[0],
                        b_alpha[0].rearrange("a b -> (a b)"), c[0], c_ctx, b_ada[0]):
                rows = vec.rearrange("(r p) -> r p", p=P)
                n = min(rows.shape[0], 112 - row0)
                sp.dma_start(vec_rows[row0:row0 + n, :], rows[0:n, :]).then_inc(vec_in, 16)
                row0 += n
            sp.dma_start(tokens[:, 0:CTX_TT, :], ctx_tokens[0].rearrange("(t p) d -> p t d", p=P)).then_inc(tok_in, 16)
            sp.dma_start(tokens[:, CTX_TT:TT, :], x[0].rearrange("(t p) d -> p t d", p=P)).then_inc(tok_in, 16)
            for n in range(1, NRING):
                sp.dma_start(ring[n][:, :, :], stream[n]).then_inc(landed[n], 16)

            def small_loads():
                sp.dma_start(wdw_rows[:, :], w_dw[0]).then_inc(rows_in, 16)
                sp.dma_start(b1_rows[:, :], b_exp_in[0]).then_inc(rows_in, 16)
                sp.dma_start(a_lr_w[:, :, :], w_in[0].rearrange("(t p) n -> p t n", p=P)[:, :, c0["a_lr"]:c0["gate_conv"]]) \
                    .then_inc(bias_in, 16)
                for d in range(2):
                    sp.dma_start(wal[d * QUAD:d * QUAD + RANK, :], w_alpha[0, d]).then_inc(bias_in, 16)
                sp.dma_start(wr[:, :, :], w_router[0].rearrange("(t p) n -> p t n", p=P)).then_inc(bias_in, 16)
                sp.dma_start(gla_g[:, :], bcast(g_gla_norm)).then_inc(bias_in, 16)

            def item_weights(e, refill=None, again=False, order=range(UPI), ready={}):
                w1 = w_exp_in[0][bass.ds(e, 1)].rearrange("a (t p) n -> (a p) t n", p=P)
                w2 = w_exp_out[0][bass.ds(e, 1)].rearrange("a (t p) n -> (a p) t n", p=P)
                for n in order:
                    pair, m = divmod(n, UPP)
                    src = w1[:, m * UK:(m + 1) * UK, pair * UN:(pair + 1) * UN] if pair < PAIRS else w2[:, m * UK:(m + 1) * UK, :]
                    if refill is not None:
                        sp.wait_ge(unit_used, refill * UPI + (n + 1 - UPI))
                    if again:
                        sp.wait_ge(unit_landed[n], 16)
                    for gate in ready.get(n, ()):
                        sp.wait_ge(*gate)
                    sp.dma_start(unit[n][:, :, :], src).then_inc(unit_landed[n], 16)

            slot_free = lambda n: [chunk_used[max(c for c in range(NSTREAM) if c % NRING == n // 2)]]
            gone = [mark["b_ada_b_read"]]
            ready = {n: slot_free(n) for n in range(6)}
            ready.update({6: gone, 7: gone, 8: [chunk_used[n_proj]], 9: [mark["mT_read"]], 10: [chunk_used[n_proj]], 11: [mark["yT_read"]]})
            EARLY_UNITS = ((10, 4), (8, 6), (11, 11))

            for n in range(NRING, NSTREAM):
                sp.wait_ge(*chunk_used[n - NRING])
                sp.dma_start(ring[n % NRING][:, :, :], stream[n]).then_inc(landed[n % NRING], 16)
                if n == NRING:
                    small_loads()
                if n == n_proj + NRING - 1:
                    sp.dma_start(b_ada_b[:, :], bcast(b_ada[0:1, 2 * D:6 * D])).then_inc(b_ada_in, 16)
                if n == NSTREAM - 1:
                    sp.wait_ge(*mark["yT_read"])
                    sp.dma_start(b2_rows[:, :], b_exp_out[0]).then_inc(b2_in, 16)
                for early, after in EARLY_UNITS:
                    if n == n_proj + after:
                        item_weights(0, order=[early], ready=ready)
                if n == n_proj + NRING:
                    sp.dma_start(x1[:, :, :], x[0].rearrange("(t p) d -> p t d", p=P)).then_inc(x_again_in, 16)
                    sp.dma_start(g_ffn_b[:, :], bcast(g_ffn_norm)).then_inc(late_in, 16)
                    sp.dma_start(b_router_b[:, :], bcast(b_router)).then_inc(late_in, 16)
            item_weights(0, order=[n for s in sorted(range(NRING), key=lambda s: (s - NSTREAM) % NRING) for n in (2 * s, 2 * s + 1)]
                         + [9, 6, 7], ready=ready)
            items = item_count(sp)
            e = sp.value_load(item_expert[0:1, 0:1], min_val=0, max_val=E - 1)
            with sp.If(e == 0):
                for n in range(UPI):
                    sp.sem_inc(unit_landed[n], 16)
            with sp.Else():
                item_weights(e, again=True)
            with sp.Fori(1, items) as i:
                item_weights(sp.value_load(item_expert[0:1, bass.ds(i, 1)], min_val=0, max_val=E - 1), refill=i)
            sp.dma_start(g_final_b[:, :], bcast(g_final.rearrange("(a d) -> a d", a=1))).then_inc(g_final_in, 16)
            for t in range(LAT_TT):
                sp.wait_ge(out_ok, t + 1)
                sp.wait_ge(out_act_ok, t + 1)
                sp.dma_start(out[0, t * P:(t + 1) * P, :], out_sb[:, t, :]).then_inc(stored, 16)
            sp.wait_ge(stored, 16 * LAT_TT)

        @block.gpsimd
        def _(pool):
            done = Tally(const_ok)

            def wait_own():
                pool.wait_ge(const_ok, done.n)

            done.sign(pool.memset(ident[:, :], 0.0))
            done.sign(pool.memset(scT[:, :, :], 0.0))
            wait_own()
            done.sign(pool.affine_select(out=ident[:, :], in_=ident[:, :], compare_op=ALU.not_equal, fill=1.0, base=0,
                                         pattern=[[-1, P]], channel_multiplier=1))
            done.sign(pool.memset(neg_half[:, :], -0.5))
            assert done.n == N_IDENT
            done.sign(pool.memset(ones[:, :], 1.0))
            done.sign(pool.memset(tile_sum[:, :], 0.0))
            done.sign(pool.memset(tile_sum_all[:, :], 0.0))
            done.sign(pool.memset(mask_f[:, :], 1.0))
            done.sign(pool.memset(mask_b[:, :], 1.0))
            done.sign(pool.memset(scan_keep[:, :], 1.0))
            done.sign(pool.memset(quad_fold[:, :], 0.0))
            for q in range(QUADS):
                wait_own()
                done.sign(pool.affine_select(out=quad_fold[:, :], in_=quad_fold[:, :], compare_op=ALU.not_equal, fill=1.0,
                                             base=-q * QUAD, pattern=[[-1, QUAD]], channel_multiplier=1))
            for q in range(QUADS):
                wait_own()
                done.sign(pool.affine_select(out=tile_sum[:, :], in_=tile_sum[:, :], compare_op=ALU.not_equal, fill=1.0,
                                             base=-q * QUAD, pattern=[[-1, 2]], channel_multiplier=1))
                done.sign(pool.affine_select(out=tile_sum_all[:, :], in_=tile_sum_all[:, :], compare_op=ALU.not_equal, fill=1.0,
                                             base=-q * QUAD, pattern=[[0, P]], channel_multiplier=1))
            done.sign(pool.iota(slot_no[:, :], [[1, SLOTS]], base=0, channel_multiplier=0,
                                allow_small_or_imprecise_dtypes=True))
            done.sign(pool.iota(slot_twice[:, :, :, :], [[HALF_P, 2], [0, 2], [1, HALF_P]], base=0, channel_multiplier=0,
                                allow_small_or_imprecise_dtypes=True))
            wait_own()
            done.sign(pool.affine_select(out=before[:, :], in_=ones[:, :], compare_op=ALU.is_gt, fill=0.0, base=0,
                                         pattern=[[1, P]], channel_multiplier=-1))
            keep = scan_keep[:, LCTX:T].rearrange("p (c t) -> p c t", t=CHUNK)
            done.sign(pool.memset(keep[:, :, 0:1], 0.0))
            done.sign(pool.memset(scan_keep[:, 0:1], 0.0))
            for b in range(P // CHUNK):
                cols = slice(b * CHUNK, (b + 1) * CHUNK)
                for mask in (mask_f, mask_b):
                    wait_own()
                    sign = 1 if mask is mask_f else -1
                    done.sign(pool.affine_select(out=mask[:, cols], in_=mask[:, cols], compare_op=ALU.is_ge, fill=0.0,
                                                 base=sign * b * CHUNK, pattern=[[sign, CHUNK]], channel_multiplier=-sign))
                    wait_own()
                    if mask is mask_f:
                        done.sign(pool.affine_select(out=mask[:, cols], in_=mask[:, cols], compare_op=ALU.is_ge, fill=0.0,
                                                     base=-b * CHUNK, pattern=[[0, CHUNK]], channel_multiplier=1))
                    else:
                        done.sign(pool.affine_select(out=mask[:, cols], in_=mask[:, cols], compare_op=ALU.is_ge, fill=0.0,
                                                     base=(b + 1) * CHUNK - 1, pattern=[[0, CHUNK]], channel_multiplier=-1))
            done.sign(pool.memset(u[:, :, :, :], 0.0))
            assert done.n == N_CONST, done.n
            steps = Tally(pool_ok)

            def rstd_of(sums, count, n, gate, gate_n, signal):
                pool.wait_ge(gate, gate_n)
                steps.sign(pool.tensor_scalar(sums, sums, 1.0 / count, EPS, ALU.mult, ALU.add))
                pool.wait_ge(pool_ok, steps.n)
                pool.tensor_tensor(sums, sums, neg_half[:, 0:n], ALU.pow).then_inc(signal, 1)

            rstd_of(stat[:, 0:TT], D, TT, sums_ok, TT, pow_ok)
            rstd_of(stat[:, 26:26 + LAT_TT], 1, LAT_TT, ln_var_ok, 1, ln_rstd_ok)
            for n in range(LAT_TT * HEADS):
                rstd_of(stat[:, 8 + n:9 + n], DV, 1, oss_ok, n + 1, orstd_ok)
            for t in range(LAT_TT):
                rstd_of(stat[:, 16 + t:17 + t], D, 1, x1_sum, t + 1, x1_pow)
            pool.wait_ge(ms_free, 1)
            pool.iota(item_no[:, :], [[1, ITEM_COLS]], base=0, channel_multiplier=0,
                      allow_small_or_imprecise_dtypes=True).then_inc(const_ok, 1)
            pool.iota(ecol[:, 2:3], [[0, 1]], base=0, channel_multiplier=1,
                      allow_small_or_imprecise_dtypes=True).then_inc(const_ok, 1)
            pool.wait_ge(g_final_in, 16)
            for t in range(LAT_TT - 1):
                pool.wait_ge(x2_ok, 2 * t + 2)
                pool.tensor_tensor(out_sb[:, t, :], x1[:, t, :], g_final_b[:, :], ALU.mult).then_inc(scaled_ok, 1)
            for t in range(LAT_TT):
                rstd_of(stat[:, 20 + t:21 + t], D, 1, fin_sum, t + 1, fin_pow)

        @block.scalar
        def _(act):
            groups = [0]

            def a_bank():
                groups[0] += 1
                act.wait_ge(a_full, groups[0])
                return A_BANKS[(groups[0] - 1) % 4]

            act.wait_ge(dve_ok, 1)
            act.activation(sc_act[:, :], vecT[:, 48:48 + 2 * KT], ACT.Sigmoid).then_inc(sc_sig, 1)
            act.wait_ge(tok_in, 32)
            for t in range(TT):
                if t >= 1:
                    act.wait_ge(sums_ok, t)
                act.activation(sq_junk[:, :], tokens[:, t, :], ACT.Square,
                               accum_out=stat[:, t:t + 1]).then_inc(sums_ok, 1)
            def mod_copy(n):
                b = a_bank()
                act.activation(mod_part[:, n * NF:(n + 1) * NF], b[:, :], ACT.Copy).then_inc(a_empty, 1)

            mod_copy(0)
            mod_copy(1)
            for kt in range(KT):
                b = a_bank()
                act.activation(hT[:, kt, :], b[:, :], ACT.Copy).then_inc(a_empty, 1)
            raw = groups[0]
            mod_copy(2)
            mod_copy(3)
            act.wait_ge(mod_ok, 1)
            act.wait_ge(a_empty, raw)
            for kt in range(MOD_DVE, KT):
                for s, (lo, hi) in enumerate(((LCTX, T), (0, LCTX))):
                    ins = act.activation(hT[:, kt, lo:hi], hT[:, kt, lo:hi], ACT.Identity, bias=modT[:, kt, s:s + 1],
                                         scale=modT[:, KT + kt, s:s + 1])
                ins.then_inc(hT_hi_ok, 1)
            b = a_bank()
            for d in range(2):
                r = slice(d * QUAD, d * QUAD + RANK)
                ins = act.activation(a_lrT[r, :], b[r, :], ACT.Copy)
            ins.then_inc(a_empty, 1)
            for h in range(HEADS):
                b = a_bank()
                act.activation(kT[:, h, :], b[:, :], ACT.Copy).then_inc(a_empty, 1)
            for h in range(HEADS):
                b = a_bank()
                act.activation(qT[:, h, :], b[:, 0:SEQ], ACT.Copy, scale=float(DK) ** -0.5).then_inc(a_empty, 1)

            def conv_input(n):
                for g in (2 * n, 2 * n + 1):
                    half, r = divmod(g, KT)
                    is_b, ct = r // 4, half * 4 + r % 4
                    b = a_bank()
                    if is_b:
                        act.activation(yT[:, ct, :], b[:, 0:SEQ], ACT.Sigmoid).then_inc(a_empty, 1)
                    else:
                        act.activation(u[:, ct, :, PAD:PAD + GRID_W], b[:, 0:SEQ].rearrange("p (r w) -> p r w", w=GRID_W),
                                       ACT.Copy).then_inc(a_empty, 1)

            def v_copies(n):
                for t in range(TT):
                    b = a_bank()
                    act.activation(v[:, t, n * NF:(n + 1) * NF], b[:, :], ACT.Copy).then_inc(a_empty, 1)

            for it in range(HD + 1):
                if it < HD:
                    act.wait_ge(z_ok, it + 1)
                    act.activation(e_t[:, :], e_t[:, :], ACT.Exp).then_inc(act_ok, 1)
                    act.wait_ge(act_ok, it + 1)
                    act.activation(e_t[:, :], e_t[:, :], ACT.Ln, bias=1.0).then_inc(ln_ok, 1)
                    conv_input(it)
                    act.wait_ge(te_ok, it + 1)
                    act.activation(la_t[:, 0:SEQ], z_t[:, 0:SEQ], ACT.Exp, scale=1.0 / TAU)
                    act.activation(e_t[:, 0:SEQ], z_t[:, 0:SEQ], ACT.Exp, scale=-1.0 / TAU)
                    act.activation(decay[:, it, :], pre_t[:, :].rearrange("p (c t) -> p c t", t=CHUNK)[:, :, CHUNK - 1],
                                   ACT.Exp, scale=1.0 / TAU)
                    act.activation(et_t[:, :], te_t[:, :], ACT.Exp, scale=1.0 / TAU).then_inc(et_ok, 1)
                if it == HD:
                    v_copies(0)
                if it >= 1:
                    b = a_bank()
                    act.activation(k_end[:, it - 1, :, :], b[:, :].rearrange("p (t k) -> p t k", k=P), ACT.Copy).then_inc(a_empty, 1)
            v_copies(1)
            act.wait_ge(kte_ok, HD)
            for dst, fn in ((sgn, ACT.Silu), (sg_conv, ACT.Sigmoid), (sg_gla, ACT.Sigmoid)):
                for n in range(2):
                    for t in range(LAT_TT):
                        b = a_bank()
                        ins = act.activation(dst[:, t, n * NF:(n + 1) * NF], b[:, :], fn)
                        ins.then_inc(a_empty, 1)
            act.wait_ge(conv_ok, KT)
            for ct in range(KT):
                act.activation(ysq[:, ct, :], yT[:, ct, :], ACT.Square).then_inc(ysq_ok, 1)
            for n in range(LAT_TT * HEADS):
                act.wait_ge(d_full, mark["before_o"] + n + 1)
                if n >= 1:
                    act.wait_ge(oss_ok, n)
                act.activation(o_junk[:, :], D_BANKS[(mark["before_o"] + n) % 4][:, 0:DV], ACT.Square,
                               accum_out=stat[:, 8 + n:9 + n]).then_inc(oss_ok, 1)

            def transposed_copy(dst):
                for g in range(4):
                    b = a_bank()
                    act.activation(dst[:, 2 * g:2 * g + 2, :], b[:, :].rearrange("p (k t) -> p k t", k=2), ACT.Copy).then_inc(a_empty, 1)

            transposed_copy(oT)
            for ct in range(KT):
                act.wait_ge(ln_in, ct + 1)
                act.activation(yT[:, ct, :], yT[:, ct, :], ACT.Silu, scale=vecT[:, 24 + ct:25 + ct],
                               bias=vecT[:, 32 + ct:33 + ct]).then_inc(act_conv_ok, 1)

            def late_copies(chunks):
                for _ in range(chunks):
                    b = a_bank()
                    n = late_done[0]
                    if n >= 2:
                        act.wait_ge(d_full, mark["late"][n - 2])
                    act.activation(late_part[:, n % 2, :], b[:, :], ACT.Copy).then_inc(a_empty, 1)
                    late_done[0] += 1

            late_done = [0]
            late_copies(sum(LATE_AFTER["gla_out"]) + sum(LATE_AFTER["conv_out"]))
            transposed_copy(mT)
            for n in range(2):
                if n == 1:
                    late_copies(LATE_AFTER["out"][0])
                for t in range(LAT_TT):
                    act.wait_ge(x1_ok, n * LAT_TT + t + 1)
                    act.activation(sq_x1[:, t, n * NF:(n + 1) * NF], x1[:, t, n * NF:(n + 1) * NF], ACT.Square,
                                   accum_out=stat[:, 32 + 2 * t + n:33 + 2 * t + n]).then_inc(sq_ok, 1)
            for t in range(LAT_TT):
                for g in range(2):
                    b = a_bank()
                    act.activation(h2T[:, g * (KT // 2):(g + 1) * (KT // 2), t * P:(t + 1) * P],
                                   b[:, :].rearrange("p (k t) -> p k t", t=P), ACT.Copy).then_inc(a_empty, 1)
                if t == 0:
                    late_copies(LATE_AFTER["out"][1])
            act.wait_ge(max_ok, 1)
            for t in range(LAT_TT):
                act.activation(expo[:, t, :], logits[:, t, :], ACT.Exp, bias=need[:, t, 3:4]).then_inc(exp_ok, 1)


            def take_xs(i, banks=(bank[7], bank[6])):
                for half in range(2):
                    act.wait_ge(xs_full, i * 2 + (half + 1))
                    act.activation(xs[:, half * (KT // 2):(half + 1) * (KT // 2), :],
                                   banks[half][:, :].rearrange("p (k c) -> p k c", c=SLOTS), ACT.Copy).then_inc(xs_out, 1)

            def take_weights(i, src):
                act.wait_ge(sc_full, i + 1)
                for blk in range(2):
                    ins = act.activation(weighT[:, blk, :, :], src[:, blk * SEQ:(blk + 1) * SEQ].rearrange("p (t c) -> p t c", c=P),
                                         ACT.Copy, accum_out=slot_prob[:, blk:blk + 1])
                ins.then_inc(weighT_ok, 1)

            def item_act(i, blocks):
                wide = B in blocks
                for n in range(PAIRS):
                    act.wait_ge(unit_used, i * UPI + (n + 1) * UPP)
                    for blk in blocks:
                        act.activation(hid[:, blk, n, :], bank[(6 if blk == B else 4) + n][:, :], ACT.Copy).then_inc(hid_out[blk], 1)
                if not wide:
                    take_weights(i, bank[6])
                for blk in blocks:
                    act.wait_ge(glu_ok[blk], i + 1)
                    act.activation(sig[:, blk, :, :], swi[:, blk, 0, :, :], ACT.Sigmoid, scale=ALPHA).then_inc(sig_ok[blk], 1)
                take_xs(i + 1)
                if wide:
                    take_weights(i, bank[4])
                    act.wait_ge(yb_full, i + 1)
                    act.wait_ge(weighT_ok, i + 1)
                    act.activation(y_hi[:, B, :], bank[5][:, :], ACT.Copy, scale=slot_prob[:, B:B + 1]).then_inc(yh_ok[B], 1)
                else:
                    act.sem_inc(hid_out[B], 2)
                    act.sem_inc(sig_ok[B], 1)
                    act.sem_inc(yh_ok[B], 1)

            take_xs(0, mark["xs0_banks"])
            items = item_count(act)
            with act.Fori(0, items) as i:
                wide = item_of(act, i)
                with act.If(wide == 0):
                    item_act(i, [A])
                with act.Else():
                    item_act(i, [B, A])
                act.wait_ge(unit_used, i * UPI + UPI)
                act.wait_ge(weighT_ok, i + 1)
                act.activation(y_hi[:, A, :], bank[7][:, :], ACT.Copy, scale=slot_prob[:, A:A + 1]).then_inc(yh_ok[A], 1)
            for t in range(LAT_TT):
                for n in range(2):
                    act.wait_ge(x2_ok, 2 * t + n + 1)
                    act.activation(fin_junk[:, t, n * NF:(n + 1) * NF], x1[:, t, n * NF:(n + 1) * NF], ACT.Square,
                                   accum_out=stat[:, 36 + 2 * t + n:37 + 2 * t + n]).then_inc(fin_sq, 1)
            for t in range(LAT_TT):
                act.wait_ge(fin_pow, t + 1)
                act.wait_ge(*((scaled_ok, t + 1) if t < LAT_TT - 1 else (scaled_last_ok, 1)))
                act.activation(out_sb[:, t, NF:D], out_sb[:, t, NF:D], ACT.Copy, scale=stat[:, 20 + t:21 + t]).then_inc(out_act_ok, 1)

        @block.vector
        def _(dve):
            step = Tally(dve_ok)
            groups = [0]

            def d_bank():
                groups[0] += 1
                dve.wait_ge(d_full, groups[0])
                return D_BANKS[(groups[0] - 1) % 4]

            def own():
                dve.wait_ge(dve_ok, step.n)

            b = d_bank()
            dve.tensor_copy(vecT[:, :], b[:, 0:112]).then_inc(d_empty, 1)
            dve.wait_ge(d_empty, 1)
            step.sign(dve.memset(stat[:, :], 0.0))
            dve.wait_ge(sc_sig, 1)
            dve.wait_ge(const_ok, N_IDENT)
            dve.tensor_tensor(scT[:, :, 0:2].rearrange("p k s -> p s k"), vecT[:, 48:48 + 2 * KT].rearrange("p (s k) -> p s k", s=2),
                              sc_act[:, :].rearrange("p (s k) -> p s k", s=2), ALU.mult).then_inc(sc_ok, 1)
            dve.wait_ge(pow_ok, 1)
            for t in range(TT):
                dve.tensor_scalar(tokens[:, t, :], tokens[:, t, :], stat[:, t:t + 1], None, ALU.mult).then_inc(norm_ok, 1)
            b = d_bank()
            bias = vecT[:, 64:64 + 2 * KT].unsqueeze(2).to_broadcast([P, 2 * KT, 2])
            dve.tensor_tensor(modT[:, :, :], b[:, 0:4 * KT].rearrange("p (k s) -> p k s", s=2), bias, ALU.add).then_inc(d_empty, 1)
            dve.wait_ge(d_empty, groups[0])
            gmix = vecT[:, 0:KT].unsqueeze(2).to_broadcast([P, KT, 2])
            dve.scalar_tensor_tensor(modT[:, KT:2 * KT, :], modT[:, KT:2 * KT, :], 1.0, gmix, ALU.add, ALU.mult).then_inc(mod_ok, 1)
            dve.wait_ge(mod_ok, 1)
            dve.wait_ge(a_empty, 2 + KT)
            for kt in range(MOD_DVE):
                for sample, (lo, hi) in enumerate(((LCTX, T), (0, LCTX))):
                    ins = dve.tensor_scalar(hT[:, kt, lo:hi], hT[:, kt, lo:hi], modT[:, KT + kt, sample:sample + 1],
                                            modT[:, kt, sample:sample + 1], ALU.mult, ALU.add)
                ins.then_inc(hT_ok, 1)
            b = d_bank()
            dve.tensor_copy(wdwT[:, :, :], b[:, 0:KT * TAPS].rearrange("p (k w) -> p k w", w=TAPS)).then_inc(d_empty, 1)
            b = d_bank()
            dve.tensor_copy(b1T[:, :, :].rearrange("p e j -> p j e"), b[:, :].rearrange("p (j e) -> p j e", e=E)).then_inc(d_empty, 1)

            dve.wait_ge(const_ok, N_CONST)
            per_chunk = lambda t: t[:, :].rearrange("p (c t) -> p c t", t=CHUNK)
            def masked_scores(chain):
                pd, ph = divmod(chain, HEADS)
                b = d_bank()
                sc2 = b[:, 0:SEQ].rearrange("p (t c) -> p t c", c=P)
                mask = (mask_f, mask_b)[pd][:, :].unsqueeze(1).to_broadcast([P, LAT_TT, P])
                if pd == 0:
                    dve.tensor_tensor(scores[:, ph, :, :], sc2, mask, ALU.mult).then_inc(d_empty, 1)
                else:
                    dve.tensor_tensor(kte_t[:, 0:SEQ].rearrange("p (t c) -> p t c", c=P), sc2, mask, ALU.mult).then_inc(d_empty, 1)
                    dve.wait_ge(d_empty, groups[0])
                    step.sign(dve.tensor_tensor(scores[:, ph, :, :], scores[:, ph, :, :],
                                                kte_t[:, 0:SEQ].rearrange("p (t c) -> p t c", c=P), ALU.add))

            for it in range(HD):
                d, h = divmod(it, HEADS)
                b = d_bank()
                dve.tensor_scalar(z_t[:, :], b[:, :], vecT[:, 40 + it:41 + it], None, ALU.add).then_inc(d_empty, 1)
                dve.wait_ge(d_empty, groups[0])
                dve.scalar_tensor_tensor(e_t[:, :], z_t[:, :], -1.0, z_t[:, :], ALU.mult, ALU.min).then_inc(z_ok, 1)
                if it >= 1:
                    masked_scores(it - 1)
                dve.wait_ge(ln_ok, it + 1)
                step.sign(dve.scalar_tensor_tensor(la_t[:, :], z_t[:, :], 0.0, e_t[:, :], ALU.min, ALU.subtract))
                own()
                step.sign(dve.tensor_tensor_scan(pre_t[:, :], scan_keep[:, :], la_t[:, :], 0.0, ALU.mult, ALU.add))
                own()
                nl = LCTX // CHUNK
                total = per_chunk(pre_t)[:, nl:NCHUNK, CHUNK - 1:CHUNK].to_broadcast([P, NCHUNK - nl, CHUNK])
                if d == 0:
                    dve.tensor_copy(z_t[:, 0:SEQ], pre_t[:, LCTX:T])
                    dve.tensor_scalar(te_t[:, 0:LCTX], pre_t[:, 0:LCTX], -1.0, pre_t[:, LCTX - 1:LCTX], ALU.mult, ALU.add)
                    dve.tensor_tensor(per_chunk(te_t)[:, nl:NCHUNK, :], total, per_chunk(pre_t)[:, nl:NCHUNK, :],
                                      ALU.subtract).then_inc(te_ok, 1)
                else:
                    step.sign(dve.tensor_tensor(te_t[:, :], pre_t[:, :], la_t[:, :], ALU.subtract))
                    own()
                    dve.tensor_tensor(z_t[:, 0:SEQ].rearrange("p (c t) -> p c t", t=CHUNK), total,
                                      per_chunk(te_t)[:, nl:NCHUNK, :], ALU.subtract).then_inc(te_ok, 1)
                dve.wait_ge(et_ok, it + 1)
                step.sign(dve.tensor_tensor(q_dec[:, it, :], qT[:, h, :], la_t[:, 0:SEQ], ALU.mult))
                step.sign(dve.tensor_tensor(te_t[:, 0:SEQ], kT[:, h, LCTX:T], e_t[:, 0:SEQ], ALU.mult))
                dve.tensor_tensor(kte_t[:, :], kT[:, h, :], et_t[:, :], ALU.mult).then_inc(kte_ok, 1)

            dve.wait_ge(a_empty, mark["conv_in"])
            for ct in range(KT):
                rows = lambda k: u[:, ct, :, k:k + GRID_W]
                yv = yT[:, ct, :].rearrange("p (r w) -> p r w", w=GRID_W)
                step.sign(dve.tensor_tensor(rows(PAD), rows(PAD), yv, ALU.mult))
                own()
                step.sign(dve.tensor_scalar(yv, rows(0), wdwT[:, ct, 0:1], vecT[:, 16 + ct:17 + ct], ALU.mult, ALU.add))
                for k in range(1, TAPS):
                    own()
                    ins = dve.scalar_tensor_tensor(yv, rows(k), wdwT[:, ct, k:k + 1], yv, ALU.mult, ALU.add)
                    if k < TAPS - 1:
                        step.sign(ins)
                    else:
                        ins.then_inc(conv_ok, 1)
            masked_scores(HD - 1)

            for hd in range(HD):
                b = d_bank()
                dve.tensor_copy(state[:, 0, hd, :], b[:, 0:DV]).then_inc(d_empty, 1)
            first = LCTX // CHUNK
            for s in range(first, NCHUNK - 1):
                for hd in range(HD):
                    b = d_bank()
                    dve.wait_ge(d_empty, groups[0] - HD)
                    ck = CHUNK_OF(hd // HEADS, s)
                    dve.scalar_tensor_tensor(state[:, s + 1 - first, hd, :], state[:, s - first, hd, :], decay[:, hd, ck:ck + 1],
                                             b[:, 0:DV], ALU.mult, ALU.add).then_inc(d_empty, 1)
            mean, var = stat[:, 24:24 + LAT_TT], stat[:, 26:26 + LAT_TT]
            b = d_bank()
            step.sign(dve.tensor_scalar(mean, b[:, 0:LAT_TT], 1.0 / D, None, ALU.mult))
            own()
            step.sign(dve.tensor_tensor(stat[:, 28:28 + LAT_TT], mean, mean, ALU.mult))
            own()
            dve.scalar_tensor_tensor(var, b[:, LAT_TT:2 * LAT_TT], 1.0 / D, stat[:, 28:28 + LAT_TT], ALU.mult,
                                     ALU.subtract).then_inc(d_empty, 1)
            dve.wait_ge(d_empty, groups[0])
            step.sign(dve.tensor_scalar(var, var, 0.0, None, ALU.max))
            own()
            dve.sem_inc(ln_var_ok, 1)
            dve.wait_ge(a_empty, mark["g"])
            for t in range(LAT_TT):
                for h in range(HEADS):
                    step.sign(dve.tensor_tensor(sgn[:, t, h * DV:(h + 1) * DV], sgn[:, t, h * DV:(h + 1) * DV], gla_g[:, :], ALU.mult))
            own()
            dve.wait_ge(ln_rstd_ok, 1)
            for n, cols in enumerate((mean, var)):
                for t in range(LAT_TT):
                    ins = dve.tensor_scalar(ln_wide[:, n, t, :], ones[:, :], cols[:, t:t + 1], None, ALU.mult)
            ins.then_inc(ln_cols_ok, 1)
            assert groups[0] == mark["before_o"], groups
            for n in range(LAT_TT * HEADS):
                t, h = divmod(n, HEADS)
                b = d_bank()
                dve.wait_ge(orstd_ok, n + 1)
                dve.scalar_tensor_tensor(o_sb[:, t, h * DV:(h + 1) * DV], b[:, 0:DV], stat[:, 8 + n:9 + n],
                                         sgn[:, t, h * DV:(h + 1) * DV], ALU.mult, ALU.mult).then_inc(d_empty, 1)
            b = d_bank()
            for ct in range(KT):
                step.sign(dve.tensor_tensor(yT[:, ct, :], yT[:, ct, :], b[:, 0:SEQ], ALU.subtract))
            own()
            for ct in range(KT):
                dve.tensor_tensor(yT[:, ct, :], yT[:, ct, :], b[:, SEQ:2 * SEQ], ALU.mult).then_inc(ln_in, 1)
            dve.wait_ge(ln_in, KT)
            dve.sem_inc(d_empty, 1)
            def flush_late():
                while late_taken[0] < late_due[0]:
                    part, n = divmod(late_taken[0], 2)
                    dst = (gt1, sh2, a2, gt2)[part]
                    b = d_bank()
                    dve.tensor_tensor(dst[:, n * NF:(n + 1) * NF], b[:, :],
                                      b_ada_b[:, part * D + n * NF:part * D + (n + 1) * NF], ALU.add).then_inc(d_empty, 1)
                    late_taken[0] += 1

            late_taken, late_due = [0], [0]
            dve.wait_ge(b_ada_in, 16)
            for n in range(2):
                for t in range(LAT_TT):
                    b = d_bank()
                    cs = slice(n * NF, (n + 1) * NF)
                    dve.tensor_tensor(m[:, t, cs], b[:, :], sg_gla[:, t, cs], ALU.mult).then_inc(d_empty, 1)
                    if t == 0:
                        flush_late()
                late_due[0] += LATE_AFTER["gla_out"][n]
            for n in range(2):
                for t in range(LAT_TT):
                    b = d_bank()
                    cs = slice(n * NF, (n + 1) * NF)
                    dve.tensor_tensor(gated[:, :], b[:, :], sg_conv[:, t, cs], ALU.mult).then_inc(d_empty, 1)
                    dve.wait_ge(d_empty, groups[0])
                    step.sign(dve.tensor_tensor(m[:, t, cs], m[:, t, cs], gated[:, :], ALU.add))
                    own()
                    dve.sem_inc(m_ok, 1)
                    if t == 0:
                        flush_late()
                late_due[0] += LATE_AFTER["conv_out"][n]
            dve.wait_ge(x_again_in, 16)
            dve.wait_ge(late_in, 32)
            for n in range(2):
                for t in range(LAT_TT):
                    b = d_bank()
                    cs = slice(n * NF, (n + 1) * NF)
                    dve.tensor_tensor(gated[:, :], b[:, :], gt1[:, cs], ALU.mult).then_inc(d_empty, 1)
                    dve.wait_ge(d_empty, groups[0])
                    step.sign(dve.tensor_tensor(x1[:, t, cs], x1[:, t, cs], gated[:, :], ALU.add))
                    own()
                    dve.sem_inc(x1_ok, 1)
                    if t == 0:
                        flush_late()
                    if n == 1 and t == 0:
                        dve.wait_ge(d_empty, groups[0])
                        step.sign(dve.scalar_tensor_tensor(a2[:, :], a2[:, :], 1.0, g_ffn_b[:, :], ALU.add, ALU.mult))
                        own()
                    if n == 1:
                        dve.wait_ge(sq_ok, LAT_TT + t + 1)
                        dve.tensor_tensor(stat[:, 16 + t:17 + t], stat[:, 32 + 2 * t:33 + 2 * t], stat[:, 33 + 2 * t:34 + 2 * t],
                                          ALU.add).then_inc(x1_sum, 1)
                        step.sign(dve.tensor_tensor(h2[:, t, :], x1[:, t, :], a2[:, :], ALU.mult))
                        own()
                        dve.wait_ge(x1_pow, t + 1)
                        dve.scalar_tensor_tensor(h2[:, t, :], h2[:, t, :], stat[:, 16 + t:17 + t], sh2[:, :], ALU.mult,
                                                 ALU.add).then_inc(h2_ok, 1)
                late_due[0] += LATE_AFTER["out"][n]
            dve.sem_inc(ms_free, 1)

            step.sign(dve.memset(y_hi[:, A, :].bitcast(F32), 0.0))
            step.sign(dve.memset(y_lo[:, A, :].bitcast(F32), 0.0))
            step.sign(dve.memset(scatter[:, :, :, :].bitcast(F32), 0.0))
            own()
            dve.sem_inc(y_out[A], 1)
            dve.sem_inc(sc_out, 1)
            b = d_bank()
            dve.tensor_copy(logit_part[:, :], b[:, 0:SEQ]).then_inc(d_empty, 1)
            b = d_bank()
            for t in range(LAT_TT):
                ins = dve.tensor_tensor(logits[:, t, :], b[:, t * E:(t + 1) * E], b_router_b[:, :], ALU.add)
            ins.then_inc(d_empty, 1)
            dve.wait_ge(d_empty, groups[0])
            for t in range(LAT_TT):
                step.sign(dve.max(top8[:, t, :], logits[:, t, :]))
            own()
            step.sign(dve.tensor_scalar(need[:, :, 3:4], top8[:, :, 0:1], -1.0, None, ALU.mult))
            own()
            dve.sem_inc(max_ok, 1)
            kth = top8[:, :, TOPK - 1:TOPK].to_broadcast([P, LAT_TT, E])
            step.sign(dve.tensor_tensor(above[:, :, :], logits[:, :, :], kth, ALU.is_gt))
            step.sign(dve.tensor_tensor(equal[:, :, :], logits[:, :, :], kth, ALU.is_equal))
            own()
            step.sign(dve.tensor_reduce(need[:, :, 0], above[:, :, :], AX_X, ALU.add))
            for t in range(LAT_TT):
                step.sign(dve.tensor_tensor_scan(nth[:, t, :], ones[:, 0:E], equal[:, t, :], 0.0, ALU.mult, ALU.add))
            own()
            step.sign(dve.tensor_scalar(need[:, :, 1:2], need[:, :, 0:1], -1.0, float(TOPK), ALU.mult, ALU.add))
            own()
            for t in range(LAT_TT):
                step.sign(dve.scalar_tensor_tensor(sel[:, t, :], nth[:, t, :], need[:, t, 1:2], equal[:, t, :], ALU.is_le, ALU.mult))
            own()
            step.sign(dve.tensor_tensor(sel[:, :, :], sel[:, :, :], above[:, :, :], ALU.add))
            own()
            dve.sem_inc(sel_ok, 1)
            dve.wait_ge(exp_ok, LAT_TT)
            step.sign(dve.tensor_tensor(expo[:, :, :], expo[:, :, :], sel[:, :, :], ALU.mult))
            own()
            step.sign(dve.tensor_reduce(need[:, :, 2], expo[:, :, :], AX_X, ALU.add))
            own()
            step.sign(dve.reciprocal(need[:, :, 2], need[:, :, 2]))
            own()
            for t in range(LAT_TT):
                step.sign(dve.tensor_scalar(prob[:, t, :], expo[:, t, :], need[:, t, 2:3], None, ALU.mult))
            flush_late()
            b = d_bank()
            step.sign(dve.tensor_copy(rank[:, :, :], b[:, 0:LAT_TT * E].rearrange("p (t e) -> p t e", e=E)))
            counts = b[:, LAT_TT * E:(LAT_TT + 1) * E]
            for j in range(ITEMS_OF_ONE):
                step.sign(dve.tensor_scalar(blocks[:, j, :], counts, float(j * SLOTS), None, ALU.is_gt))
            own()
            for j in range(1, ITEMS_OF_ONE):
                step.sign(dve.tensor_tensor(blocks[:, 0, :], blocks[:, 0, :], blocks[:, j, :], ALU.add))
            own()
            step.sign(dve.tensor_tensor_scan(ends[:, 1, :], ones[:, 0:E], blocks[:, 0, :], 0.0, ALU.mult, ALU.add))
            own()
            step.sign(dve.tensor_tensor(ends[:, 0, :], ends[:, 1, :], blocks[:, 0, :], ALU.subtract))
            own()
            dve.scalar_tensor_tensor(ends[:, 2, :], ends[:, 0, :], float(SLOTS), counts, ALU.mult, ALU.add).then_inc(d_empty, 1)
            step.sign(dve.tensor_scalar(above[:, :, :], sel[:, :, :], -BIG, BIG, ALU.mult, ALU.add))
            own()
            step.sign(dve.tensor_tensor(rank[:, :, :], rank[:, :, :], above[:, :, :], ALU.add))
            own()
            first_item = ends[:, 0, :].unsqueeze(1).to_broadcast([P, LAT_TT, E])
            step.sign(dve.scalar_tensor_tensor(rank[:, :, :], first_item, float(SLOTS), rank[:, :, :], ALU.mult, ALU.add))
            own()
            dve.wait_ge(d_empty, groups[0])
            dve.sem_inc(rank_ok, 1)
            step.sign(dve.tensor_reduce(need[:, :, 3], rank[:, :, :], AX_X, ALU.min))
            own()
            for t in range(LAT_TT):
                ins = dve.tensor_scalar(pick[:, t, :], slot_no[:, :], need[:, t, 3:4], None, ALU.is_equal)
            ins.then_inc(pick_ok, 1)
            b = d_bank()
            step.sign(dve.tensor_copy(rankT[:, :, :], b[0:E, 0:LAT_TT * P].rearrange("p (t c) -> p t c", c=P)))
            dve.tensor_copy(probT[:, :, :], b[0:E, LAT_TT * P:2 * LAT_TT * P].rearrange("p (t c) -> p t c", c=P)).then_inc(d_empty, 1)
            b = d_bank()
            dve.tensor_copy(ecol[:, 0:1], b[0:E, 0:1])
            dve.wait_ge(const_ok, N_CONST + 2)
            dve.tensor_copy(ecol[:, 3:4], b[0:E, 2 * P:2 * P + 1])
            dve.tensor_copy(ecol[:, 1:2], b[0:E, P:P + 1]).then_inc(d_empty, 1)
            dve.wait_ge(d_empty, groups[0])
            step.sign(dve.tensor_scalar(one_item[:, :], item_no[0:E, :], ecol[:, 1:2], None, ALU.is_lt))
            own()
            step.sign(dve.scalar_tensor_tensor(one_item[:, :], item_no[0:E, :], ecol[:, 0:1], one_item[:, :], ALU.is_ge, ALU.mult))
            own()
            dve.sem_inc(one_item_ok, 1)
            b = d_bank()
            for t in range(LAT_TT):
                step.sign(dve.scalar_tensor_tensor(slot_tok[:, t, :], item_no[:, :], -float(SLOTS), b[:, t * ITEM_COLS:(t + 1) * ITEM_COLS],
                                                   ALU.mult, ALU.add))
            own()
            step.sign(dve.scalar_tensor_tensor(spill[:, :], item_no[0:1, :], -float(SLOTS),
                                               b[0:1, (2 * LAT_TT + 1) * ITEM_COLS:(2 * LAT_TT + 2) * ITEM_COLS], ALU.mult, ALU.add))
            own()
            step.sign(dve.tensor_scalar(item_wide[:, :], spill[:, :], float(HALF_P), None, ALU.is_gt))
            step.sign(dve.tensor_copy(item_expert[0:1, ITEM_COLS:ITEM_COLS + 1], ends[0:1, 1, E - 1:E]))
            dve.tensor_copy(prob_tok[:, :, :], b[:, LAT_TT * ITEM_COLS:2 * LAT_TT * ITEM_COLS].rearrange("p (t i) -> p t i", i=ITEM_COLS))
            dve.tensor_copy(item_expert[0:1, 0:ITEM_COLS], b[0:1, 2 * LAT_TT * ITEM_COLS:(2 * LAT_TT + 1) * ITEM_COLS]).then_inc(d_empty, 1)
            dve.wait_ge(d_empty, groups[0])
            own()
            dve.sem_inc(items_ok, 1)

            items = item_count(dve)

            def make_pick(i):
                for t in range(LAT_TT):
                    ins = dve.tensor_scalar(pick[:, t, :], slot_no[:, :], slot_tok[:, t, bass.ds(i, 1)], None, ALU.is_equal)
                ins.then_inc(pick_ok, 1)

            STEPS = 2

            def swiglu(i, blk, before):
                own_steps = i * (2 * STEPS) + before
                banks = bank[6:8] if blk == B else bank[4:6]
                glu, lin = swi[:, blk, 0, :, :], swi[:, blk, 1, :, :]

                def add_bias(part, dst):
                    dve.wait_ge(ht_full[blk], i * 2 + (part + 1))
                    b1 = b1T[:, bass.ds(e, 1), part * (FF // P):(part + 1) * (FF // P)].rearrange("p a j -> p (a j)") \
                        .unsqueeze(2).to_broadcast([P, FF // P, HALF_P])
                    dve.tensor_tensor(dst, banks[part][:, :].rearrange("p (j c) -> p j c", c=HALF_P), b1, ALU.add).then_inc(ht_out[blk], 1)
                    dve.wait_ge(ht_out[blk], i * 2 + (part + 1))

                add_bias(0, glu)
                dve.tensor_scalar(glu, glu, LIMIT, None, ALU.min).then_inc(glu_ok[blk], 1)
                add_bias(1, lin)
                dve.tensor_scalar(lin, lin, LIMIT, -LIMIT, ALU.min, ALU.max).then_inc(swi_step, 1)
                dve.wait_ge(swi_step, own_steps + 1)
                dve.wait_ge(glu_ok[blk], i + 1)
                dve.scalar_tensor_tensor(lin, lin, 1.0, glu, ALU.add, ALU.mult).then_inc(swi_step, 1)
                dve.wait_ge(swi_step, own_steps + 2)
                dve.wait_ge(sig_ok[blk], i + 1)
                dve.tensor_tensor(hs[:, blk, :, :], lin, sig[:, blk, :, :], ALU.mult).then_inc(hs_ok[blk], 1)

            with dve.Fori(0, items) as i:
                e = dve.value_load(item_expert[0:1, bass.ds(i, 1)], min_val=0, max_val=E - 1)
                wide = item_of(dve, i)
                dve.wait_ge(xs_full, i * 2 + 2)
                make_pick(i + 1)
                dve.wait_ge(unit_used, i * UPI + 1)
                for t in range(LAT_TT):
                    ins = dve.tensor_scalar(weigh[:, t, :, :].rearrange("p b (d c) -> p b d c", d=2), slot_twice[:, :, :, :],
                                            slot_tok[:, t, bass.ds(i, 1)], prob_tok[:, t, bass.ds(i, 1)], ALU.is_equal, ALU.mult)
                ins.then_inc(weigh_ok, 1)
                def finish(i, blk):
                    dve.wait_ge(yh_ok[blk], i + 1)
                    dve.scalar_tensor_tensor(y_lo[:, blk, :], bank[5 if blk == B else 7][:, :], slot_prob[:, blk:blk + 1],
                                             y_hi[:, blk, :].bitcast(F32), ALU.mult, ALU.subtract).then_inc(y_out[blk], 1)

                def after_swiglu(i):
                    dve.wait_ge(weighT_ok, i + 1)
                    dve.wait_ge(scattered, i + 1)
                    dve.tensor_scalar(scatter[:, :, :, :], weighT[:, :, :, :], 0.0, None, ALU.is_gt).then_inc(sc_out, 1)

                with dve.If(wide == 0):
                    dve.sem_inc(y_out[B], 1)
                    dve.sem_inc(swi_step, STEPS)
                    for done in (glu_ok[B], hs_ok[B]):
                        dve.sem_inc(done, 1)
                    dve.sem_inc(ht_out[B], 2)
                    swiglu(i, A, STEPS)
                    after_swiglu(i)
                with dve.Else():
                    swiglu(i, B, 0)
                    swiglu(i, A, STEPS)
                    after_swiglu(i)
                    finish(i, B)
                finish(i, A)
            dve.wait_ge(g_final_in, 16)
            for t in range(LAT_TT):
                dve.wait_ge(acc_full, t + 1)
                for n in range(2):
                    cs = slice(n * NF, (n + 1) * NF)
                    step.sign(dve.tensor_tensor(sums[:, t, cs], bank[2 * t + n][:, :], gt2[:, cs], ALU.mult))
                    own()
                    dve.tensor_tensor(x1[:, t, cs], x1[:, t, cs], sums[:, t, cs], ALU.add).then_inc(x2_ok, 1)
            for t in range(LAT_TT):
                dve.wait_ge(fin_sq, 2 * t + 2)
                dve.tensor_tensor(stat[:, 20 + t:21 + t], stat[:, 36 + 2 * t:37 + 2 * t], stat[:, 37 + 2 * t:38 + 2 * t],
                                  ALU.add).then_inc(fin_sum, 1)
            dve.tensor_tensor(out_sb[:, LAT_TT - 1, :], x1[:, LAT_TT - 1, :], g_final_b[:, :], ALU.mult).then_inc(scaled_last_ok, 1)
            for t in range(LAT_TT):
                if t < LAT_TT - 1:
                    dve.wait_ge(scaled_ok, t + 1)
                else:
                    dve.wait_ge(scaled_last_ok, 1)
                dve.wait_ge(fin_pow, t + 1)
                dve.tensor_scalar(out_sb[:, t, 0:NF], out_sb[:, t, 0:NF], stat[:, 20 + t:21 + t], None, ALU.mult).then_inc(out_ok, 1)



_INS = ["x", "c", "ctx", "c_ctx", "w_ada", "b_ada", "g_mix_norm", "w_in", "w_dw", "b_dw", "g_conv_ln", "b_conv_ln",
        "w_conv_out", "w_alpha", "b_alpha", "g_gla_norm", "w_gla_out", "w_out", "g_ffn_norm", "w_router", "b_router",
        "w_exp_in", "b_exp_in", "w_exp_out", "b_exp_out", "g_final"]


def kernel(**inputs):
    import numpy as np
    import concourse.bacc as bacc
    from concourse.bass_utils import run_bass_kernel_spmd

    nc = bacc.Bacc("TRN2", target_bir_lowering=False, num_devices=1)
    arrays, args = {}, []
    for name in _INS:
        a = np.ascontiguousarray(inputs[name])
        arrays[f"in_{name}"] = a
        args.append(nc.dram_tensor(f"in_{name}", a.shape, mybir.dt.from_np(a.dtype), kind="ExternalInput").ap())
    out = nc.dram_tensor("out_0", inputs["x"].shape, F32, kind="ExternalOutput").ap()
    build(nc, *args, out)
    r = run_bass_kernel_spmd(nc, [arrays], core_ids=[0])
    return r.results[0]["out_0"]
```
